# Optimizing a Trainium2 kernel written in Bass

```python
import math
import jax
import jax.numpy as jnp
from jax import lax
import numpy as np

D_MODEL = 2048
BATCH = 1
SEQ = 256
DEPTH = 1

F32 = jnp.float32
MIX_WIDTH = D_MODEL
N_MIXERS = 4
GROUP_WIDTH = MIX_WIDTH // N_MIXERS
SWA_HEADS = 8
SWA_KV_HEADS = 2
SWA_HEAD_DIM = GROUP_WIDTH // SWA_HEADS
WINDOW = 128
SWA_BLOCK = 128
CONV_CH = GROUP_WIDTH
CONV_WIDTH = 31
MLA_HEADS = 4
MLA_Q_LORA = 512
MLA_KV_LORA = 256
MLA_NOPE = 128
MLA_ROPE = 64
MLA_V = GROUP_WIDTH // MLA_HEADS
MLA_QBLK = 128
ROPE_THETA = 10000.0
SSM_CH = GROUP_WIDTH
SSM_GROUP_IN = 16
SSM_GROUPS = SSM_CH // SSM_GROUP_IN
SSM_STATE = 64
DT_MIN = 0.001
DT_MAX = 0.1
REL_BUCKETS = 32
REL_MAX_DIST = 128
MEM_TOKENS = 256
XA_HEADS = 4
XA_HEAD_DIM = 128
N_EXPERT_GROUPS = 4
EXPERTS_PER_GROUP = 8
N_EXPERTS = N_EXPERT_GROUPS * EXPERTS_PER_GROUP
EXPERT_TOPK = 2
EXPERT_FF = 512
EXPERT_BLOCK = 256
NORM_EPS = 1e-6
NEG_INF = -1e30
IN_SPLITS = (SWA_HEADS * SWA_HEAD_DIM, SWA_KV_HEADS * SWA_HEAD_DIM, SWA_KV_HEADS * SWA_HEAD_DIM,
             CONV_CH, CONV_CH, MLA_Q_LORA, MLA_KV_LORA, MLA_ROPE, SSM_CH)
IN_WIDTH = sum(IN_SPLITS)

kernel_name = 'hybrid_parallel_heads_hmoe_trunk'

def rms_norm(x, g):
    x32 = x.astype(F32)
    y = x32 * lax.rsqrt(jnp.mean(x32 * x32, axis=-1, keepdims=True) + NORM_EPS)
    return (y * g.astype(F32)).astype(x.dtype)

def layer_norm(x, g, b):
    x32 = x.astype(F32)
    xc = x32 - jnp.mean(x32, axis=-1, keepdims=True)
    y = xc * lax.rsqrt(jnp.mean(xc * xc, axis=-1, keepdims=True) + NORM_EPS)
    return (y * g.astype(F32) + b.astype(F32)).astype(x.dtype)

def rope_tables(seq_len):
    inv = 1.0 / (ROPE_THETA ** (jnp.arange(0, MLA_ROPE, 2, dtype=F32) / MLA_ROPE))
    ang = jnp.arange(seq_len, dtype=F32)[:, None] * inv[None, :]
    return jnp.cos(ang), jnp.sin(ang)

def apply_rope(x, cos, sin):
    x32 = x.astype(F32)
    x1, x2 = jnp.split(x32, 2, axis=-1)
    return jnp.concatenate([x1 * cos - x2 * sin, x1 * sin + x2 * cos], axis=-1).astype(x.dtype)

def t5_band_buckets():
    qi = np.arange(SWA_BLOCK)[:, None]
    kj = np.arange(2 * SWA_BLOCK)[None, :]
    dist = SWA_BLOCK + qi - kj
    valid = (dist >= 0) & (dist < WINDOW)
    max_exact = REL_BUCKETS // 2
    d0 = np.maximum(dist, 0)
    dl = np.maximum(dist, 1).astype(np.float32)
    large = max_exact + (np.log(dl / max_exact) / np.log(REL_MAX_DIST / max_exact)
                         * (REL_BUCKETS - max_exact)).astype(np.int32)
    large = np.minimum(large, REL_BUCKETS - 1)
    bucket = np.where(d0 < max_exact, d0, large).astype(np.int32)
    return bucket, valid

def swa_sink_attention(q, k, v, sinks, rel_bias):
    b, s, _, dh = q.shape
    nb = s // SWA_BLOCK
    grp = SWA_HEADS // SWA_KV_HEADS
    qb = q.reshape(b, nb, SWA_BLOCK, SWA_KV_HEADS, grp, dh)

    def band(t):
        tb = t.reshape(b, nb, SWA_BLOCK, SWA_KV_HEADS, dh)
        prev = jnp.concatenate([jnp.zeros_like(tb[:, :1]), tb[:, :-1]], axis=1)
        return jnp.concatenate([prev, tb], axis=2)

    kb, vb = band(k), band(v)
    bucket, valid = t5_band_buckets()
    bias = rel_bias.astype(F32)[bucket]
    bias = bias.reshape(SWA_BLOCK, 2 * SWA_BLOCK, SWA_KV_HEADS, grp).transpose(2, 3, 0, 1)
    not_first = (np.arange(nb)[:, None, None] > 0) | (np.arange(2 * SWA_BLOCK)[None, None, :] >= SWA_BLOCK)
    mask = jnp.asarray(valid[None] & not_first)[None, :, None, None]
    logits = jnp.einsum('bnqkgd,bnjkd->bnkgqj', qb, kb).astype(F32) * (dh ** -0.5) + bias
    logits = jnp.where(mask, logits, NEG_INF)
    sink = sinks.astype(F32).reshape(SWA_KV_HEADS, grp)[None, None, :, :, None, None]
    m = jnp.maximum(jnp.max(logits, axis=-1, keepdims=True), sink)
    p = jnp.exp(logits - m)
    probs = p / (jnp.sum(p, axis=-1, keepdims=True) + jnp.exp(sink - m))
    out = jnp.einsum('bnkgqj,bnjkd->bnqkgd', probs.astype(v.dtype), vb)
    return out.reshape(b, s, SWA_HEADS * dh)

def conformer_conv(a, g, dw_w, dw_b, ln_g, ln_b, pw_w, pw_b):
    z = a * jax.nn.sigmoid(g)
    z = lax.conv_general_dilated(z, dw_w[:, None, :].astype(z.dtype), window_strides=(1,),
                                 padding=[(CONV_WIDTH - 1, 0)],
                                 dimension_numbers=('NWC', 'WIO', 'NWC'),
                                 feature_group_count=CONV_CH) + dw_b
    z = jax.nn.silu(layer_norm(z, ln_g, ln_b))
    return z @ pw_w + pw_b

def mla_attention(q_lat, kv_lat, k_rope_in, qa_g, kva_g, wq_b, wkv_b,
                  qn_nope_g, qn_rope_g, kn_nope_g, kn_rope_g, cos, sin):
    b, s, _ = q_lat.shape
    q = (rms_norm(q_lat, qa_g) @ wq_b).reshape(b, s, MLA_HEADS, MLA_NOPE + MLA_ROPE)
    kv = (rms_norm(kv_lat, kva_g) @ wkv_b).reshape(b, s, MLA_HEADS, MLA_NOPE + MLA_V)
    q_nope = rms_norm(q[..., :MLA_NOPE], qn_nope_g)
    q_rope = apply_rope(rms_norm(q[..., MLA_NOPE:], qn_rope_g), cos[:, None, :], sin[:, None, :])
    k_nope = rms_norm(kv[..., :MLA_NOPE], kn_nope_g)
    v = kv[..., MLA_NOPE:]
    k_rope = apply_rope(rms_norm(k_rope_in, kn_rope_g), cos, sin)
    nb = s // MLA_QBLK

    def to_blocks(t):
        return jnp.moveaxis(t.reshape(b, nb, MLA_QBLK, *t.shape[2:]), 1, 0)

    q_pos = jnp.arange(s, dtype=jnp.int32).reshape(nb, MLA_QBLK)
    k_pos = jnp.arange(s, dtype=jnp.int32)
    scale = (MLA_NOPE + MLA_ROPE) ** -0.5

    def one_block(args):
        qn, qr, qp = args
        logits = (jnp.einsum('bqhd,bkhd->bhqk', qn, k_nope)
                  + jnp.einsum('bqhr,bkr->bhqk', qr, k_rope)).astype(F32) * scale
        logits = jnp.where(k_pos[None, :] <= qp[:, None], logits, NEG_INF)
        probs = jax.nn.softmax(logits, axis=-1)
        return jnp.einsum('bhqk,bkhd->bqhd', probs.astype(v.dtype), v)

    out = lax.map(one_block, (to_blocks(q_nope), to_blocks(q_rope), q_pos))
    return jnp.moveaxis(out, 0, 1).reshape(b, s, MLA_HEADS * MLA_V)

def s5_mixer(u, a_re, a_im, log_dt, b_re, b_im, c_re, c_im, d_skip, glu_w, glu_b):
    b, s, _ = u.shape
    u32 = u.astype(F32).reshape(b, s, SSM_GROUPS, SSM_GROUP_IN)
    lam = lax.complex(a_re.astype(F32), a_im.astype(F32))
    dt = jnp.exp(log_dt.astype(F32))[:, None]
    lam_bar = jnp.exp(lam * dt)
    b_bar = ((lam_bar - 1.0) / lam)[..., None] * lax.complex(b_re.astype(F32), b_im.astype(F32))
    bu = jnp.einsum('bsgi,gpi->bsgp', u32.astype(jnp.complex64), b_bar)
    a_seq = jnp.broadcast_to(lam_bar, bu.shape)

    def combine(left, right):
        a_l, x_l = left
        a_r, x_r = right
        return a_r * a_l, a_r * x_l + x_r

    _, states = lax.associative_scan(combine, (a_seq, bu), axis=1)
    c = lax.complex(c_re.astype(F32), c_im.astype(F32))
    y = (jnp.einsum('gop,bsgp->bsgo', c, states).real
         + d_skip.astype(F32).reshape(SSM_GROUPS, SSM_GROUP_IN) * u32)
    y = jax.nn.gelu(y.reshape(b, s, SSM_CH))
    out = y * jax.nn.sigmoid(y @ glu_w.astype(F32) + glu_b.astype(F32))
    return out.astype(u.dtype)

def memory_cross_attention(h, mem_n, wq, wk, wv, qn_g, kn_g, wo):
    b, s, _ = h.shape
    m = mem_n.shape[1]
    q = rms_norm((h @ wq).reshape(b, s, XA_HEADS, XA_HEAD_DIM), qn_g)
    k = rms_norm((mem_n @ wk).reshape(b, m, XA_HEADS, XA_HEAD_DIM), kn_g)
    v = (mem_n @ wv).reshape(b, m, XA_HEADS, XA_HEAD_DIM)
    logits = jnp.einsum('bshd,bmhd->bhsm', q, k).astype(F32) * (XA_HEAD_DIM ** -0.5)
    probs = jax.nn.softmax(logits, axis=-1)
    o = jnp.einsum('bhsm,bmhd->bshd', probs.astype(v.dtype), v).reshape(b, s, XA_HEADS * XA_HEAD_DIM)
    return o @ wo

def dispatch_experts(ht, expert_flat, w_flat, w_gate, w_up, w_down):
    n_tok, d = ht.shape
    n_assign = expert_flat.shape[0]
    n_blocks = -(-(n_assign + N_EXPERTS * (EXPERT_BLOCK - 1)) // EXPERT_BLOCK)
    padded_len = n_blocks * EXPERT_BLOCK
    tok_flat = jnp.repeat(jnp.arange(n_tok, dtype=jnp.int32), EXPERT_TOPK)
    order = jnp.argsort(expert_flat)
    e_sorted = expert_flat[order]
    tok_sorted = tok_flat[order]
    w_sorted = w_flat[order]
    counts = jnp.bincount(expert_flat, length=N_EXPERTS)
    starts = jnp.cumsum(counts) - counts
    padded = (counts + EXPERT_BLOCK - 1) // EXPERT_BLOCK * EXPERT_BLOCK
    pad_ends = jnp.cumsum(padded)
    pad_starts = pad_ends - padded
    dest = pad_starts[e_sorted] + jnp.arange(n_assign, dtype=jnp.int32) - starts[e_sorted]
    tok_buf = jnp.full((padded_len,), n_tok, jnp.int32).at[dest].set(tok_sorted)
    w_buf = jnp.zeros((padded_len,), ht.dtype).at[dest].set(w_sorted.astype(ht.dtype))
    block_starts = jnp.arange(n_blocks, dtype=jnp.int32) * EXPERT_BLOCK
    block_expert = jnp.minimum(jnp.searchsorted(pad_ends, block_starts, side='right'),
                               N_EXPERTS - 1).astype(jnp.int32)
    x_pad = jnp.concatenate([ht, jnp.zeros((1, d), ht.dtype)], axis=0)
    xb = x_pad[tok_buf].reshape(n_blocks, EXPERT_BLOCK, d)

    def expert_block(args):
        xblk, e = args
        hid = jax.nn.silu(xblk @ w_gate[e]) * (xblk @ w_up[e])
        return hid @ w_down[e]

    out = lax.map(expert_block, (xb, block_expert)).reshape(padded_len, d)
    y = jnp.zeros((n_tok + 1, d), ht.dtype).at[tok_buf].add(out * w_buf[:, None])
    return y[:n_tok]

def hier_moe(h, w_group, b_group, w_expert, b_expert, w_gate, w_up, w_down):
    b, s, d = h.shape
    n_tok = b * s
    ht = h.reshape(n_tok, d)
    tok = jnp.arange(n_tok)
    g_logits = (ht @ w_group).astype(F32) + b_group.astype(F32)
    g_idx = jnp.argmax(g_logits, axis=-1)
    g_w = jax.nn.softmax(g_logits, axis=-1)[tok, g_idx]
    e_logits = ((ht @ w_expert).astype(F32) + b_expert.astype(F32)).reshape(
        n_tok, N_EXPERT_GROUPS, EXPERTS_PER_GROUP)[tok, g_idx]
    top_val, top_idx = lax.top_k(e_logits, EXPERT_TOPK)
    gate = jax.nn.softmax(top_val, axis=-1) * g_w[:, None]
    expert_id = (g_idx[:, None] * EXPERTS_PER_GROUP + top_idx).astype(jnp.int32)
    y = dispatch_experts(ht, expert_id.reshape(-1), gate.reshape(-1), w_gate, w_up, w_down)
    return y.reshape(b, s, d)

def setup_inputs(seed: int = 0) -> dict:
    key = jax.random.key(seed)
    keys = list(jax.random.split(key, 64))
    L = DEPTH

    def nk():
        return keys.pop()

    def nrm(shape, scale):
        return scale * jax.random.normal(nk(), shape, F32)

    def gain(shape):
        return 1.0 + 0.02 * jax.random.normal(nk(), shape, F32)

    a_im = jnp.pi * jnp.arange(SSM_STATE, dtype=F32)[None, None, :] + nrm((L, SSM_GROUPS, SSM_STATE), 0.01)
    return {
        'x': nrm((BATCH, SEQ, D_MODEL), 1.0),
        'mem': nrm((BATCH, MEM_TOKENS, D_MODEL), 1.0),
        'rel_bias': nrm((REL_BUCKETS, SWA_HEADS), 0.5),
        'ln_mix_g': gain((L, D_MODEL)),
        'w_in': nrm((L, D_MODEL, IN_WIDTH), D_MODEL ** -0.5),
        'swa_qn_g': gain((L, SWA_HEAD_DIM)),
        'swa_kn_g': gain((L, SWA_HEAD_DIM)),
        'swa_sinks': nrm((L, SWA_HEADS), 0.5),
        'conv_dw_w': nrm((L, CONV_WIDTH, CONV_CH), CONV_WIDTH ** -0.5),
        'conv_dw_b': nrm((L, CONV_CH), 0.02),
        'conv_ln_g': gain((L, CONV_CH)),
        'conv_ln_b': nrm((L, CONV_CH), 0.02),
        'conv_pw_w': nrm((L, CONV_CH, CONV_CH), CONV_CH ** -0.5),
        'conv_pw_b': nrm((L, CONV_CH), 0.02),
        'mla_qa_g': gain((L, MLA_Q_LORA)),
        'mla_kva_g': gain((L, MLA_KV_LORA)),
        'mla_wq_b': nrm((L, MLA_Q_LORA, MLA_HEADS * (MLA_NOPE + MLA_ROPE)), MLA_Q_LORA ** -0.5),
        'mla_wkv_b': nrm((L, MLA_KV_LORA, MLA_HEADS * (MLA_NOPE + MLA_V)), MLA_KV_LORA ** -0.5),
        'mla_qn_nope_g': gain((L, MLA_NOPE)),
        'mla_qn_rope_g': gain((L, MLA_ROPE)),
        'mla_kn_nope_g': gain((L, MLA_NOPE)),
        'mla_kn_rope_g': gain((L, MLA_ROPE)),
        'ssm_a_re': -0.5 + nrm((L, SSM_GROUPS, SSM_STATE), 0.01),
        'ssm_a_im': a_im,
        'ssm_log_dt': jax.random.uniform(nk(), (L, SSM_GROUPS), F32, math.log(DT_MIN), math.log(DT_MAX)),
        'ssm_b_re': nrm((L, SSM_GROUPS, SSM_STATE, SSM_GROUP_IN), (2 * SSM_GROUP_IN) ** -0.5),
        'ssm_b_im': nrm((L, SSM_GROUPS, SSM_STATE, SSM_GROUP_IN), (2 * SSM_GROUP_IN) ** -0.5),
        'ssm_c_re': nrm((L, SSM_GROUPS, SSM_GROUP_IN, SSM_STATE), SSM_STATE ** -0.5),
        'ssm_c_im': nrm((L, SSM_GROUPS, SSM_GROUP_IN, SSM_STATE), SSM_STATE ** -0.5),
        'ssm_d': nrm((L, SSM_CH), 1.0),
        'ssm_glu_w': nrm((L, SSM_CH, SSM_CH), SSM_CH ** -0.5),
        'ssm_glu_b': nrm((L, SSM_CH), 0.02),
        'mix_out_g': gain((L, MIX_WIDTH)),
        'w_out': nrm((L, MIX_WIDTH, D_MODEL), MIX_WIDTH ** -0.5),
        'ln_cross_g': gain((L, D_MODEL)),
        'mem_ln_g': gain((L, D_MODEL)),
        'xa_wq': nrm((L, D_MODEL, XA_HEADS * XA_HEAD_DIM), D_MODEL ** -0.5),
        'xa_wk': nrm((L, D_MODEL, XA_HEADS * XA_HEAD_DIM), D_MODEL ** -0.5),
        'xa_wv': nrm((L, D_MODEL, XA_HEADS * XA_HEAD_DIM), D_MODEL ** -0.5),
        'xa_qn_g': gain((L, XA_HEAD_DIM)),
        'xa_kn_g': gain((L, XA_HEAD_DIM)),
        'xa_wo': nrm((L, XA_HEADS * XA_HEAD_DIM, D_MODEL), (XA_HEADS * XA_HEAD_DIM) ** -0.5),
        'ln_moe_g': gain((L, D_MODEL)),
        'moe_w_group': nrm((L, D_MODEL, N_EXPERT_GROUPS), D_MODEL ** -0.5),
        'moe_b_group': nrm((L, N_EXPERT_GROUPS), 0.01),
        'moe_w_expert': nrm((L, D_MODEL, N_EXPERTS), D_MODEL ** -0.5),
        'moe_b_expert': nrm((L, N_EXPERTS), 0.01),
        'moe_w_gate': nrm((L, N_EXPERTS, D_MODEL, EXPERT_FF), D_MODEL ** -0.5),
        'moe_w_up': nrm((L, N_EXPERTS, D_MODEL, EXPERT_FF), D_MODEL ** -0.5),
        'moe_w_down': nrm((L, N_EXPERTS, EXPERT_FF, D_MODEL), EXPERT_FF ** -0.5),
    }

def reference(x, mem, rel_bias, ln_mix_g, w_in, swa_qn_g, swa_kn_g, swa_sinks,
              conv_dw_w, conv_dw_b, conv_ln_g, conv_ln_b, conv_pw_w, conv_pw_b,
              mla_qa_g, mla_kva_g, mla_wq_b, mla_wkv_b, mla_qn_nope_g, mla_qn_rope_g,
              mla_kn_nope_g, mla_kn_rope_g,
              ssm_a_re, ssm_a_im, ssm_log_dt, ssm_b_re, ssm_b_im, ssm_c_re, ssm_c_im,
              ssm_d, ssm_glu_w, ssm_glu_b,
              mix_out_g, w_out,
              ln_cross_g, mem_ln_g, xa_wq, xa_wk, xa_wv, xa_qn_g, xa_kn_g, xa_wo,
              ln_moe_g, moe_w_group, moe_b_group, moe_w_expert, moe_b_expert,
              moe_w_gate, moe_w_up, moe_w_down):
    b, s, _ = x.shape
    cos, sin = rope_tables(s)
    split_at = [int(i) for i in np.cumsum(IN_SPLITS)[:-1]]
    for l in range(DEPTH):
        h = rms_norm(x, ln_mix_g[l])
        a_q, a_k, a_v, b_a, b_g, c_q, c_kv, c_kr, d_u = jnp.split(h @ w_in[l], split_at, axis=-1)
        q = rms_norm(a_q.reshape(b, s, SWA_HEADS, SWA_HEAD_DIM), swa_qn_g[l])
        k = rms_norm(a_k.reshape(b, s, SWA_KV_HEADS, SWA_HEAD_DIM), swa_kn_g[l])
        v = a_v.reshape(b, s, SWA_KV_HEADS, SWA_HEAD_DIM)
        o_a = swa_sink_attention(q, k, v, swa_sinks[l], rel_bias)
        o_b = conformer_conv(b_a, b_g, conv_dw_w[l], conv_dw_b[l], conv_ln_g[l], conv_ln_b[l],
                             conv_pw_w[l], conv_pw_b[l])
        o_c = mla_attention(c_q, c_kv, c_kr, mla_qa_g[l], mla_kva_g[l], mla_wq_b[l], mla_wkv_b[l],
                            mla_qn_nope_g[l], mla_qn_rope_g[l], mla_kn_nope_g[l], mla_kn_rope_g[l],
                            cos, sin)
        o_d = s5_mixer(d_u, ssm_a_re[l], ssm_a_im[l], ssm_log_dt[l], ssm_b_re[l], ssm_b_im[l],
                       ssm_c_re[l], ssm_c_im[l], ssm_d[l], ssm_glu_w[l], ssm_glu_b[l])
        o = jnp.concatenate([o_a, o_b, o_c, o_d], axis=-1).reshape(b, s, N_MIXERS, GROUP_WIDTH)
        o = rms_norm(o, mix_out_g[l].reshape(N_MIXERS, GROUP_WIDTH)).reshape(b, s, MIX_WIDTH)
        x = x + o @ w_out[l]
        x = x + memory_cross_attention(rms_norm(x, ln_cross_g[l]), rms_norm(mem, mem_ln_g[l]),
                                       xa_wq[l], xa_wk[l], xa_wv[l], xa_qn_g[l], xa_kn_g[l], xa_wo[l])
        x = x + hier_moe(rms_norm(x, ln_moe_g[l]), moe_w_group[l], moe_b_group[l],
                         moe_w_expert[l], moe_b_expert[l], moe_w_gate[l], moe_w_up[l], moe_w_down[l])
    return x


_drawn_inputs = setup_inputs


def setup_inputs(seed=0):
    import zlib

    import numpy as np

    out = dict(_drawn_inputs(seed))
    spreads = {}
    factors = {'swa_qn_g': 3.206,
     'swa_kn_g': 3.668,
     'swa_sinks': 6.294,
     'conv_ln_b': 2.779,
     'conv_pw_b': 2.685,
     'mla_qa_g': 4.238,
     'mla_kva_g': 2.876,
     'mla_qn_nope_g': 4.886,
     'mla_qn_rope_g': 3.996,
     'mla_kn_nope_g': 3.851,
     'mla_kn_rope_g': 5.939,
     'ssm_a_re': 63.536,
     'ssm_glu_b': 4.138,
     'ln_cross_g': 7.841,
     'mem_ln_g': 4.207,
     'xa_qn_g': 8.0,
     'xa_kn_g': 4.224,
     'moe_b_group': 25.408,
     'moe_b_expert': 23.416,
     'ln_moe_g': 8.0}
    for name, (base, spread) in spreads.items():
        noise = np.random.default_rng([zlib.crc32(name.encode()), seed]).standard_normal(out[name].shape)
        drawn = base * np.exp(spread * noise) if base else spread * noise
        out[name] = jnp.asarray(drawn.astype(out[name].dtype))
    for name, factor in factors.items():
        out[name] = (out[name] * factor).astype(out[name].dtype)
    return out
```

```python
from contextlib import ExitStack

import numpy as np
import concourse.bass as bass
from concourse import mybir

F32 = mybir.dt.float32
F32R = mybir.dt.float32r
I32 = mybir.dt.int32
U32 = mybir.dt.uint32
ALU = mybir.AluOpType
ACT = mybir.ActivationFunctionType
AX = mybir.AxisListType

P = 128
T = 256
TT = T // P
D = 2048
KD = D // P
GW = 512
GC = GW // P
EPS = 1e-6
NEG = -1e30
SWA_H, SWA_KV, SWA_D = 8, 2, 64
CONV_W = 31
MLA_H, NOPE, ROPE = 4, 128, 64
QK_D = NOPE + ROPE
XA_H = 4
SSM_TILES = 16
HALF = SSM_TILES // 2
SCAN_L = 16
N_GROUPS, PER_GROUP = 4, 8
N_EXP = N_GROUPS * PER_GROUP
FF = 512
SLOTS = 64
MAX_BLOCKS = N_EXP + 2 * T // SLOTS
TABLE = MAX_BLOCKS + 2
ROWS = 4 * T
FAR = 4.0 * ROWS
PIECE = 2048
RING = 12
FRONT_RING = 6
PPE = 12
HI_RING, LO_RING = 3, 2

CONST = {}
_at = 0
for _n, _w in (("ident", 128), ("flip", 128), ("ones", 128), ("ltri", 128), ("causal", 256), ("cmask", 128), ("slot", 128),
               ("stack", 64), ("i32", 32), ("cos", 64), ("sin", 64), ("row0", 2),
               ("half", 1), ("eps", 1), ("part", 1)):
    CONST[_n] = (_at, _at + _w)
    _at += _w
N_CONST = _at
BIAS_W = 384
N_BUCKET = 32


def constants():
    c = np.zeros((P, N_CONST), np.float32)

    def put(name, a):
        c[:, CONST[name][0]:CONST[name][1]] = a

    p = np.arange(P)
    put("ident", np.eye(P))
    put("flip", np.eye(P)[::-1])
    put("ones", 1.0)
    put("ltri", p[:, None] < p[None, :])
    put("causal", np.concatenate([np.zeros((P, P)), np.where(p[None, :] <= p[:, None], 0.0, NEG)], 1))
    put("cmask", ((p[:, None] // 16) % 2) == (p[None, :] // 64))
    put("slot", p[None, :] % SLOTS)
    put("stack", (p[:, None] % SLOTS) == np.arange(SLOTS)[None, :])
    put("i32", np.arange(N_EXP)[None, :])
    put("part", p[:, None])
    inv = (1.0 / (np.float32(10000.0) ** (np.arange(0, ROPE, 2, dtype=np.float32) / np.float32(ROPE)))).astype(np.float32)
    ang = np.arange(T, dtype=np.float32)[:, None] * inv[None, :]
    put("cos", np.cos(ang).reshape(TT, P, 32).transpose(1, 0, 2).reshape(P, 64))
    put("sin", np.sin(ang).reshape(TT, P, 32).transpose(1, 0, 2).reshape(P, 64))
    put("row0", 4.0 * (p[:, None] + P * np.arange(TT)[None, :]) - FAR)
    put("half", (p[:, None] // SLOTS) + FAR)
    put("eps", EPS)
    m = np.arange(BIAS_W)
    dist = 255 - m
    ok = (dist >= 0) & (dist < 128)
    d0 = np.maximum(dist, 0)
    large = 16 + (np.log(np.maximum(dist, 1).astype(np.float32) / 16) / np.log(128 / 16) * 16).astype(np.int32)
    bucket = np.where(d0 < 16, d0, np.minimum(large, 31))
    oh = np.zeros((N_BUCKET + 1, BIAS_W), np.float32)
    oh[bucket[ok], m[ok]] = 1.0
    oh[N_BUCKET, ~ok] = NEG
    return c, oh


def task_order():
    t = [f"xT{tt}{q}" for tt in range(TT) for q in range(4)]
    t += ["u0", "u1", "ssmP", "params", "bias", "ssmB0", "ssmB1", "ssmC0", "ssmC1"]
    t += [f"bu{j}" for j in range(HALF)]
    t += ["za0", "za1", "zg0", "zg1", "cq0", "cq1", "y0"]
    t += [f"bu{j}" for j in range(HALF, SSM_TILES)]
    t += ["ckv0", "ckv1", "sq0", "sq1", "skv0", "skv1", "cqT0", "cqT1", "ckvT"]
    t += ["mq00", "mq01", "mq10", "mq11", "mkv00", "mkv01", "mkv10", "mkv11"]
    t += [f"mT0{q}" for q in range(4)]
    t += ["y1", "qnT0", "qnT1", "qrT0", "qrT1", "knT0", "knT1", "krT"]
    t += ["ml0", "ml10", "ml11", "sqT0", "sqT1", "skT"]
    t += [f"mT1{q}" for q in range(4)]
    t += ["xv0", "xv1", "mp0", "mo0", "sl00", "sl01", "mp10", "mp11", "mo1"]
    t += ["glu0", "glu1", "sl10", "sl11", "sl12", "sl13", "xk0", "xk1"]
    t += ["sp00", "sp01", "so0", "sp10", "sp11", "sp12", "sp13", "so1"]
    t += ["kxT0", "kxT1", "gs2", "gs3", "gs0", "cm", "cv", "pw0", "pw1", "gs1"]
    t += [f"wo{n}{tt}" for n in range(4) for tt in range(TT)]
    for tt in range(TT):
        t += [f"cT{tt}{q}" for q in range(4)] + [f"xq{tt}"]
    for tt in range(TT):
        t += [f"qxT{tt}", f"xl{tt}0", f"xl{tt}1"]
    for tt in range(TT):
        t += [f"xp{tt}0", f"xp{tt}1", f"xo{tt}"] + [f"co{n}{tt}" for n in range(4)]
    for tt in range(TT):
        t += [f"hT{tt}{q}" for q in range(4)] + [f"rl{tt}"]
    t += ["pos", "tab"]
    return t


TASKS = task_order()
TASK_NO = {name: i for i, name in enumerate(TASKS)}

IN_COLS = {"u": (2624, 512), "za": (768, 512), "zg": (1280, 512), "cq": (1792, 512), "ckv": (2304, 320),
           "sq": (0, 512), "skv": (512, 256)}
WO_ORDER = (2, 3, 0, 1)


def piece_order():
    w = [(g, q) for g in ("u", "za", "zg", "cq", "ckv", "sq", "skv") for q in range(4)]
    w += [("wqb", 0), ("wqb", 1), ("wkvb", 0)]
    w += [("xv", q) for q in range(4)]
    w += [("glu", 0)]
    w += [("xk", q) for q in range(4)]
    w += [("pw", 0)]
    w += [(f"wo{n}", q) for n in range(4) for q in WO_ORDER]
    w += [("xq", q) for q in range(4)]
    w += [("co", n) for n in range(4)]
    return w


PIECES = piece_order()
LAST_USE = {"u": "u1", "za": "za1", "zg": "zg1", "cq": "cq1", "ckv": "ckv1", "sq": "sq1", "skv": "skv1",
            "wqb": "mq11", "wkvb": "mkv11", "xv": "xv1", "glu": "glu1", "xk": "xk1", "pw": "pw1", "wo0": "wo01",
            "wo1": "wo11", "wo2": "wo21", "wo3": "wo31", "xq": "xq1"}
PIECE_NO = {key: i for i, key in enumerate(PIECES)}
NP = len(PIECES)
MOE_SLOT = [(FRONT_RING + q) % RING for q in range(PPE)]


def spot(h):
    return (h % 2) * 4 + h // 2


HEAD_AT = [2 * (i % 4) + i // 4 for i in range(SWA_H)]

ROW = {}
ROW_SIZE = (("conv_dw_b", 4), ("conv_ln_g", 4), ("conv_ln_b", 4), ("conv_pw_b", 4), ("ssm_glu_b", 4), ("ssm_d", 4),
            ("mix_out_g", 16), ("mla_qn_nope_g", 1), ("mla_kn_nope_g", 1), ("xa_qn_g", 1), ("xa_kn_g", 1),
            ("swa_qn_g", 1), ("swa_kn_g", 1))
NROW = 0
for _n, _w in ROW_SIZE:
    ROW[_n] = NROW
    NROW += _w
TAPS = CONV_W * GC

SEMS = [
    "psum_filled", "psum_drained", "act_order", "dve_order", "pool_order",
    "const_in", "bias_in", "x_in0", "x_in1", "params_in", "ssm_in", "gain_in", "rows_in", "mem_in", "mem1_in",
    "mem_gain_in", "cross_gain_in", "moe_gain_in", "router_in", "dist_out", "band_in", "x2_out",
    "zeroed", "mean_sq", "xn", "step_size", "lam_in", "lam_out", "ssm_lam", "ssm_b", "ssm_c", "scan_done", "gate_th",
    "gated", "conv_done", "cq_n", "ckv_n", "mq_n", "mkv_n", "sq_n", "mem_sq", "mem_n", "gelu_in", "gelu_th", "gelu",
    "ml_max", "ml_exp", "ml_p", "sl_max", "sl_exp", "sl_p", "glu_o", "kx_n", "og_sq", "og_n", "conv_x", "conv_sq",
    "conv_y", "conv_th", "conv_z", "c_sq", "c_n", "qx_n", "xl_max", "xl_exp", "xl_p", "m_sq", "m_n", "g_max",
    "g_exp", "choice", "columns", "tables", "split_h", "sel", "gathered", "xg_ready", "hi_ready", "lo_ready", "split_free",
    "gu_sb", "t_done", "th_done", "hid", "y_sb", "scatter_begun", "y_free", "d_bank", "dw_set", "dest_done", "dest_idx", "scattered",
    "all_scattered", "sink_in", "sel_part", "hid_steps", "ring_free", "pair_sum", "summed", "stored",
]


def trunk(nc, inp, const_d, bucket_d, out):
    ctx = ExitStack()
    with ctx:
        def sb(name, shape, dt=F32, stack=ctx):
            return stack.enter_context(nc.sbuf_tensor(name, shape, dt))

        s = {n: ctx.enter_context(nc.semaphore(n)) for n in SEMS}
        slot_in = [ctx.enter_context(nc.semaphore(f"slot_in{i}")) for i in range(RING)]
        rows_back = [ctx.enter_context(nc.semaphore(f"rows_back{i}")) for i in range(4)]
        bank = [ctx.enter_context(nc.psum_tensor(f"bank{i}", [P, 512], F32)) for i in range(8)]

        dist_d = nc.dram_tensor("dist_scratch", [SWA_H, BIAS_W], F32).ap()
        x2_d = nc.dram_tensor("x2_scratch", [T, D], F32).ap()
        rows_d = nc.dram_tensor("rows_scratch", [ROWS, D], F32).ap()

        K = sb("consts", [P, N_CONST])

        def const(name):
            a, b = CONST[name]
            return K[:, a:b]

        ident = const("ident")
        X = sb("x_tok", [P, TT, D])
        ring = sb("ring", [P, RING * PIECE])
        blk_e = sb("blk_expert", [1, TABLE], I32)
        n_blk = sb("n_blocks", [1, 1], I32)
        off = sb("blk_offset", [P, TABLE])
        posm = sb("pos_masked", [P, TT, N_EXP])
        dv = sb("dest_weight", [P, TT, N_EXP, 2])
        dvs = sb("dest_weight_block", [P, TT, 2])
        dw = sb("slot_row_weight", [P, 2])
        dw_next = sb("next_row_weight", [P, 2])
        slot_row = sb("slot_row", [P, 1], U32)
        tick = sb("tick", [P, 1])
        PR = sb("param_cols", [P, TAPS + NROW])
        SM = sb("small", [P, 320])
        GK = sb("gain_cols", [P, 6])
        BC = sb("row_bcast", [P, 172])

        front = ExitStack()
        HT = sb("hT", [P, KD, T], stack=front)
        OT = sb("oT", [P, KD, T], stack=front)
        XN = sb("xn_tok", [P, D], stack=front)
        GB = sb("gain_rows", [P, D], stack=front)
        UT = sb("uT", [P, GC, T], stack=front)
        ZP = sb("z_padded", [P, GC, T + CONV_W - 1], stack=front)
        CKV = sb("ckv", [P, TT, 320], stack=front)
        KNT = sb("knT", [P, MLA_H, T], stack=front)
        KRT = sb("krT", [P, T], stack=front)
        SQ = sb("sq_tok", [P, TT, GW], stack=front)
        SKV = sb("skv_tok", [P, TT, 256], stack=front)
        SQT = sb("sqT", [P, GC, T], stack=front)
        SKT = sb("skT", [P, SWA_KV, T], stack=front)
        PW = sb("lam_powers", [P, 2, SSM_TILES, SCAN_L], stack=front)
        BL = sb("ssm_b_lhs", [P, 2, 4, P], stack=front)
        CL = sb("ssm_c_lhs", [P, 2, 4, P], stack=front)
        front.close()

        def flat(ap):
            return ap.rearrange("p a b -> p (a b)")

        scr = ring[:, FRONT_RING * PIECE:RING * PIECE]
        XS = scr[:, 0:4096].rearrange("p (c j k l) -> p c j k l", c=2, j=HALF, k=SCAN_L)
        XSt = scr[:, 0:4096].rearrange("p (c j t) -> p c j t", c=2, j=HALF)
        APT = scr[:, 4096:6144]
        L0, L1 = scr[:, 0:2048], scr[:, 7168:9216]
        PT = scr[:, 2048:4096]
        BT = scr[:, 4096:6144].rearrange("p (h j) -> p h j", h=SWA_H)
        CQ = scr[:, 6144:7168].rearrange("p (t n) -> p t n", t=TT)
        QRT = scr[:, 6144:7168].rearrange("p (h t) -> p h t", h=MLA_H)
        CQT = scr[:, 7168:8192].rearrange("p (k t) -> p k t", k=4)
        QNT = CQT
        MQ = scr[:, 8192:9728].rearrange("p (t n) -> p t n", t=TT)
        MKV = scr[:, 9728:11776].rearrange("p (t n) -> p t n", t=TT)
        T1 = scr[:, 11776:12032].rearrange("p (c j k) -> p c j k", c=2, j=HALF)
        T2 = scr[:, 12032:12288].rearrange("p (c j k) -> p c j k", c=2, j=HALF)
        XNO = flat(OT[:, 0:8, :])
        xn_of = [XN[:, :], XNO]
        CKVT = OT[:, 0:2, :]
        KD2 = flat(OT[:, 2:4, :]).rearrange("p (t v n) -> p t v n", t=TT, v=SWA_KV)
        ZG = OT[:, 8:12, :]
        BDm = flat(OT[:, 0:4, :]).rearrange("p (c n) -> p c n", c=2)
        CMm = flat(OT[:, 4:8, :]).rearrange("p (c n) -> p c n", c=2)
        b_raw = flat(OT[:, 12:14, :]).rearrange("p (c n) -> p c n", c=2)
        c_raw = flat(OT[:, 14:16, :]).rearrange("p (c n) -> p c n", c=2)
        SR = flat(SQT[:, :, :]).rearrange("p (r n) -> p r n", r=8)[0:SSM_TILES]
        VR = flat(SQ[:, :, :])
        DSB = flat(SKV[:, :, :])[0:SWA_H, 0:BIAS_W]
        SQG = CL[:, :, :, :].rearrange("p a b c -> p (a b c)").rearrange("p (k t) -> p k t", k=GC)
        RG = PW[:, :, :, :].rearrange("p a b c -> p (a b c)").rearrange("p (r t) -> p r t", r=2)
        ZT = ZP[:, :, 0:T]
        VX = GB[:, 0:1024].rearrange("p (m n) -> p m n", m=2)
        KX = GB[:, 1024:2048].rearrange("p (m n) -> p m n", m=2)
        KXT = UT
        GB2 = scr[:, 2048:4096]
        QX = scr[:, 4096:5120].rearrange("p (t n) -> p t n", t=TT)
        QXT = scr[:, 5120:6144].rearrange("p (k t) -> p k t", k=4)
        XL = scr[:, 6144:8192].rearrange("p (n h w) -> p n h w", n=TT, h=XA_H)
        XPT = scr[:, 8192:10240].rearrange("p (n i q) -> p n i q", n=TT, i=8)
        XOT = scr[:, 10240:11264].rearrange("p (k t) -> p k t", k=4)
        WR = flat(OT[:, 12:16, :])[:, 0:KD * 36].rearrange("p (k n) -> p k n", k=KD)
        RT = flat(OT[:, 8:12, :])
        RB = XN

        WH = sb("w_hi", [P, HI_RING, PIECE], F32R)
        WL = sb("w_lo", [P, LO_RING, PIECE], F32R)
        XG = sb("x_gathered", [P, KD, P], F32R)
        HH = sb("h_hi", [P, TT, D], F32R)
        HL = sb("h_lo", [P, TT, D], F32R)
        HID = sb("hidden", [P, 4, P], F32R)
        SEL = sb("select", [P, TT, P], F32R)
        GU = X[:, 0, 0:1024]
        TH = X[:, 0, 1024:1280]
        H2 = X[:, 0, 1280:1536]
        YS = X[:, 1, :]

        tb = bank[TASK_NO["tab"] % 8]
        others = [b for i, b in enumerate(bank) if i != TASK_NO["tab"] % 8]
        gu, rest, yb, db = others[0:2], others[2:4], others[4:6], others[6]

        def wait_task(eng, name):
            eng.wait_ge(s["psum_drained"], TASK_NO[name] + 1)

        def wait_filled(eng, name):
            eng.wait_ge(s["psum_filled"], TASK_NO[name] + 1)

        class Steps:

            def __init__(self, eng, order):
                self.eng, self.order, self.count = eng, order, {}

            def sent(self, ins, sem=None):
                sem = sem or self.order
                self.count[sem] = self.count.get(sem, 0) + 1
                ins.then_inc(s[sem], 1)
                return sem, self.count[sem]

            def link(self, ins, sem=None):
                sem, n = self.sent(ins, sem)
                self.eng.wait_ge(s[sem], n)

        def col(name, c=0):
            return PR[:, TAPS + ROW[name] + c:TAPS + ROW[name] + c + 1]

        in_w = inp["w_in"][0].rearrange("(p k) n -> p k n", k=KD)

        def piece_source(key):
            g, q = key
            if g in IN_COLS:
                a, n = IN_COLS[g]
                return in_w[:, 4 * q:4 * q + 4, a:a + n], 4, n
            if g in ("xv", "xk", "xq"):
                w = inp[{"xv": "xa_wv", "xk": "xa_wk", "xq": "xa_wq"}[g]][0]
                return w.rearrange("(p k) n -> p k n", k=KD)[:, 4 * q:4 * q + 4, :], 4, 512
            if g in ("glu", "pw"):
                w = inp[{"glu": "ssm_glu_w", "pw": "conv_pw_w"}[g]][0]
                return w.rearrange("(k p) n -> p k n", p=P), 4, 512
            if g == "wqb":
                w = inp["mla_wq_b"][0].rearrange("(p k) n -> p k n", k=4)
                return w[:, :, 384 * q:384 * q + 384], 4, 384
            if g == "wkvb":
                return inp["mla_wkv_b"][0].rearrange("(p k) n -> p k n", k=2), 2, 1024
            if g == "co":
                w = inp["xa_wo"][0].rearrange("(k p) n -> p k n", p=P)
                return w[:, :, 512 * q:512 * q + 512], 4, 512
            n = int(g[2:])
            w = inp["w_out"][0].rearrange("(k p) n -> p k n", p=P)
            return w[:, 4 * q:4 * q + 4, 512 * n:512 * n + 512], 4, 512

        def piece_view(key):
            _, k, n = piece_source(key)
            a = (PIECE_NO[key] % FRONT_RING) * PIECE
            return ring[:, a:a + k * n].rearrange("p (k n) -> p k n", k=k)

        def moe_source(e, q):
            if q < 8:
                w = inp["moe_w_gate" if q < 4 else "moe_w_up"][0].rearrange("e (p k) n -> p e k n", k=KD)
                return w[:, e, 4 * (q % 4):4 * (q % 4) + 4, :]
            w = inp["moe_w_down"][0].rearrange("e (p k) n -> p e k n", k=4)
            return w[:, e, :, 512 * (q - 8):512 * (q - 8) + 512]

        def moe_slot(q):
            a = MOE_SLOT[q] * PIECE
            return ring[:, a:a + PIECE]

        front_uses = [len([n for n in range(NP) if n % FRONT_RING == i]) if i < FRONT_RING else 0
                      for i in range(RING)]

        block = ctx.enter_context(nc.Block())

        @block.sync
        def _(sp):
            sp.dma_start(X[:, 0, :], inp["x"][0, 0:P, :]).then_inc(s["x_in0"], 16)
            sp.dma_start(GB[:, :], inp["ln_mix_g"].to_broadcast([P, D])).then_inc(s["gain_in"], 16)
            sp.dma_start(X[:, 1, :], inp["x"][0, P:T, :]).then_inc(s["x_in1"], 16)
            for i, key in enumerate(PIECES):
                if i >= FRONT_RING:
                    wait_filled(sp, LAST_USE[PIECES[i - FRONT_RING][0]])
                src, _, _ = piece_source(key)
                sp.dma_start(piece_view(key), src).then_inc(slot_in[i % FRONT_RING], 16)
                if key == ("u", 3):
                    sp.wait_ge(s["xn"], 2)
                    wait_filled(sp, "xT03")
                    sp.dma_start(XN[:, :], inp["mem"][0, 0:P, :]).then_inc(s["mem_in"], 16)
                    sp.dma_start(GB[:, :], inp["mem_ln_g"].to_broadcast([P, D])).then_inc(s["mem_gain_in"], 16)
                if key == ("xv", 0):
                    wait_filled(sp, "mT03")
                    sp.dma_start(XN[:, :], inp["mem"][0, P:T, :]).then_inc(s["mem1_in"], 16)
                if key == ("xv", 3):
                    sp.wait_ge(s["dist_out"], 16)
                    sp.wait_ge(s["sq_n"], 3)
                    sp.wait_ge(s["gelu"], 1)
                    for b in range(2):
                        band = bass.AP(dist_d.tensor, BIAS_W * b, [[1, P], [2 * BIAS_W, 4], [1, 2 * P]])
                        sp.dma_start(BT[:, 4 * b:4 * b + 4, :], band).then_inc(s["band_in"], 16)
                if key == ("wo0", WO_ORDER[3]):
                    wait_filled(sp, "so1")
                    sp.dma_start(GB2, inp["ln_cross_g"].to_broadcast([P, D])).then_inc(s["cross_gain_in"], 16)
                if key == ("xq", 1):
                    wait_filled(sp, "wo31")
                    sp.dma_start(WR[:, :, 0:4], inp["moe_w_group"][0].rearrange("(p k) n -> p k n", k=KD)).then_inc(
                        s["router_in"], 16)
                    sp.dma_start(WR[:, :, 4:36], inp["moe_w_expert"][0].rearrange("(p k) n -> p k n", k=KD)).then_inc(
                        s["router_in"], 16)
            wait_filled(sp, "xo1")
            sp.dma_start(GB[:, :], inp["ln_moe_g"].to_broadcast([P, D])).then_inc(s["moe_gain_in"], 16)
            wait_filled(sp, "co31")
            for q in range(PPE):
                sp.dma_start(moe_slot(q).rearrange("p (k n) -> p k n", k=4), moe_source(0, q)).then_inc(
                    slot_in[MOE_SLOT[q]], 16)
                if q == 7:
                    wait_task(sp, "co31")
                    for tt in range(TT):
                        sp.dma_start(x2_d[P * tt:P * tt + P, :], X[:, tt, :]).then_inc(s["x2_out"], 16)
            sp.wait_ge(s["tables"], 1)
            n_reg = sp.value_load(n_blk[0:1, 0:1], min_val=2, max_val=MAX_BLOCKS)

            def load_pieces(block_no, j, qs):
                e = sp.value_load(blk_e[0:1, bass.ds(block_no, 1)], min_val=0, max_val=N_EXP - 1)
                for q in qs:
                    sp.wait_ge(s["lo_ready"], PPE * j + q + 1)
                    sp.dma_start(moe_slot(q).rearrange("p (e k n) -> p e k n", e=1, k=4),
                                 moe_source(bass.ds(e, 1), q)).then_inc(slot_in[MOE_SLOT[q]], 16)

            load_pieces(1, 1, range(8))
            with sp.Fori(2, n_reg) as j:
                load_pieces(j, j, range(8))
                load_pieces(j - 1, j, range(8, PPE))
            load_pieces(n_reg - 1, n_reg, range(8, PPE))
            sp.wait_ge(s["ring_free"], 1)
            sp.wait_ge(s["all_scattered"], 1)
            sp.wait_ge(s["x2_out"], 32)
            for i in range(4):
                tt, half = i // 2, i % 2
                src = rows_d.rearrange("(t p r) d -> t p r d", t=TT, r=4)[tt][:, :, 1024 * half:1024 * half + 1024]
                sp.dma_start(ring[:, 4096 * i:4096 * i + 4096].rearrange("p (r d) -> p r d", r=4), src).then_inc(
                    rows_back[i], 16)
                sp.dma_start(ring[:, 16384 + 1024 * i:16384 + 1024 * i + 1024],
                             x2_d[P * tt:P * tt + P, 1024 * half:1024 * half + 1024]).then_inc(rows_back[i], 16)
            for i in range(4):
                tt, half = i // 2, i % 2
                sp.wait_ge(s["summed"], i + 1)
                sp.dma_start(out[0, P * tt:P * tt + P, 1024 * half:1024 * half + 1024],
                             ring[:, 16384 + 1024 * i:16384 + 1024 * i + 1024]).then_inc(s["stored"], 16)
            sp.wait_ge(s["stored"], 64)

        @block.gpsimd
        def _(pool):
            st = Steps(pool, "pool_order")
            pool.wait_ge(s["gated"], 1)
            wait_task(pool, "params")
            wait_filled(pool, "ssmC1")
            acc, product = OT[:, 4:8, :], ZG
            for w in range(CONV_W):
                tap = PR[:, GC * w:GC * w + GC].unsqueeze(2).to_broadcast([P, GC, T])
                st.link(nc.gpsimd.tensor_tensor(product if w else acc, ZP[:, :, w:w + T], tap, ALU.mult))
                if w:
                    st.link(nc.gpsimd.tensor_tensor(acc, acc, product, ALU.add))
            bias = PR[:, TAPS + ROW["conv_dw_b"]:TAPS + ROW["conv_dw_b"] + GC].unsqueeze(2).to_broadcast([P, GC, T])
            st.link(nc.gpsimd.tensor_tensor(acc, acc, bias, ALU.add), "conv_done")
            pool.wait_ge(s["tables"], 1)
            n_reg = pool.value_load(n_blk[0:1, 0:1], min_val=2, max_val=MAX_BLOCKS)
            pool.sem_inc(s["y_free"], 1)
            with pool.Fori(0, n_reg) as j:
                pool.wait_ge(s["dest_idx"], j + 1)
                pool.wait_ge(s["y_sb"], 4 * j + 9)
                pool.sem_inc(s["scatter_begun"], 1)
                pool.indirect_dma_start(rows_d, bass.IndirectOffsetOnAxis(ap=slot_row[:, :], axis=0), YS, None,
                                        bounds_check=ROWS - 1, oob_is_err=False).then_inc(s["scattered"], 16)
                pool.wait_ge(s["scattered"], 16 * j + 16)
                pool.sem_inc(s["y_free"], 1)
            pool.sem_inc(s["all_scattered"], 1)
            for i in range(4):
                pool.wait_ge(rows_back[i], 32)
                r = ring[:, 4096 * i:4096 * i + 4096].rearrange("p (r d) -> p r d", r=4)
                nc.gpsimd.tensor_tensor(r[:, 0, :], r[:, 0, :], r[:, 1, :], ALU.add).then_inc(s["pair_sum"], 1)

        @block.tensor
        def _(pe):
            task = [0]

            def fill(name, cols=512, parts=P):
                assert TASKS[task[0]] == name, (name, TASKS[task[0]])
                if task[0] >= 8:
                    pe.wait_ge(s["psum_drained"], task[0] - 7)
                task[0] += 1
                return bank[(task[0] - 1) % 8][0:parts, 0:cols]

            def filled(mm):
                mm.then_inc(s["psum_filled"], 1)

            def arrived(key):
                i = PIECE_NO[key]
                pe.wait_ge(slot_in[i % FRONT_RING], 16 * (i // FRONT_RING + 1))


            def transposes(name, ins, parts=P, cols=P):
                b = fill(name, cols=len(ins) * cols, parts=parts)
                for i, a in enumerate(ins):
                    mm = pe.transpose(b[:, cols * i:cols * i + cols], a, ident[0:a.shape[0], 0:a.shape[0]])
                filled(mm)

            def model_transposes(prefix, tt, src):
                v = src.rearrange("p (f k) -> p k f", k=KD)
                for q in range(4):
                    transposes(f"{prefix}{tt}{q}", [v[:, 4 * q + i, :] for i in range(4)])

            def token_major(name, pieces, lhs, tt, n, cols, at=0):
                b = fill(name, cols=cols)
                chunks = [(key, c) for key in pieces for c in range(piece_source(key)[1])]
                for i, (key, c) in enumerate(chunks):
                    if c == 0:
                        arrived(key)
                    mm = pe.matmul(b, lhs(i)[:, P * tt:P * tt + P], piece_view(key)[:, c, at:at + cols],
                                   start=i == 0, stop=i == n - 1)
                filled(mm)
                return mm

            def feature_major(name, pieces, rhs, first, n):
                b = fill(name)
                chunks = [(key, c) for key in pieces for c in range(4)]
                for f in range(2):
                    a = P * (first + f)
                    for i, (key, c) in enumerate(chunks):
                        if c == 0:
                            arrived(key)
                        mm = pe.matmul(b[:, T * f:T * f + T], piece_view(key)[:, c, a:a + P], rhs(i),
                                       start=i == 0, stop=i == n - 1)
                filled(mm)

            def hT(i):
                return HT[:, i, :]

            def b_products(js):
                for j in js:
                    q, jj = j % 4, j // 4
                    b = fill(f"bu{j}")
                    for c in range(2):
                        mm = pe.matmul(b[:, T * c:T * c + T], BL[32 * q:32 * q + 32, c, jj, :],
                                       UT[32 * q:32 * q + 32, jj, :], start=True, stop=True)
                    filled(mm)

            def c_products(half):
                b = fill(f"y{half}")
                for f in range(2):
                    for q in range(4):
                        for c in range(2):
                            mm = pe.matmul(b[32 * q:32 * q + 32, T * f:T * f + T],
                                           CL[:, c, 2 * half + f, 32 * q:32 * q + 32], XSt[:, c, 4 * f + q, :],
                                           start=c == 0, stop=c == 1)
                filled(mm)

            pe.wait_ge(s["const_in"], 16)
            for tt in range(TT):
                pe.wait_ge(s["xn"], tt + 1)
                model_transposes("xT", tt, xn_of[tt])
            wait_task(pe, "xT13")
            u = [("u", q) for q in range(4)]
            feature_major("u0", u, hT, 0, KD)
            feature_major("u1", u, hT, 2, KD)
            pe.wait_ge(s["ssm_lam"], 1)
            transposes("ssmP", [SR[:, r, :] for r in (5, 6, 2, 7)], cols=SSM_TILES)
            pe.wait_ge(s["params_in"], 16 * 16)
            b = fill("params", cols=TAPS + NROW)
            pe.transpose(b[:, 0:TAPS], VR[0:TAPS, 0:P], ident[0:TAPS, 0:TAPS])
            filled(pe.transpose(b[:, TAPS:TAPS + NROW], VR[0:NROW, P:2 * P], ident[0:NROW, 0:NROW]))
            pe.wait_ge(s["bias_in"], 32)
            pe.wait_ge(s["zeroed"], 1)
            filled(pe.matmul(fill("bias", cols=BIAS_W, parts=SWA_H), VR[0:N_BUCKET + 1, 256:264],
                             VR[0:N_BUCKET + 1, 264:264 + BIAS_W], start=True, stop=True))
            for c in range(2):
                pe.wait_ge(s["ssm_b"], 1)
                transposes(f"ssmB{c}", [BDm[:, c, P * i:P * i + P] for i in range(4)])
            for c in range(2):
                pe.wait_ge(s["ssm_c"], 1)
                transposes(f"ssmC{c}", [CMm[:, c, P * i:P * i + P] for i in range(4)])
            wait_task(pe, "ssmB1")
            b_products(range(HALF))
            za, zg = [("za", q) for q in range(4)], [("zg", q) for q in range(4)]
            feature_major("za0", za, hT, 0, KD)
            feature_major("za1", za, hT, 2, KD)
            feature_major("zg0", zg, hT, 0, KD)
            feature_major("zg1", zg, hT, 2, KD)

            def projection(g, cols, names=None):
                for tt in range(TT):
                    token_major(f"{g}{tt}", [(g, q) for q in range(4)], hT, tt, KD, cols)

            projection("cq", 512)
            pe.wait_ge(s["scan_done"], 1)
            wait_task(pe, "ssmC1")
            c_products(0)
            b_products(range(HALF, SSM_TILES))
            projection("ckv", 320)
            projection("sq", 512)
            projection("skv", 256)
            pe.wait_ge(s["cq_n"], 1)
            for tt in range(TT):
                v = CQ[:, tt, :].rearrange("p (f k) -> p k f", k=4)
                transposes(f"cqT{tt}", [v[:, k, :] for k in range(4)])
            pe.wait_ge(s["ckv_n"], 1)
            transposes("ckvT", [CKV[:, tt, 0:256].rearrange("p (f k) -> p k f", k=2)[:, k, :]
                                for k in range(2) for tt in range(TT)])
            wait_task(pe, "cqT1")
            for tt in range(TT):
                for g in range(2):
                    b = fill(f"mq{tt}{g}", cols=384)
                    arrived(("wqb", g))
                    for k in range(4):
                        mm = pe.matmul(b, CQT[:, k, P * tt:P * tt + P], piece_view(("wqb", g))[:, k, :],
                                       start=k == 0, stop=k == 3)
                    filled(mm)
            wait_task(pe, "ckvT")
            for tt in range(TT):
                for g in range(2):
                    b = fill(f"mkv{tt}{g}")
                    arrived(("wkvb", 0))
                    for k in range(2):
                        mm = pe.matmul(b, CKVT[:, k, P * tt:P * tt + P],
                                       piece_view(("wkvb", 0))[:, k, 512 * g:512 * g + 512],
                                       start=k == 0, stop=k == 1)
                    filled(mm)
            pe.wait_ge(s["mem_n"], 1)
            model_transposes("mT", 0, XN)
            pe.wait_ge(s["scan_done"], 2)
            c_products(1)
            pe.wait_ge(s["mq_n"], 1)
            for tt in range(TT):
                transposes(f"qnT{tt}", [MQ[:, tt, QK_D * h:QK_D * h + NOPE] for h in range(MLA_H)])
            for tt in range(TT):
                transposes(f"qrT{tt}", [MQ[:, tt, QK_D * h + NOPE:QK_D * h + QK_D] for h in range(MLA_H)], parts=64)
            pe.wait_ge(s["mkv_n"], 1)
            for tt in range(TT):
                transposes(f"knT{tt}", [MKV[:, tt, 256 * h:256 * h + NOPE] for h in range(MLA_H)])
            transposes("krT", [CKV[:, tt, 256:320] for tt in range(TT)], parts=64)
            wait_task(pe, "krT")

            def latent_scores(name, n, heads):
                w = P * (n + 1)
                b = fill(name, cols=len(heads) * w)
                for i, h in enumerate(heads):
                    q = slice(P * n, P * n + P)
                    o = b[:, w * i:w * i + w]
                    pe.matmul(o, QNT[:, h, q], KNT[:, h, 0:w], start=True, stop=False)
                    mm = pe.matmul(o, QRT[0:64, h, q], KRT[0:64, 0:w], start=False, stop=True)
                filled(mm)

            latent_scores("ml0", 0, range(4))
            latent_scores("ml10", 1, (0, 1))
            latent_scores("ml11", 1, (2, 3))
            pe.wait_ge(s["sq_n"], 3)
            for tt in range(TT):
                transposes(f"sqT{tt}", [SQ[:, tt, P * k:P * k + P] for k in range(GC)])
            transposes("skT", [KD2[:, tt, v, :] for tt in range(TT) for v in range(SWA_KV)])
            pe.wait_ge(s["mem_n"], 2)
            model_transposes("mT", 1, XN)
            wait_task(pe, "mT13")
            for tt in range(TT):
                token_major(f"xv{tt}", [("xv", q) for q in range(4)], hT, tt, KD, 512)

            def latent_output(n):
                b = fill(f"mo{n}")
                for h in range(MLA_H):
                    for kb in range(n + 1):
                        mm = pe.matmul(b[:, P * h:P * h + P], MKV[:, kb, 256 * h + NOPE:256 * h + 256],
                                       PT[:, 512 * n + P * (h * (n + 1) + kb):512 * n + P * (h * (n + 1) + kb) + P],
                                       start=kb == 0, stop=kb == n)
                filled(mm)

            def window_scores(name, n, places):
                w = P * (n + 1)
                b = fill(name, cols=len(places) * w)
                pe.matmul(b.rearrange("p (h w) -> p h w", w=w), const("flip"),
                          BT[:, places[0]:places[0] + len(places), P * (1 - n):], start=True, stop=False)
                for i, at in enumerate(places):
                    h = HEAD_AT[at]
                    r = slice(64 * (h % 2), 64 * (h % 2) + 64)
                    mm = pe.matmul(b[:, w * i:w * i + w], SQT[r, h // 2, P * n:P * n + P], SKT[r, h // 4, 0:w],
                                   start=False, stop=i == len(places) - 1)
                filled(mm)

            def window_output(n):
                b = fill(f"so{n}")
                for at in range(SWA_H):
                    h = HEAD_AT[at]
                    o = b[64 * (h % 2):64 * (h % 2) + 64, P * (h // 2):P * (h // 2) + P]
                    for kb in range(n + 1):
                        a = P * (at * (n + 1) + kb)
                        mm = pe.matmul(o, SKV[:, kb, P + 64 * (h // 4):P + 64 * (h // 4) + 64], PT[:, a:a + P],
                                       start=kb == 0, stop=kb == n)
                filled(mm)

            pe.wait_ge(s["ml_p"], 1)
            transposes("mp0", [L0[:, P * h:P * h + P] for h in range(4)])
            wait_task(pe, "mp0")
            latent_output(0)
            pe.wait_ge(s["band_in"], 32)
            window_scores("sl00", 0, range(4))
            window_scores("sl01", 0, range(4, 8))
            pe.wait_ge(s["ml_p"], 2)
            for i in range(2):
                transposes(f"mp1{i}", [L0[:, 512 * (i + 1) + P * k:512 * (i + 1) + P * k + P] for k in range(4)])
            wait_task(pe, "mp11")
            latent_output(1)
            pe.wait_ge(s["gelu"], 1)
            for i in range(2):
                feature_major(f"glu{i}", [("glu", 0)], lambda k: OT[:, 12 + k, :], 2 * i, GC)
            for i in range(4):
                window_scores(f"sl1{i}", 1, (2 * i, 2 * i + 1))
            for tt in range(TT):
                token_major(f"xk{tt}", [("xk", q) for q in range(4)], hT, tt, KD, 512)
            pe.wait_ge(s["sl_p"], 1)
            for i in range(2):
                transposes(f"sp0{i}", [L1[:, 512 * i + P * k:512 * i + P * k + P] for k in range(4)])
            wait_task(pe, "sp01")
            window_output(0)
            pe.wait_ge(s["sl_p"], 2)
            for i in range(4):
                transposes(f"sp1{i}", [L0[:, 512 * i + P * k:512 * i + P * k + P] for k in range(4)])
            wait_task(pe, "sp13")
            window_output(1)
            pe.wait_ge(s["kx_n"], 1)
            for tt in range(TT):
                transposes(f"kxT{tt}", [KX[:, tt, P * h:P * h + P] for h in range(XA_H)])

            def column_sums(name, src):
                b = fill(name, cols=T)
                for k in range(GC):
                    mm = pe.matmul(b, const("ones"), src[:, k, :], start=k == 0, stop=k == GC - 1)
                filled(mm)

            for i, g in enumerate((2, 3, 0)):
                pe.wait_ge(s["og_sq"], i + 1)
                column_sums(f"gs{g}", SQG)
            pe.wait_ge(s["conv_done"], 1)
            column_sums("cm", OT[:, 4:8, :])
            pe.wait_ge(s["conv_sq"], 1)
            column_sums("cv", SQG)
            pe.wait_ge(s["conv_z"], 1)
            for i in range(2):
                feature_major(f"pw{i}", [("pw", 0)], lambda k: ZT[:, k, :], 2 * i, GC)
            pe.wait_ge(s["og_sq"], 4)
            column_sums("gs1", SQG)
            for n in range(4):
                for tt in range(TT):
                    b = fill(f"wo{n}{tt}")
                    for q in WO_ORDER:
                        arrived((f"wo{n}", q))
                        if n == 0 and tt == 0:
                            pe.wait_ge(s["og_n"], {2: 1, 3: 2, 0: 3, 1: 4}[q])
                        for c in range(4):
                            pe.matmul(b, OT[:, 4 * q + c, P * tt:P * tt + P], piece_view((f"wo{n}", q))[:, c, :],
                                      start=q == WO_ORDER[0] and c == 0, stop=False)
                    filled(pe.matmul(b, ident, X[:, tt, 512 * n:512 * n + 512], start=False, stop=True))
            for tt in range(TT):
                pe.wait_ge(s["c_n"], tt + 1)
                model_transposes("cT", tt, xn_of[tt])
                wait_task(pe, f"cT{tt}3")
                token_major(f"xq{tt}", [("xq", q) for q in range(4)], hT, tt, KD, 512)
            for n in range(TT):
                pe.wait_ge(s["qx_n"], n + 1)
                transposes(f"qxT{n}", [QX[:, n, P * h:P * h + P] for h in range(XA_H)])
                wait_task(pe, f"qxT{n}")
                for i in range(2):
                    b = fill(f"xl{n}{i}")
                    for h in (2 * i, 2 * i + 1):
                        mm = pe.matmul(b[:, T * (h % 2):T * (h % 2) + T], QXT[:, h, P * n:P * n + P], KXT[:, h, :],
                                       start=True, stop=True)
                    filled(mm)
            for n in range(TT):
                pe.wait_ge(s["xl_p"], n + 1)
                for i in range(2):
                    transposes(f"xp{n}{i}", [XL[:, n, 2 * i + h, P * kb:P * kb + P] for h in range(2) for kb in range(2)])
                wait_task(pe, f"xp{n}1")
                b = fill(f"xo{n}")
                for h in range(XA_H):
                    for kb in range(2):
                        mm = pe.matmul(b[:, P * h:P * h + P], VX[:, kb, P * h:P * h + P], XPT[:, n, 2 * h + kb, :],
                                       start=kb == 0, stop=kb == 1)
                filled(mm)
                wait_task(pe, f"xo{n}")
                for c in range(4):
                    arrived(("co", c))
                    b = fill(f"co{c}{n}")
                    for k in range(XA_H):
                        pe.matmul(b, XOT[:, k, P * n:P * n + P], piece_view(("co", c))[:, k, :],
                                  start=k == 0, stop=False)
                    filled(pe.matmul(b, ident, X[:, n, 512 * c:512 * c + 512], start=False, stop=True))
            for tt in range(TT):
                pe.wait_ge(s["m_n"], tt + 1)
                model_transposes("hT", tt, xn_of[tt])
                wait_task(pe, f"hT{tt}3")
                pe.wait_ge(s["router_in"], 32)
                b = fill(f"rl{tt}", cols=36)
                for k in range(KD):
                    mm = pe.matmul(b, HT[:, k, P * tt:P * tt + P], WR[:, k, :], start=k == 0, stop=k == KD - 1)
                filled(mm)
            pe.wait_ge(s["choice"], 1)
            b = fill("pos", cols=96)
            chosen = RT[:, 0:64].rearrange("p (t e) -> p t e", t=TT)
            pe.matmul(b[:, 0:32], const("ltri"), chosen[:, 0, :], start=True, stop=True)
            pe.matmul(b[:, 32:64], const("ones"), chosen[:, 0, :], start=True, stop=False)
            pe.matmul(b[:, 32:64], const("ltri"), chosen[:, 1, :], start=False, stop=True)
            pe.matmul(b[:, 64:96], const("ones"), chosen[:, 0, :], start=True, stop=False)
            filled(pe.matmul(b[:, 64:96], const("ones"), chosen[:, 1, :], start=False, stop=True))
            wait_task(pe, "pos")
            pe.sem_inc(s["split_free"], HI_RING)


            def gather(b, k0):
                for k in range(k0, k0 + 4):
                    for part, h in ((0, HH), (1, HL)):
                        a = P * (k - k0) + SLOTS * part
                        v = h[:, :, :].rearrange("p t (f k) -> p t k f", k=KD)
                        for tt in range(TT):
                            mm = pe.matmul(b[:, a:a + SLOTS], v[:, tt, k, :], SEL[:, tt, 0:SLOTS],
                                           start=tt == 0, stop=tt == TT - 1)
                mm.then_inc(s["gathered"], 1)

            def gate_up(j):
                pe.wait_ge(s["xg_ready"], 4 * j + 4)
                for q in range(8):
                    pe.wait_ge(s["lo_ready"], PPE * j + PPE + q + 1)
                    for c in range(4):
                        for part, w in ((0, WH[:, q % HI_RING, :]), (1, WL[:, q % LO_RING, :])):
                            mm = pe.matmul(gu[q // 4][:, :], XG[:, 4 * (q % 4) + c, :], w[:, FF * c:FF * c + FF],
                                           start=q % 4 == 0 and c == 0 and part == 0,
                                           stop=q % 4 == 3 and c == 3 and part == 1)
                    if q < 7:
                        mm.then_inc(s["split_free"], 1)
                return mm

            def down(j, first, at, parts):
                pe.wait_ge(s["hid"], j)
                for n in parts:
                    pe.wait_ge(s["lo_ready"], PPE * j + PPE + first + n + 1)
                    pe.wait_ge(s["y_sb"], 4 * j + n)
                    for c in range(4):
                        for part, w in ((0, WH[:, (at + n) % HI_RING, :]), (1, WL[:, (at + n) % LO_RING, :])):
                            mm = pe.matmul(yb[n % 2][:, :], HID[:, c, :], w[:, 512 * c:512 * c + 512],
                                           start=c == 0 and part == 0, stop=c == 3 and part == 1)
                    mm.then_inc(s["split_free"], 1)

            def transpose_hidden(j):
                pe.wait_ge(s["gu_sb"], 2 * j + 2)
                for g in range(2):
                    v = GU[:, FF * g:FF * g + FF].rearrange("p (f k) -> p k f", k=4)
                    for k in range(4):
                        mm = pe.matmul(tb[:, 256 * g + SLOTS * k:256 * g + SLOTS * k + SLOTS], v[:, k, :],
                                       const("stack"), start=True, stop=True)
                mm.then_inc(s["t_done"], 1)

            def destinations():
                for tt in range(TT):
                    mm = pe.matmul(db[:, 0:2], SEL[:, tt, :].bitcast(F32), dvs[:, tt, :], start=tt == 0, stop=tt == 1)
                mm.then_inc(s["dest_done"], 1)

            pe.wait_ge(s["split_h"], 4)
            pe.wait_ge(s["sel"], 1)
            for i, b in enumerate([*rest, *gu]):
                gather(b, 4 * i)
                if i == 0:
                    pe.wait_ge(s["columns"], 1)
                    filled(pe.matmul(fill("tab", cols=2 * TABLE), const("ones"), RT[:, 360:360 + 2 * TABLE],
                                     start=True, stop=True))
            destinations()
            gate_up(0).then_inc(s["split_free"], 5)
            pe.wait_ge(s["sel"], 2)
            for i in range(2):
                gather(rest[i], 4 * i)
            transpose_hidden(0)
            for i in range(2):
                gather(gu[i], 8 + 4 * i)
            pe.wait_ge(s["d_bank"], 1)
            destinations()
            n_reg = pe.value_load(n_blk[0:1, 0:1], min_val=2, max_val=MAX_BLOCKS)
            with pe.Fori(1, n_reg) as j:
                gate_up(j).then_inc(s["split_free"], 1)
                down(j, 8, 8, (0, 1))
                pe.wait_ge(s["sel"], j + 2)
                for i in range(2):
                    gather(rest[i], 4 * i)
                down(j, 8, 8, (2, 3))
                transpose_hidden(j)
                for i in range(2):
                    gather(gu[i], 8 + 4 * i)
                pe.wait_ge(s["d_bank"], j + 1)
                destinations()
            down(n_reg, 0, 0, range(4))


        @block.scalar
        def _(act):
            st = Steps(act, "act_order")
            task = [0]

            def load(dst, src, sem):
                act.dma_start(dst, src).then_inc(s[sem], 16)

            load(K[:, :], const_d, "const_in")
            for r, name in enumerate(("ssm_a_re", "ssm_a_im")):
                load(SR[:, r, :], inp[name][0].rearrange("(j g) n -> j (g n)", g=2), "ssm_in")
            load(SM[0:SSM_TILES, 0:2], inp["ssm_log_dt"][0].rearrange("(j g) -> j g", g=2), "ssm_in")
            for c, name in enumerate(("ssm_b_re", "ssm_b_im")):
                load(b_raw[:, c, :].rearrange("p (j i) -> p j i", i=16),
                     inp[name][0].rearrange("(j g) n i -> (g n) j i", g=2), "ssm_in")
            for c, name in enumerate(("ssm_c_re", "ssm_c_im")):
                load(c_raw[:, c, 0:256].rearrange("p (j n) -> p j n", j=4),
                     inp[name][0].rearrange("(j g) o n -> (g o) j n", g=8), "ssm_in")
            load(VR[0:TAPS, 0:P], inp["conv_dw_w"][0].rearrange("w (k p) -> (w k) p", p=P), "params_in")
            for name, n in ROW_SIZE[:11]:
                load(VR[ROW[name]:ROW[name] + n, P:2 * P], inp[name][0].rearrange("(k p) -> k p", p=P), "params_in")
            for name in ("swa_qn_g", "swa_kn_g"):
                for i in range(2):
                    load(VR[ROW[name]:ROW[name] + 1, P + 64 * i:P + 64 * i + 64], inp[name], "params_in")
            load(VR[0:N_BUCKET, 256:264], inp["rel_bias"], "bias_in")
            load(VR[0:N_BUCKET + 1, 264:264 + BIAS_W], bucket_d, "bias_in")
            o = 0
            for name, n in (("swa_sinks", 8), ("mla_qn_rope_g", 64), ("mla_kn_rope_g", 64), ("moe_b_group", 4),
                            ("moe_b_expert", 32)):
                load(BC[:, o:o + n], inp[name].to_broadcast([P, n]), "rows_in")
                o += n
            load(GK[:, 0:4], inp["mla_qa_g"][0].rearrange("(p k) -> p k", k=4), "rows_in")
            load(GK[:, 4:6], inp["mla_kva_g"][0].rearrange("(p k) -> p k", k=2), "rows_in")

            def drain(name, dst, view=None, cols=512, parts=P, func=ACT.Copy, scale=1.0, bias=None):
                assert TASKS[task[0]] == name, (name, TASKS[task[0]])
                act.wait_ge(s["psum_filled"], task[0] + 1)
                src = bank[task[0] % 8][0:parts, 0:cols]
                src = src if view is None else view(src)
                task[0] += 1
                if bias is None:
                    ins = nc.scalar.activation(dst, src, func, scale=scale)
                else:
                    ins = nc.scalar.activation(dst, src, func, bias=bias, scale=scale)
                ins.then_inc(s["psum_drained"], 1)

            def drain_parts(name, parts):
                assert TASKS[task[0]] == name, (name, TASKS[task[0]])
                act.wait_ge(s["psum_filled"], task[0] + 1)
                b = bank[task[0] % 8]
                task[0] += 1
                for i, (dst, src, kw) in enumerate(parts):
                    ins = nc.scalar.activation(dst, src(b), **kw)
                    if i < len(parts) - 1:
                        st.link(ins)
                    else:
                        ins.then_inc(s["psum_drained"], 1)

            def four(n):
                return lambda b: b.rearrange("p (k t) -> p k t", k=n)

            def mean_square(src, junk, at, sem):
                st.link(nc.scalar.activation(junk, src, ACT.Square, scale=float(D) ** -0.5,
                                             accum_out=SM[:, at:at + 1]), sem)

            def drain_model(prefix, tt):
                for q in range(4):
                    drain(f"{prefix}{tt}{q}", HT[:, 4 * q:4 * q + 4, P * tt:P * tt + P], four(4))

            def exps(scores, n, w, base, sem):
                for i in range(n):
                    ins = nc.scalar.activation(scores[:, w * i:w * i + w], scores[:, w * i:w * i + w], ACT.Exp,
                                               bias=SM[:, 224 + base + i:225 + base + i],
                                               accum_out=SM[:, 240 + base + i:241 + base + i])
                    st.link(ins, sem if i == n - 1 else None)

            act.wait_ge(s["x_in0"], 16)
            mean_square(X[:, 0, :], xn_of[0], 144, "mean_sq")
            act.wait_ge(s["x_in1"], 16)
            mean_square(X[:, 1, :], xn_of[1], 145, "mean_sq")
            act.wait_ge(s["ssm_in"], 16 * 7)
            st.link(nc.scalar.activation(SM[0:SSM_TILES, 2:4], SM[0:SSM_TILES, 0:2], ACT.Exp), "step_size")
            drain_model("xT", 0)
            drain_model("xT", 1)
            act.wait_ge(s["lam_in"], 1)
            st.link(nc.scalar.activation(SR[:, 4, :], SR[:, 2, :], ACT.Exp))
            st.link(nc.scalar.activation(SR[:, 6, :], SR[:, 3, :], ACT.Sin))
            st.link(nc.scalar.activation(SR[:, 7, :], SR[:, 3, :], ACT.Sin, scale=0.5), "lam_out")
            drain("u0", UT[:, 0:2, :], four(2))
            drain("u1", UT[:, 2:4, :], four(2))
            drain("ssmP", SM[:, 16:80], cols=64)
            drain("params", PR[:, :], cols=TAPS + NROW)
            drain("bias", DSB, cols=BIAS_W, parts=SWA_H)
            act.wait_ge(s["psum_drained"], TASK_NO["bias"] + 1)
            act.dma_start(dist_d, DSB).then_inc(s["dist_out"], 16)
            for c in range(2):
                drain(f"ssmB{c}", BL[:, c, :, :], four(4))
            for c in range(2):
                drain(f"ssmC{c}", CL[:, c, :, :], four(4), scale=1.0 if c == 0 else -1.0)

            def drain_states(js):
                for j in js:
                    drain(f"bu{j}", XSt[:, :, j % HALF, :], four(2))

            drain_states(range(HALF))
            act.wait_ge(s["zeroed"], 1)
            for i in range(2):
                drain(f"za{i}", ZP[:, 2 * i:2 * i + 2, CONV_W - 1:CONV_W - 1 + T], four(2))
            for i in range(2):
                drain(f"zg{i}", ZG[:, 2 * i:2 * i + 2, :], four(2), func=ACT.Tanh, scale=0.5)
            for tt in range(TT):
                drain(f"cq{tt}", CQ[:, tt, :])
            drain("y0", OT[:, 12:14, :], four(2))
            drain_states(range(HALF, SSM_TILES))
            for tt in range(TT):
                drain(f"ckv{tt}", CKV[:, tt, :], cols=320)
            act.wait_ge(s["psum_drained"], TASK_NO["bias"] + 1)
            for tt in range(TT):
                drain(f"sq{tt}", SQ[:, tt, :])
            act.wait_ge(s["dist_out"], 16)
            for tt in range(TT):
                drain(f"skv{tt}", SKV[:, tt, :], cols=256)
            act.wait_ge(s["rows_in"], 16 * 7)
            for tt in range(TT):
                drain_parts(f"cqT{tt}", [(CQT[:, k, P * tt:P * tt + P], lambda b, k=k: b[:, P * k:P * k + P],
                                          dict(func=ACT.Copy, scale=GK[:, k:k + 1])) for k in range(4)])
            drain_parts("ckvT", [(CKVT[:, k, :], lambda b, k=k: b[:, T * k:T * k + T],
                                  dict(func=ACT.Copy, scale=GK[:, 4 + k:5 + k])) for k in range(2)])
            for tt in range(TT):
                for g in range(2):
                    drain(f"mq{tt}{g}", MQ[:, tt, 384 * g:384 * g + 384], cols=384)
            for tt in range(TT):
                for g in range(2):
                    drain(f"mkv{tt}{g}", MKV[:, tt, 512 * g:512 * g + 512])
            act.wait_ge(s["mem_in"], 16)
            mean_square(XN[:, :], flat(HT[:, 0:8, :]), 146, "mem_sq")
            drain_model("mT", 0)
            drain("y1", OT[:, 14:16, :], four(2))
            act.wait_ge(s["gelu_in"], 1)
            st.link(nc.scalar.activation(APT[:, 0:1024], APT[:, 0:1024], ACT.Tanh, scale=0.7978845608028654),
                    "gelu_th")
            for tt in range(TT):
                drain(f"qnT{tt}", QNT[:, :, P * tt:P * tt + P], four(4), scale=col("mla_qn_nope_g"))
            for tt in range(TT):
                drain(f"qrT{tt}", QRT[0:64, :, P * tt:P * tt + P], four(4), parts=64)
            for tt in range(TT):
                drain(f"knT{tt}", KNT[:, :, P * tt:P * tt + P], four(4), scale=col("mla_kn_nope_g"))
            drain("krT", KRT[0:64, :], cols=T, parts=64)
            mla_scale = float(QK_D) ** -0.5
            drain("ml0", L0[:, 0:512], scale=mla_scale)
            drain("ml10", L0[:, 512:1024], scale=mla_scale)
            drain("ml11", L0[:, 1024:1536], scale=mla_scale)
            for tt in range(TT):
                drain(f"sqT{tt}", SQT[:, :, P * tt:P * tt + P], four(4), scale=SM[:, 152:153])
            drain("skT", SKT[:, :, :].rearrange("p v (t q) -> p t v q", t=TT),
                  lambda b: b.rearrange("p (t v q) -> p t v q", t=TT, v=SWA_KV), scale=col("swa_kn_g"))
            act.wait_ge(s["mem1_in"], 16)
            mean_square(XN[:, :], PT, 147, "mem_sq")
            act.wait_ge(s["ml_max"], 1)
            exps(L0[:, 0:512], 4, P, 0, "ml_exp")
            drain_model("mT", 1)
            for m in range(2):
                drain(f"xv{m}", VX[:, m, :])
            drain("mp0", PT[:, 0:512])
            act.wait_ge(s["conv_done"], 1)
            drain("mo0", OT[:, 8:12, 0:P], four(4))
            act.wait_ge(s["ml_max"], 2)
            exps(L0[:, 512:1536], 4, T, 4, "ml_exp")
            drain("sl00", L1[:, 0:512])
            drain("sl01", L1[:, 512:1024])
            drain("mp10", PT[:, 512:1024])
            drain("mp11", PT[:, 1024:1536])
            drain("mo1", OT[:, 8:12, P:T], four(4))
            for i in range(2):
                drain_parts(f"glu{i}", [(UT[:, 2 * i + f, :], lambda b, f=f: b[:, T * f:T * f + T],
                                         dict(func=ACT.Tanh, scale=0.5, bias=SM[:, 153 + 2 * i + f:154 + 2 * i + f]))
                                        for f in range(2)])
            for i in range(4):
                drain(f"sl1{i}", L0[:, 512 * i:512 * i + 512])
            for m in range(2):
                drain(f"xk{m}", KX[:, m, :])
            act.wait_ge(s["sink_in"], 1)
            st.link(nc.scalar.activation(SM[:, 256:264], SM[:, 256:264], ACT.Exp))
            exps(L1[:, 0:1024], 8, P, 0, "sl_exp")
            drain("sp00", PT[:, 0:512])
            drain("sp01", PT[:, 512:1024])
            drain("so0", OT[:, 0:4, 0:P], four(4))
            act.wait_ge(s["sink_in"], 2)
            st.link(nc.scalar.activation(SM[:, 264:272], SM[:, 264:272], ACT.Exp))
            exps(L0[:, 0:2048], 8, T, 8, "sl_exp")
            for i in range(4):
                drain(f"sp1{i}", PT[:, 512 * i:512 * i + 512])
            drain("so1", OT[:, 0:4, P:T], four(4))
            for m in range(2):
                drain(f"kxT{m}", KXT[:, :, P * m:P * m + P], four(4), scale=col("xa_kn_g"))
            for i, g in enumerate((2, 3, 0)):
                if i:
                    act.wait_ge(s["og_n"], i)
                drain(f"gs{g}", RG[:, 0, :], cols=T, func=ACT.Sqrt, scale=1.0 / GW, bias=const("eps"))
            act.wait_ge(s["og_n"], 3)
            drain("cm", RG[:, 0, :], cols=T, scale=1.0 / GW)
            drain("cv", RG[:, 1, :], cols=T, func=ACT.Sqrt, scale=1.0 / GW, bias=const("eps"))
            act.wait_ge(s["conv_y"], 1)
            st.link(nc.scalar.activation(SQG, ZT, ACT.Tanh, scale=0.5), "conv_th")
            for i in range(2):
                drain_parts(f"pw{i}", [(OT[:, 4 + 2 * i + f, :], lambda b, f=f: b[:, T * f:T * f + T],
                                        dict(func=ACT.Identity, scale=1.0, bias=col("conv_pw_b", 2 * i + f)))
                                       for f in range(2)])
            drain("gs1", RG[:, 0, :], cols=T, func=ACT.Sqrt, scale=1.0 / GW, bias=const("eps"))
            for n in range(4):
                for tt in range(TT):
                    drain(f"wo{n}{tt}", X[:, tt, 512 * n:512 * n + 512])
                    if n == 3:
                        wait_task(act, f"wo3{tt}")
                        mean_square(X[:, tt, :], xn_of[tt], 148 + tt, "c_sq")
            for tt in range(TT):
                drain_model("cT", tt)
                drain(f"xq{tt}", QX[:, tt, :])
            for n in range(TT):
                drain(f"qxT{n}", QXT[:, :, P * n:P * n + P], four(4), scale=col("xa_qn_g"))
                for i in range(2):
                    drain(f"xl{n}{i}", XL[:, n, 2 * i:2 * i + 2, :], four(2), scale=float(P) ** -0.5)
            for n in range(TT):
                act.wait_ge(s["xl_max"], n + 1)
                exps(XL[:, n, :, :].rearrange("p h w -> p (h w)"), 4, T, 4 * n, "xl_exp")
            for n in range(TT):
                for i in range(2):
                    drain(f"xp{n}{i}", XPT[:, n, 4 * i:4 * i + 4, :], four(4))
                drain(f"xo{n}", XOT[:, :, P * n:P * n + P], four(4))
                if n:
                    wait_task(act, "co30")
                    mean_square(X[:, 0, :], xn_of[0], 150, "m_sq")
                for c in range(4):
                    drain(f"co{c}{n}", X[:, n, 512 * c:512 * c + 512])
            wait_task(act, "co31")
            mean_square(X[:, 1, :], xn_of[1], 151, "m_sq")
            for tt in range(TT):
                drain_model("hT", tt)
                drain(f"rl{tt}", RT[:, 128 + 36 * tt:164 + 36 * tt], cols=36)
            act.wait_ge(s["g_max"], 2)
            st.link(nc.scalar.activation(RB[:, 0:8], RB[:, 0:8], ACT.Exp))
            st.link(nc.scalar.activation(RB[:, 8:10], RB[:, 8:10], ACT.Exp), "g_exp")
            drain("pos", RT[:, 256:352], cols=96)
            drain("tab", RT[:, 450:450 + 2 * TABLE], cols=2 * TABLE)
            assert task[0] == len(TASKS)

            wait_task(act, "pos")
            act.wait_ge(s["split_h"], 4)
            act.wait_ge(s["x2_out"], 32)
            act.sem_inc(s["y_sb"], 5)

            def drain_rows(b, k0, n):
                act.wait_ge(s["gathered"], n)
                nc.scalar.activation(XG[:, k0:k0 + 4, :], b[:, :].rearrange("p (k m) -> p k m", k=4),
                                     ACT.Copy).then_inc(s["xg_ready"], 1)

            def high_part(j, at, q):
                seen = 16 * (front_uses[MOE_SLOT[q]] + (1 if q < 8 else 0))
                act.wait_ge(slot_in[MOE_SLOT[q]], 16 * j + seen)
                act.wait_ge(s["split_free"], PPE * j + at + 1)
                return nc.scalar.activation(WH[:, at % HI_RING, :], moe_slot(q), ACT.Copy)

            def drain_gate_up(j):
                act.wait_ge(s["split_free"], PPE * j + HI_RING + 8)
                for g in range(2):
                    nc.scalar.activation(GU[:, FF * g:FF * g + FF], gu[g][:, :], ACT.Copy).then_inc(s["gu_sb"], 1)

            def tanh_gate(j):
                act.wait_ge(s["t_done"], j)
                nc.scalar.activation(TH, tb[:, 0:256], ACT.Tanh, scale=0.5).then_inc(s["th_done"], 1)

            def drain_results(j, first, parts):
                act.wait_ge(s["dest_idx"], j)
                for n in parts:
                    act.wait_ge(s["split_free"], PPE * j + HI_RING + first + n + 1)
                    nc.scalar.activation(YS[:, 512 * n:512 * n + 512], yb[n % 2][:, :], ACT.Copy,
                                         scale=dw[:, 1:2]).then_inc(s["y_sb"], 1)

            for q in range(HI_RING):
                high_part(0, q, q).then_inc(s["hi_ready"], 1)
            for i, b in enumerate([*rest, *gu]):
                drain_rows(b, 4 * i, i + 1)
            for q in range(HI_RING, 8):
                high_part(0, q, q).then_inc(s["hi_ready"], 1 if q < 7 else 5)
            drain_gate_up(0)
            drain_rows(rest[0], 0, 5)
            drain_rows(rest[1], 4, 6)
            act.wait_ge(s["tables"], 1)
            n_reg = act.value_load(n_blk[0:1, 0:1], min_val=2, max_val=MAX_BLOCKS)
            with act.Fori(1, n_reg) as j:
                for q in range(2):
                    high_part(j, q, q).then_inc(s["hi_ready"], 1)
                drain_rows(gu[0], 8, 4 * j + 3)
                drain_rows(gu[1], 12, 4 * j + 4)
                tanh_gate(j)
                for q in range(2, 10):
                    high_part(j, q, q).then_inc(s["hi_ready"], 1)
                high_part(j, 10, 10).then_inc(s["hi_ready"], 1)
                drain_gate_up(j)
                high_part(j, 11, 11).then_inc(s["hi_ready"], 1)
                drain_results(j, 8, (0, 1))
                drain_rows(rest[0], 0, 4 * j + 5)
                drain_rows(rest[1], 4, 4 * j + 6)
                drain_results(j, 8, (2, 3))
            tanh_gate(n_reg)
            for n in range(4):
                high_part(n_reg, n, 8 + n).then_inc(s["hi_ready"], 1)
            drain_results(n_reg, 0, range(4))


        @block.vector
        def _(dve):
            st = Steps(dve, "dve_order")
            link = st.link
            v = nc.vector

            def bc(ap, shape):
                return ap.to_broadcast(shape)

            def rsqrt(r):
                a, y, w = (SM[:, o:o + r] for o in (160, 176, 192))
                link(v.tensor_scalar(w.bitcast(I32), a.bitcast(I32), 1, None, ALU.arith_shift_right))
                link(v.tensor_scalar(y.bitcast(I32), w.bitcast(I32), -1.0, float(0x5F3759DF), ALU.mult, ALU.add))
                for _ in range(3):
                    link(v.tensor_tensor(w, y, y, ALU.mult))
                    link(v.tensor_tensor(w, w, a, ALU.mult))
                    link(v.tensor_scalar(w, w, -0.5, 1.5, ALU.mult, ALU.add))
                    link(v.tensor_tensor(y, y, w, ALU.mult))

            def model_norm(dst, src, gain, at, sem):
                link(v.tensor_scalar(SM[:, 160:161], SM[:, at:at + 1], EPS, None, ALU.add))
                rsqrt(1)
                link(v.scalar_tensor_tensor(dst, src, SM[:, 176:177], gain, ALU.mult, ALU.mult), sem)

            def head_norm(src, tmp, r, d, sem=None):
                t = tmp[:, 0:r * d].rearrange("p (r d) -> p r d", r=r)
                link(v.tensor_tensor(t, src, src, ALU.mult))
                link(v.tensor_reduce(SM[:, 160:160 + r], t, AX.X, ALU.add))
                link(v.tensor_scalar(SM[:, 160:160 + r], SM[:, 160:160 + r], 1.0 / d, EPS, ALU.mult, ALU.add))
                rsqrt(r)
                link(v.tensor_tensor(src, src, bc(SM[:, 176:176 + r].unsqueeze(2), [P, r, d]), ALU.mult), sem)

            def complex_product(dst, a, b, tmp, shape):
                link(v.tensor_tensor(tmp, a[1], b[1], ALU.mult))
                link(v.tensor_tensor(dst[0], a[0], b[0], ALU.mult))
                link(v.tensor_tensor(dst[0], dst[0], tmp, ALU.subtract))
                link(v.tensor_tensor(tmp, a[1], b[0], ALU.mult))
                link(v.tensor_tensor(dst[1], a[0], b[1], ALU.mult))
                link(v.tensor_tensor(dst[1], dst[1], tmp, ALU.add))

            dve.wait_ge(s["gain_in"], 16)
            for tt in range(TT):
                dve.wait_ge(s["mean_sq"], tt + 1)
                model_norm(xn_of[tt], X[:, tt, :], GB[:, :], 144 + tt, "xn")

            dve.wait_ge(s["ssm_in"], 16 * 7)
            dve.wait_ge(s["step_size"], 1)
            dt = bc(SM[0:SSM_TILES, 2:4].unsqueeze(2), [SSM_TILES, 2, 64])

            def row(r):
                return SR[:, r, :]

            def grouped(r):
                return SR[:, r, :].rearrange("p (g n) -> p g n", g=2)

            link(v.tensor_tensor(grouped(2), grouped(0), dt, ALU.mult))
            link(v.tensor_tensor(grouped(3), grouped(1), dt, ALU.mult))
            magic = 12582912.0
            link(v.tensor_scalar(row(5), row(3), 1.0 / (2.0 * np.pi), magic, ALU.mult, ALU.add))
            link(v.tensor_scalar(row(5), row(5), magic, None, ALU.subtract))
            link(v.scalar_tensor_tensor(row(3), row(5), -6.28125, row(3), ALU.mult, ALU.add))
            link(v.scalar_tensor_tensor(row(3), row(5), -(2.0 * np.pi - 6.28125), row(3), ALU.mult, ALU.add))
            link(v.tensor_scalar(row(3), row(3), 3.1415925, -3.1415925, ALU.min, ALU.max), "lam_in")
            link(v.memset(VR[N_BUCKET:N_BUCKET + 1, 256:264], 1.0), "zeroed")
            link(v.memset(ZP[:, :, 0:CONV_W - 1], 0.0))
            dve.wait_ge(s["lam_out"], 1)
            link(v.tensor_tensor(row(7), row(7), row(7), ALU.mult))
            link(v.tensor_scalar(row(7), row(7), -2.0, 1.0, ALU.mult, ALU.add))
            link(v.tensor_tensor(row(5), row(4), row(7), ALU.mult))
            link(v.tensor_tensor(row(6), row(4), row(6), ALU.mult))
            link(v.tensor_tensor(row(4), row(0), row(0), ALU.mult))
            link(v.tensor_tensor(row(7), row(1), row(1), ALU.mult))
            link(v.tensor_tensor(row(4), row(4), row(7), ALU.add))
            link(v.reciprocal(row(4), row(4)))
            link(v.tensor_scalar(row(3), row(5), 1.0, None, ALU.subtract))
            link(v.tensor_tensor(row(2), row(3), row(0), ALU.mult))
            link(v.tensor_tensor(row(7), row(6), row(1), ALU.mult))
            link(v.tensor_tensor(row(2), row(2), row(7), ALU.add))
            link(v.tensor_tensor(row(2), row(2), row(4), ALU.mult))
            link(v.tensor_tensor(row(7), row(6), row(0), ALU.mult))
            link(v.tensor_tensor(row(3), row(3), row(1), ALU.mult))
            link(v.tensor_tensor(row(7), row(7), row(3), ALU.subtract))
            link(v.tensor_tensor(row(7), row(7), row(4), ALU.mult), "ssm_lam")
            wait_filled(dve, "xT13")
            dve.wait_ge(s["const_in"], 16)
            for c in range(2):
                shape = [P, 4, 2, 64]
                out4 = CMm[:, c, :].rearrange("p (j g n) -> p j g n", j=4, g=2)
                link(v.tensor_tensor(out4, bc(c_raw[:, c, 0:256].rearrange("p (j n) -> p j n", j=4).unsqueeze(2), shape),
                                     bc(const("cmask").rearrange("p (g n) -> p g n", g=2).unsqueeze(1), shape),
                                     ALU.mult), "ssm_c" if c else None)
            link(v.memset(BDm, 0.0))
            wait_task(dve, "ssmP")
            lam_r, lam_i, fac_r, fac_i = (SM[:, 16 + 16 * i:32 + 16 * i] for i in range(4))
            bs = [P, SSM_TILES, 16]
            bt = [APT[:, 256 * i:256 * i + 256].rearrange("p (j i) -> p j i", i=16) for i in range(3)]
            complex_product((bt[0], bt[1]), (b_raw[:, 0, 0:256].rearrange("p (j i) -> p j i", i=16),
                                             b_raw[:, 1, 0:256].rearrange("p (j i) -> p j i", i=16)),
                            (bc(fac_r.unsqueeze(2), bs), bc(fac_i.unsqueeze(2), bs)), bt[2], bs)
            for c in range(2):
                for g in range(2):
                    o = BDm[64 * g:64 * g + 64, c, :].rearrange("p (j i) -> p j i", i=32)
                    link(v.tensor_copy(o[:, :, 16 * g:16 * g + 16], bt[c][64 * g:64 * g + 64]),
                         "ssm_b" if c and g else None)
            for c, lam in enumerate((lam_r, lam_i)):
                link(v.tensor_copy(PW[:, c, :, 0:1], lam.unsqueeze(2)))
            for n in (1, 2, 4, 8):
                sh = [P, SSM_TILES, n]
                t = APT[:, 0:SSM_TILES * n].rearrange("p (j n) -> p j n", n=n)
                complex_product((PW[:, 0, :, n:2 * n], PW[:, 1, :, n:2 * n]), (PW[:, 0, :, 0:n], PW[:, 1, :, 0:n]),
                                (bc(PW[:, 0, :, n - 1:n], sh), bc(PW[:, 1, :, n - 1:n], sh)), t, sh)
            signed = []
            for at, power in ((80, 0), (112, SCAN_L - 1)):
                a = SM[:, at:at + 32].rearrange("p (c j) -> p c j", c=2)
                link(v.tensor_copy(a[:, 0, :].unsqueeze(2), PW[:, 1, :, power:power + 1]))
                link(v.tensor_scalar(a[:, 1, :], a[:, 0, :], -1.0, None, ALU.mult))
                signed.append(a)

            def scan_half(half):
                tiles = slice(HALF * half, HALF * half + HALF)

                def step(dst, src, power, sign, t1, t2, shape):
                    re = bc(PW[:, 0, tiles, power].unsqueeze(1).unsqueeze(3), shape)
                    im = bc(sign[:, :, tiles].unsqueeze(3), shape)
                    link(v.tensor_tensor(t1, src, re, ALU.mult))
                    link(v.tensor_tensor(t2, src, im, ALU.mult))
                    link(v.tensor_tensor(dst, dst, t1, ALU.add))
                    link(v.tensor_tensor(dst, dst, t2[:, ::-1], ALU.add))

                for i in range(1, SCAN_L):
                    step(XS[:, :, :, :, i], XS[:, :, :, :, i - 1], 0, signed[0], T1, T2, [P, 2, HALF, SCAN_L])
                for k in range(1, SCAN_L):
                    step(XS[:, :, :, k, SCAN_L - 1:], XS[:, :, :, k - 1, SCAN_L - 1:], SCAN_L - 1, signed[1],
                         T1[:, :, :, 0:1], T2[:, :, :, 0:1], [P, 2, HALF, 1])
                n = SCAN_L - 1
                sh = [P, HALF, n, n]
                t = APT[:, 0:HALF * n * n].rearrange("p (j k l) -> p j k l", j=HALF, k=n)
                for dst, src, power, op in ((0, 0, 0, ALU.add), (0, 1, 1, ALU.subtract), (1, 1, 0, ALU.add),
                                            (1, 0, 1, ALU.add)):
                    link(v.tensor_tensor(t, bc(PW[:, power, tiles, 0:n].unsqueeze(2), sh),
                                         bc(XS[:, src, :, 0:n, n:], sh), ALU.mult))
                    o = XS[:, dst, :, 1:, 0:n]
                    link(v.tensor_tensor(o, o, t, op), "scan_done" if (dst, src) == (1, 0) else None)

            wait_task(dve, f"bu{HALF - 1}")
            scan_half(0)

            wait_task(dve, "zg1")
            zg = ZG
            link(v.tensor_scalar(zg, zg, 0.5, 0.5, ALU.mult, ALU.add))
            za = ZP[:, :, CONV_W - 1:]
            link(v.tensor_tensor(za, za, zg, ALU.mult), "gated")
            wait_task(dve, "cq1")
            head_norm(CQ, APT, TT, 512, "cq_n")
            wait_task(dve, f"bu{SSM_TILES - 1}")
            scan_half(1)

            wait_task(dve, "ckv1")
            head_norm(CKV[:, :, 0:256], APT, TT, 256, "ckv_n")

            def rope(x, heads):
                sh = [P, TT, heads, 32]
                cos, sin = (bc(const(n).rearrange("p (t f) -> p t f", t=TT).unsqueeze(2), sh) for n in ("cos", "sin"))
                a, b, c, d = (APT[:, 256 * i:256 * i + 64 * heads].rearrange("p (t h f) -> p t h f", t=TT, h=heads)
                              for i in range(4))
                x1, x2 = x[:, :, :, 0:32], x[:, :, :, 32:64]
                link(v.tensor_tensor(a, x1, cos, ALU.mult))
                link(v.tensor_tensor(b, x2, sin, ALU.mult))
                link(v.tensor_tensor(c, x1, sin, ALU.mult))
                link(v.tensor_tensor(d, x2, cos, ALU.mult))
                link(v.tensor_tensor(x1, a, b, ALU.subtract))
                return v.tensor_tensor(x2, c, d, ALU.add)

            dve.wait_ge(s["rows_in"], 16 * 7)
            kr = CKV[:, :, 256:320]
            head_norm(kr, APT, TT, 64)
            link(v.tensor_tensor(kr, kr, bc(BC[:, 72:136].unsqueeze(1), [P, TT, 64]), ALU.mult))
            link(rope(kr.unsqueeze(2), 1))
            dve.wait_ge(s["mem_gain_in"], 16)
            wait_task(dve, "mq11")
            q8 = flat(MQ).rearrange("p (r n) -> p r n", n=QK_D)
            head_norm(q8[:, :, 0:NOPE], APT, TT * MLA_H, NOPE)
            qr = q8[:, :, NOPE:QK_D]
            head_norm(qr, APT, TT * MLA_H, ROPE)
            link(v.tensor_tensor(qr, qr, bc(BC[:, 8:72].unsqueeze(1), [P, TT * MLA_H, ROPE]), ALU.mult))
            link(rope(MQ.rearrange("p t (h n) -> p t h n", n=QK_D)[:, :, :, NOPE:QK_D], MLA_H), "mq_n")
            dve.wait_ge(s["mem_sq"], 1)
            model_norm(XN[:, :], XN[:, :], GB[:, :], 146, "mem_n")
            wait_task(dve, "mkv11")
            head_norm(flat(MKV).rearrange("p (r n) -> p r n", n=256)[:, :, 0:NOPE], APT, TT * MLA_H, NOPE, "mkv_n")
            wait_task(dve, "skv1")
            wait_filled(dve, "ssmB1")
            link(v.tensor_scalar(SM[:, 152:153], col("swa_qn_g"), float(SWA_D) ** -0.5, None, ALU.mult))
            link(v.tensor_scalar(SM[:, 153:157], PR[:, TAPS + ROW["ssm_glu_b"]:TAPS + ROW["ssm_glu_b"] + 4], 0.5, None,
                                 ALU.mult))
            head_norm(flat(SQ[:, :, :]).rearrange("p (r n) -> p r n", n=SWA_D), APT, TT * SWA_H, SWA_D, "sq_n")
            for tt in range(TT):
                keys = SKV[:, tt, 0:128].rearrange("p (v n) -> p v n", v=SWA_KV)
                head_norm(keys, APT, SWA_KV, SWA_D)
                link(v.tensor_copy(KD2[:, tt, :, :].rearrange("p v (d n) -> p v d n", d=2),
                                   bc(keys.unsqueeze(2), [P, SWA_KV, 2, SWA_D])), "sq_n")

            wait_task(dve, "y1")
            yo = OT[:, 12:16, :]
            for k in range(GC):
                link(v.scalar_tensor_tensor(yo[:, k, :], UT[:, k, :], col("ssm_d", k), yo[:, k, :], ALU.mult, ALU.add))
            g1 = APT[:, 0:1024].rearrange("p (k t) -> p k t", k=GC)
            link(v.tensor_tensor(g1, yo, yo, ALU.mult))
            link(v.tensor_scalar(g1, g1, 0.044715, 1.0, ALU.mult, ALU.add))
            link(v.tensor_tensor(g1, g1, yo, ALU.mult), "gelu_in")
            dve.wait_ge(s["gelu_th"], 1)
            link(v.tensor_scalar(g1, g1, 0.5, 0.5, ALU.mult, ALU.add))
            link(v.tensor_tensor(yo, yo, g1, ALU.mult), "gelu")

            def row_maximum(scores, n, w, base, sem, sink=None):
                m, neg = SM[:, 208:208 + n], SM[:, 224 + base:224 + base + n]
                link(v.tensor_reduce(m, scores.rearrange("p (h w) -> p h w", w=w), AX.X, ALU.max))
                if sink is not None:
                    link(v.tensor_tensor(m.rearrange("p (b i) -> p b i", b=2), m.rearrange("p (b i) -> p b i", b=2),
                                         sink, ALU.max))
                link(v.tensor_scalar(neg, m, -1.0, None, ALU.mult), sem)

            def normalise(scores, n, w, base, sem):
                sums = SM[:, 240 + base:240 + base + n]
                link(v.reciprocal(sums, sums))
                p3 = scores.rearrange("p (h w) -> p h w", w=w)
                link(v.tensor_tensor(p3, p3, bc(sums.unsqueeze(2), [P, n, w]), ALU.mult), sem)

            wait_task(dve, "ml11")
            for n, scores in ((0, L0[:, 0:512]), (1, L0[:, 512:1536])):
                w = P * (n + 1)
                p3 = scores.rearrange("p (h w) -> p h w", w=w)
                mask = const("causal")[:, P * (1 - n):]
                link(v.tensor_tensor(p3, p3, bc(mask.unsqueeze(1), [P, MLA_H, w]), ALU.add))
                row_maximum(scores, MLA_H, w, 4 * n, "ml_max")
            dve.wait_ge(s["mem_sq"], 2)
            model_norm(XN[:, :], XN[:, :], GB[:, :], 147, "mem_n")
            for n, scores in ((0, L0[:, 0:512]), (1, L0[:, 512:1536])):
                dve.wait_ge(s["ml_exp"], n + 1)
                normalise(scores, MLA_H, P * (n + 1), 4 * n, "ml_p")

            sink = BC[:, 0:8].rearrange("p (i b) -> p b i", b=2)
            for n, scores, last in ((0, L1[:, 0:1024], "sl01"), (1, L0[:, 0:2048], "sl13")):
                w = P * (n + 1)
                wait_task(dve, last)
                row_maximum(scores, SWA_H, w, 8 * n, "sl_max", sink=sink)
                link(v.tensor_tensor(SM[:, 256 + 8 * n:264 + 8 * n].rearrange("p (b i) -> p b i", b=2), sink,
                                     SM[:, 224 + 8 * n:232 + 8 * n].rearrange("p (b i) -> p b i", b=2), ALU.add),
                     "sink_in")
            wait_task(dve, "glu1")
            link(v.tensor_scalar(UT[:, :, :], UT[:, :, :], 0.5, 0.5, ALU.mult, ALU.add))
            link(v.tensor_tensor(yo, yo, UT[:, :, :], ALU.mult), "glu_o")
            for n, scores in ((0, L1[:, 0:1024]), (1, L0[:, 0:2048])):
                dve.wait_ge(s["sl_exp"], n + 1)
                sums = SM[:, 240 + 8 * n:248 + 8 * n]
                link(v.tensor_tensor(sums, sums, SM[:, 256 + 8 * n:264 + 8 * n], ALU.add))
                normalise(scores, SWA_H, P * (n + 1), 8 * n, "sl_p")
            wait_task(dve, "xk1")
            wait_filled(dve, "mT13")
            head_norm(flat(KX).rearrange("p (r n) -> p r n", n=P), XN, TT * XA_H, P, "kx_n")

            def group_norm(i, g, last):
                o = OT[:, 4 * g:4 * g + 4, :]
                if last:
                    wait_task(dve, last)
                link(v.tensor_tensor(SQG, o, o, ALU.mult), "og_sq")
                wait_task(dve, f"gs{g}")
                link(v.reciprocal(RG[:, 0, :], RG[:, 0, :]))
                for k in range(GC):
                    link(v.scalar_tensor_tensor(o[:, k, :], o[:, k, :], col("mix_out_g", 4 * g + k), RG[:, 0, :],
                                                ALU.mult, ALU.mult), "og_n" if k == GC - 1 else None)

            group_norm(0, 2, "mo1")
            group_norm(1, 3, None)
            group_norm(2, 0, "so1")
            oc = OT[:, 4:8, :]
            wait_task(dve, "cm")
            link(v.tensor_tensor(oc, oc, bc(RG[:, 0, :].unsqueeze(1), [P, GC, T]), ALU.subtract))
            link(v.tensor_tensor(SQG, oc, oc, ALU.mult), "conv_sq")
            wait_task(dve, "cv")
            link(v.reciprocal(RG[:, 1, :], RG[:, 1, :]))
            link(v.tensor_tensor(oc, oc, bc(RG[:, 1, :].unsqueeze(1), [P, GC, T]), ALU.mult))
            for k in range(GC):
                link(v.tensor_scalar(ZT[:, k, :], oc[:, k, :], col("conv_ln_g", k), col("conv_ln_b", k), ALU.mult,
                                     ALU.add), "conv_y" if k == GC - 1 else None)
            dve.wait_ge(s["conv_th"], 1)
            link(v.tensor_scalar(SQG, SQG, 0.5, 0.5, ALU.mult, ALU.add))
            link(v.tensor_tensor(ZT, ZT, SQG, ALU.mult), "conv_z")
            group_norm(3, 1, "pw1")

            dve.wait_ge(s["cross_gain_in"], 16)
            for tt in range(TT):
                dve.wait_ge(s["c_sq"], tt + 1)
                model_norm(xn_of[tt], X[:, tt, :], GB2, 148 + tt, "c_n")
            wait_filled(dve, "cT03")
            for tt in range(TT):
                wait_task(dve, f"xq{tt}")
                head_norm(QX[:, tt, :].rearrange("p (r n) -> p r n", n=P), XN, XA_H, P, "qx_n")
            for n in range(TT):
                wait_task(dve, f"xl{n}1")
                row_maximum(XL[:, n].rearrange("p h w -> p (h w)"), XA_H, T, 4 * n, "xl_max")
            for n in range(TT):
                dve.wait_ge(s["xl_exp"], n + 1)
                normalise(XL[:, n].rearrange("p h w -> p (h w)"), XA_H, T, 4 * n, "xl_p")

            dve.wait_ge(s["moe_gain_in"], 16)
            for tt in range(TT):
                dve.wait_ge(s["m_sq"], tt + 1)
                model_norm(xn_of[tt], X[:, tt, :], GB[:, :], 150 + tt, "m_n")
                link(v.tensor_copy(HH[:, tt, :], xn_of[tt]), "split_h")
                link(v.tensor_tensor(HL[:, tt, :], xn_of[tt], HH[:, tt, :].bitcast(F32), ALU.subtract), "split_h")

            wait_task(dve, "rl1")
            wait_filled(dve, "hT03")
            RL = RT[:, 128:200].rearrange("p (t n) -> p t n", t=TT)
            link(v.tensor_tensor(RL, RL, bc(BC[:, 136:172].unsqueeze(1), [P, TT, 36]), ALU.add))
            place = [16]

            def take(*shape):
                n = int(np.prod(shape))
                a = RB[:, place[0]:place[0] + n]
                place[0] += n
                if len(shape) == 1:
                    return a
                if len(shape) == 2:
                    return a.rearrange("p (a b) -> p a b", a=shape[0])
                return a.rearrange("p (a b c) -> p a b c", a=shape[0], b=shape[1])

            far = 64.0
            numbers = const("i32")

            def first_max(x, n, top, which, one_hot):
                t = take(TT, n)
                link(v.tensor_reduce(top, x, AX.X, ALU.max))
                link(v.tensor_tensor(t, x, bc(top.unsqueeze(2), [P, TT, n]), ALU.is_equal))
                link(v.tensor_scalar(t, t, -far, far, ALU.mult, ALU.add))
                link(v.tensor_tensor(t, t, bc(numbers[:, 0:n].unsqueeze(1), [P, TT, n]), ALU.add))
                link(v.tensor_reduce(which, t, AX.X, ALU.min))
                link(v.tensor_tensor(one_hot, bc(numbers[:, 0:n].unsqueeze(1), [P, TT, n]),
                                     bc(which.unsqueeze(2), [P, TT, n]), ALU.is_equal))

            g_top, g_at, g_hot = take(TT), take(TT), take(TT, N_GROUPS)
            first_max(RL[:, :, 0:4], N_GROUPS, g_top, g_at, g_hot)
            link(v.tensor_tensor(RB[:, 0:8].rearrange("p (t n) -> p t n", t=TT), RL[:, :, 0:4],
                                 bc(g_top.unsqueeze(2), [P, TT, N_GROUPS]), ALU.subtract), "g_max")
            in_g = take(TT, N_GROUPS, PER_GROUP)
            shape = [P, TT, N_GROUPS, PER_GROUP]
            link(v.tensor_tensor(in_g, RL[:, :, 4:36].rearrange("p t (g e) -> p t g e", g=N_GROUPS),
                                 bc(g_hot.unsqueeze(3), shape), ALU.mult))
            el = take(TT, PER_GROUP)
            link(v.tensor_reduce(el, in_g.rearrange("p t g e -> p t e g"), AX.X, ALU.add))
            tops, ats, hots = [], [], []
            for k in range(2):
                tops.append(take(TT))
                ats.append(take(TT))
                hots.append(take(TT, PER_GROUP))
                first_max(el, PER_GROUP, tops[k], ats[k], hots[k])
                if k == 0:
                    link(v.scalar_tensor_tensor(el, hots[0], NEG, el, ALU.mult, ALU.add))
            link(v.tensor_tensor(RB[:, 8:10], tops[1], tops[0], ALU.subtract), "g_max")
            marks = [take(TT, N_EXP) for _ in range(2)]
            for k in range(2):
                e_at = take(TT)
                link(v.scalar_tensor_tensor(e_at, g_at, float(PER_GROUP), ats[k], ALU.mult, ALU.add))
                link(v.tensor_tensor(marks[k], bc(numbers.unsqueeze(1), [P, TT, N_EXP]),
                                     bc(e_at.unsqueeze(2), [P, TT, N_EXP]), ALU.is_equal))
            chosen = RT[:, 0:64].rearrange("p (t e) -> p t e", t=TT)
            link(v.tensor_tensor(chosen, marks[0], marks[1], ALU.add), "choice")
            dve.wait_ge(s["g_exp"], 1)
            gs, p1, w1, w2 = take(TT), take(TT), take(TT), take(TT)
            link(v.tensor_reduce(gs, RB[:, 0:8].rearrange("p (t n) -> p t n", t=TT), AX.X, ALU.add))
            link(v.tensor_scalar(p1, RB[:, 8:10], 1.0, None, ALU.add))
            link(v.tensor_tensor(p1, p1, gs, ALU.mult))
            link(v.reciprocal(p1, p1))
            link(v.tensor_scalar(w1, p1, 0.5, None, ALU.mult))
            link(v.tensor_tensor(w2, w1, RB[:, 8:10], ALU.mult))
            row2 = take(TT)
            link(v.tensor_scalar(row2, const("row0"), 2.0, None, ALU.add))
            t = take(TT, N_EXP)
            for part, (a, b) in enumerate(((const("row0"), row2), (w1, w2))):
                o = dv[:, :, :, part]
                link(v.tensor_tensor(t, marks[1], bc(b.unsqueeze(2), [P, TT, N_EXP]), ALU.mult))
                link(v.tensor_tensor(o, marks[0], bc(a.unsqueeze(2), [P, TT, N_EXP]), ALU.mult))
                link(v.tensor_tensor(o, o, t, ALU.add))
            wait_task(dve, "pos")
            link(v.tensor_scalar(posm[:, :, :], RT[:, 256:320].rearrange("p (t e) -> p t e", t=TT), 1.0, None, ALU.add))
            link(v.tensor_tensor(posm[:, :, :], posm[:, :, :], chosen, ALU.mult))
            link(v.tensor_scalar(posm[:, :, :], posm[:, :, :], 1.0, None, ALU.subtract))
            for tt in range(TT):
                link(v.tensor_scalar(SEL[:, tt, :], const("slot"), posm[:, tt, 0:1], None, ALU.is_equal), "sel_part")
            link(v.tensor_copy(dvs[:, :, :].unsqueeze(2), dv[:, :, 0:1, :]), "sel")
            cnt = RT[:, 320:352]
            nb, cum, start = take(N_EXP), take(N_EXP), take(N_EXP)
            link(v.tensor_scalar(nb, cnt, 0.0, None, ALU.is_gt))
            for m in range(1, T // SLOTS):
                link(v.scalar_tensor_tensor(nb, cnt, float(m * SLOTS), nb, ALU.is_gt, ALU.add))
            link(v.tensor_scalar(nb[:, 0:1], nb[:, 0:1], 1.0, None, ALU.max))
            link(v.tensor_tensor_scan(cum, const("ones")[:, 0:N_EXP], nb, 0.0, ALU.mult, ALU.add))
            link(v.tensor_tensor(start, cum, nb, ALU.subtract))
            link(v.tensor_copy(n_blk[:, :], cum[0:1, N_EXP - 1:N_EXP]))
            be, first, started = take(1), take(1), take(N_EXP)
            link(v.tensor_scalar(started, cum, const("part"), None, ALU.is_le))
            link(v.tensor_reduce(be, started, AX.X, ALU.add))
            link(v.scalar_tensor_tensor(started, start, const("part"), start, ALU.is_le, ALU.mult))
            link(v.tensor_reduce(first, started, AX.X, ALU.max))
            link(v.tensor_tensor(first, const("part"), first, ALU.subtract))
            assert place[0] <= D
            link(v.tensor_scalar(RT[:, 360:360 + TABLE], ident[:, 0:TABLE], be, None, ALU.mult))
            link(v.tensor_scalar(RT[:, 360 + TABLE:360 + 2 * TABLE], ident[:, 0:TABLE], first, None, ALU.mult),
                 "columns")
            wait_task(dve, "tab")
            link(v.tensor_scalar(blk_e[:, :], RT[0:1, 450:450 + TABLE], float(N_EXP - 1), None, ALU.min))
            link(v.tensor_scalar(off[:, :], RT[:, 450 + TABLE:450 + 2 * TABLE], float(SLOTS), None, ALU.mult), "tables")

            def select(b, e):
                for tt in range(TT):
                    nc.vector.tensor_scalar(SEL[:, tt, :], const("slot"), off[:, bass.ds(b, 1)],
                                            posm[:, tt, bass.ds(e, 1)], ALU.add, ALU.is_equal).then_inc(
                        s["sel_part"], 1)
                return nc.vector.tensor_copy(dvs[:, :, :].unsqueeze(2), dv[:, :, bass.ds(e, 1), :])


            dve.sem_inc(s["lo_ready"], PPE)
            dve.sem_inc(s["hid_steps"], 3)

            def low_part(j, at, q):
                dve.wait_ge(s["hi_ready"], PPE * j + at + 1)
                dve.wait_ge(s["split_free"], PPE * j + at + 1 + HI_RING - LO_RING)
                return nc.vector.tensor_tensor(WL[:, at % LO_RING, :], moe_slot(q),
                                               WH[:, at % HI_RING, :].bitcast(F32), ALU.subtract)

            def use_destinations(j):
                dve.wait_ge(s["y_free"], j)
                nc.vector.tensor_copy(dw[:, :], dw_next[:, :]).then_inc(s["dw_set"], 1)
                dve.wait_ge(s["dw_set"], j)
                nc.vector.tensor_scalar(slot_row[:, :], dw[:, 0:1], const("half"), None, ALU.add).then_inc(
                    s["dest_idx"], 1)

            def take_destinations(j):
                dve.wait_ge(s["dest_done"], j + 1)
                nc.vector.tensor_copy(dw_next[:, :], db[:, 0:2]).then_inc(s["d_bank"], 1)

            def hidden(j):
                dve.wait_ge(s["th_done"], j)
                nc.vector.scalar_tensor_tensor(H2, TH, 1.0, tb[:, 0:256], ALU.add, ALU.mult).then_inc(
                    s["hid_steps"], 1)
                dve.wait_ge(s["hid_steps"], 3 * j + 1)
                nc.vector.tensor_tensor(H2, H2, tb[:, 256:512], ALU.mult).then_inc(s["hid_steps"], 1)
                dve.wait_ge(s["hid_steps"], 3 * j + 2)
                h4 = H2.rearrange("p (k m) -> p k m", k=4)
                nc.vector.tensor_copy(HID[:, :, 0:SLOTS], h4).then_inc(s["hid_steps"], 1)
                dve.wait_ge(s["hid_steps"], 3 * j + 3)
                nc.vector.tensor_tensor(HID[:, :, SLOTS:P], h4, HID[:, :, 0:SLOTS].bitcast(F32),
                                        ALU.subtract).then_inc(s["hid"], 1)

            for q in range(2):
                low_part(0, q, q).then_inc(s["lo_ready"], 1)
            take_destinations(0)
            e1 = dve.value_load(blk_e[0:1, 1:2], min_val=0, max_val=N_EXP - 1)
            select(1, e1).then_inc(s["sel"], 1)
            for q in range(2, 8):
                low_part(0, q, q).then_inc(s["lo_ready"], 1 if q < 7 else 5)
            n_reg = dve.value_load(n_blk[0:1, 0:1], min_val=2, max_val=MAX_BLOCKS)
            with dve.Fori(1, n_reg) as j:
                for q in range(2):
                    low_part(j, q, q).then_inc(s["lo_ready"], 1)
                e = dve.value_load(blk_e[0:1, bass.ds(j + 1, 1)], min_val=0, max_val=N_EXP - 1)
                dve.wait_ge(s["dest_done"], j + 1)
                select(j + 1, e).then_inc(s["sel"], 1)
                low_part(j, 2, 2).then_inc(s["lo_ready"], 1)
                hidden(j)
                for q in range(3, 6):
                    low_part(j, q, q).then_inc(s["lo_ready"], 1)
                use_destinations(j)
                take_destinations(j)
                for q in range(6, PPE):
                    low_part(j, q, q).then_inc(s["lo_ready"], 1)
            use_destinations(n_reg)
            hidden(n_reg)
            for n in range(4):
                low_part(n_reg, n, 8 + n).then_inc(s["lo_ready"], 1)
            link(v.memset(tick[:, :], 0.0), "ring_free")
            for i in range(4):
                dve.wait_ge(rows_back[i], 32)
                r = ring[:, 4096 * i:4096 * i + 4096].rearrange("p (r d) -> p r d", r=4)
                xo = ring[:, 16384 + 1024 * i:16384 + 1024 * i + 1024]
                link(v.tensor_tensor(xo, xo, r[:, 2, :], ALU.add))
                link(v.tensor_tensor(xo, xo, r[:, 3, :], ALU.add))
                dve.wait_ge(s["pair_sum"], i + 1)
                link(v.tensor_tensor(xo, xo, r[:, 0, :], ALU.add), "summed")


_INS = ['x', 'mem', 'rel_bias', 'ln_mix_g', 'w_in', 'swa_qn_g', 'swa_kn_g', 'swa_sinks', 'conv_dw_w', 'conv_dw_b',
        'conv_ln_g', 'conv_ln_b', 'conv_pw_w', 'conv_pw_b', 'mla_qa_g', 'mla_kva_g', 'mla_wq_b', 'mla_wkv_b',
        'mla_qn_nope_g', 'mla_qn_rope_g', 'mla_kn_nope_g', 'mla_kn_rope_g', 'ssm_a_re', 'ssm_a_im', 'ssm_log_dt',
        'ssm_b_re', 'ssm_b_im', 'ssm_c_re', 'ssm_c_im', 'ssm_d', 'ssm_glu_w', 'ssm_glu_b', 'mix_out_g', 'w_out',
        'ln_cross_g', 'mem_ln_g', 'xa_wq', 'xa_wk', 'xa_wv', 'xa_qn_g', 'xa_kn_g', 'xa_wo', 'ln_moe_g',
        'moe_w_group', 'moe_b_group', 'moe_w_expert', 'moe_b_expert', 'moe_w_gate', 'moe_w_up', 'moe_w_down']


def kernel(**inputs):
    import concourse.bacc as _bacc
    from concourse.bass_utils import run_bass_kernel_spmd as _run

    nc = _bacc.Bacc("TRN2", target_bir_lowering=False, num_devices=1)
    arrays, args = {}, {}
    for name in _INS:
        a = np.ascontiguousarray(inputs[name])
        arrays[f"in_{name}_dram"] = a
        args[name] = nc.dram_tensor(f"in_{name}_dram", a.shape, mybir.dt.from_np(a.dtype), kind="ExternalInput").ap()
    fixed = []
    for name, a in zip(("const", "bucket"), constants()):
        arrays[f"in_{name}_dram"] = a
        fixed.append(nc.dram_tensor(f"in_{name}_dram", a.shape, F32, kind="ExternalInput").ap())
    out = nc.dram_tensor("out_0_dram", (1, T, D), F32, kind="ExternalOutput").ap()
    trunk(nc, args, *fixed, out)
    r = _run(nc, [arrays], core_ids=[0])
    return r.results[0]["out_0_dram"]
```

```python
from contextlib import ExitStack

import numpy as np
import concourse.bass as bass
from concourse import mybir

F32 = mybir.dt.float32
F32R = mybir.dt.float32r
I32 = mybir.dt.int32
U32 = mybir.dt.uint32
ALU = mybir.AluOpType
ACT = mybir.ActivationFunctionType
AX = mybir.AxisListType

P = 128
T = 256
TT = T // P
D = 2048
KD = D // P
GW = 512
GC = GW // P
EPS = 1e-6
NEG = -1e30
SWA_H, SWA_KV, SWA_D = 8, 2, 64
CONV_W = 31
MLA_H, NOPE, ROPE = 4, 128, 64
QK_D = NOPE + ROPE
XA_H = 4
SSM_TILES = 16
HALF = SSM_TILES // 2
SCAN_L = 16
N_GROUPS, PER_GROUP = 4, 8
N_EXP = N_GROUPS * PER_GROUP
FF = 512
SLOTS = 32
S2 = 2 * SLOTS
MAX_BLOCKS = N_EXP + 2 * T // SLOTS
TABLE = MAX_BLOCKS + 2
ROWS = 4 * T
FAR = 4.0 * ROWS
PIECE = 2048
RING = 12
FRONT_RING = 6
PPE = 12
HI_RING, LO_RING = 3, 3

CONST = {}
_at = 0
for _n, _w in (("ident", 128), ("flip", 128), ("ones", 128), ("ltri", 128), ("causal", 256), ("cmask", 128), ("slot", S2),
               ("stack", SLOTS), ("i32", 32), ("cos", 64), ("sin", 64), ("row0", 2),
               ("half", 1), ("eps", 1), ("part", 1)):
    CONST[_n] = (_at, _at + _w)
    _at += _w
N_CONST = _at
BIAS_W = 384
N_BUCKET = 32


def constants():
    c = np.zeros((P, N_CONST), np.float32)

    def put(name, a):
        c[:, CONST[name][0]:CONST[name][1]] = a

    p = np.arange(P)
    put("ident", np.eye(P))
    put("flip", np.eye(P)[::-1])
    put("ones", 1.0)
    put("ltri", p[:, None] < p[None, :])
    put("causal", np.concatenate([np.zeros((P, P)), np.where(p[None, :] <= p[:, None], 0.0, NEG)], 1))
    put("cmask", ((p[:, None] // 16) % 2) == (p[None, :] // 64))
    put("slot", np.arange(S2)[None, :] % SLOTS)
    put("stack", (p[:, None] % SLOTS) == np.arange(SLOTS)[None, :])
    put("i32", np.arange(N_EXP)[None, :])
    put("part", p[:, None])
    inv = (1.0 / (np.float32(10000.0) ** (np.arange(0, ROPE, 2, dtype=np.float32) / np.float32(ROPE)))).astype(np.float32)
    ang = np.arange(T, dtype=np.float32)[:, None] * inv[None, :]
    put("cos", np.cos(ang).reshape(TT, P, 32).transpose(1, 0, 2).reshape(P, 64))
    put("sin", np.sin(ang).reshape(TT, P, 32).transpose(1, 0, 2).reshape(P, 64))
    put("row0", 4.0 * (p[:, None] + P * np.arange(TT)[None, :]) - FAR)
    put("half", (p[:, None] // SLOTS) + FAR)
    put("eps", EPS)
    m = np.arange(BIAS_W)
    dist = 255 - m
    ok = (dist >= 0) & (dist < 128)
    d0 = np.maximum(dist, 0)
    large = 16 + (np.log(np.maximum(dist, 1).astype(np.float32) / 16) / np.log(128 / 16) * 16).astype(np.int32)
    bucket = np.where(d0 < 16, d0, np.minimum(large, 31))
    oh = np.zeros((N_BUCKET + 1, BIAS_W), np.float32)
    oh[bucket[ok], m[ok]] = 1.0
    oh[N_BUCKET, ~ok] = NEG
    return c, oh


def task_order():
    t = [f"xT{tt}{q}" for tt in range(TT) for q in range(4)]
    t += ["u0", "u1", "ssmP", "params", "bias", "za0", "ssmB0", "ssmB1", "ssmC0", "ssmC1"]
    t += [f"bu{j}" for j in range(HALF)]
    t += ["za1", "zg0", "zg1", "cq0", "y0"]
    t += [f"bu{j}" for j in range(HALF, SSM_TILES)]
    t += ["cq1", "ckv0", "ckv1", "sq0", "sq1", "skv0", "skv1", "y1"]
    t += [f"mT0{q}" for q in range(4)]
    t += ["cqT0", "cqT1", "ckvT", "mq00", "mq01", "mq10", "mq11", "mkv00", "mkv01", "mkv10", "mkv11"]
    t += ["sqT0", "sqT1", "skT"] + [f"mT1{q}" for q in range(4)]
    t += ["xv0", "qnT0", "qnT1", "qrT0", "qrT1", "knT0", "knT1", "krT"]
    t += ["ml0", "ml10", "ml11", "sl00", "sl01", "xv1", "mp0", "mo0", "mp10", "mp11", "mo1"]
    t += ["glu0", "glu1", "cm", "sl10", "sl11", "sl12", "sl13", "xk0", "cv", "gs2"]
    t += ["sp00", "sp01", "so0", "xk1", "gs3", "pw0", "pw1", "sp10", "sp11", "sp12", "sp13", "so1"]
    t += ["kxT0", "kxT1", "gs1", "gs0"]
    t += [f"wo{n}{tt}" for n in range(4) for tt in range(TT)]
    for tt in range(TT):
        t += [f"cT{tt}{q}" for q in range(4)] + [f"xq{tt}"]
    for tt in range(TT):
        t += [f"qxT{tt}", f"xl{tt}0", f"xl{tt}1"]
    for tt in range(TT):
        t += [f"xp{tt}0", f"xp{tt}1", f"xo{tt}"] + [f"co{n}{tt}" for n in range(4)]
    for tt in range(TT):
        t += [f"hT{tt}{q}" for q in range(4)] + [f"rl{tt}"]
    t += ["pos", "tab"]
    return t


TASKS = task_order()
TASK_NO = {name: i for i, name in enumerate(TASKS)}

IN_COLS = {"u": (2624, 512), "za": (768, 512), "zg": (1280, 512), "cq": (1792, 512), "ckv": (2304, 320),
           "sq": (0, 512), "skv": (512, 256)}
WO_ORDER = (2, 3, 1, 0)


def piece_order():
    w = [(g, q) for g in ("u", "za", "zg", "cq", "ckv", "sq", "skv") for q in range(4)]
    w += [("wqb", 0), ("wqb", 1), ("wkvb", 0)]
    w += [("xv", q) for q in range(4)]
    w += [("glu", 0), ("pw", 0)]
    w += [("xk", q) for q in range(4)]
    w += [(f"wo{n}", q) for n in range(4) for q in WO_ORDER]
    w += [("xq", q) for q in range(4)]
    w += [("co", n) for n in range(4)]
    return w


PIECES = piece_order()
LAST_USE = {"u": "u1", "za": "za1", "zg": "zg1", "cq": "cq1", "ckv": "ckv1", "sq": "sq1", "skv": "skv1",
            "wqb": "mq11", "wkvb": "mkv11", "xv": "xv1", "glu": "glu1", "xk": "xk1", "pw": "pw1", "wo0": "wo01",
            "wo1": "wo11", "wo2": "wo21", "wo3": "wo31", "xq": "xq1"}
PIECE_NO = {key: i for i, key in enumerate(PIECES)}
NP = len(PIECES)
MOE_SLOT = [(FRONT_RING + q) % RING for q in range(PPE)]


def spot(h):
    return (h % 2) * 4 + h // 2


HEAD_AT = [2 * (i % 4) + i // 4 for i in range(SWA_H)]

ROW = {}
ROW_SIZE = (("conv_dw_b", 4), ("conv_ln_g", 4), ("conv_ln_b", 4), ("conv_pw_b", 4), ("ssm_glu_b", 4), ("ssm_d", 4),
            ("mix_out_g", 16), ("mla_qn_nope_g", 1), ("mla_kn_nope_g", 1), ("xa_qn_g", 1), ("xa_kn_g", 1),
            ("swa_qn_g", 1), ("swa_kn_g", 1))
NROW = 0
for _n, _w in ROW_SIZE:
    ROW[_n] = NROW
    NROW += _w
TAPS = CONV_W * GC

SEMS = [
    "psum_filled", "psum_drained", "act_order", "dve_order", "pool_order",
    "const_in", "bias_in", "x_in0", "x_in1", "params_in", "ssm_in", "gain_in", "rows_in", "mem_in", "mem1_in",
    "mem_gain_in", "cross_gain_in", "moe_gain_in", "router_in", "dist_out", "band_in", "x2_out",
    "zeroed", "mean_sq", "xn", "step_size", "lam_in", "lam_out", "ssm_lam", "ssm_b", "ssm_c", "scan_done", 
    "conv_done", "cq_n", "ckv_n", "mq_n", "mkv_n", "sq_n", "mem_sq", "mem_n", "gelu_in", "gelu_th", "gelu",
    "ml_max", "ml_exp", "ml_p", "sl_max", "sl_exp", "sl_p", "glu_o", "kx_n", "og_sq", "og_n", "conv_sq",
    "conv_y", "conv_th", "conv_z", "c_sq", "c_n", "qx_n", "xl_max", "xl_exp", "xl_p", "m_sq", "m_n", "g_max",
    "g_exp", "choice", "columns", "tables", "split_h", "sel", "gathered", "xg_ready", "hi_ready", "lo_ready", "split_free",
    "gu_sb", "t_done", "th_done", "hid", "y_sb", "scatter_begun", "y_free", "d_bank", "dw_set", "dest_done", "dest_idx", "scattered",
    "all_scattered", "sink_in", "sel_part", "hid_steps", "ring_free", "pair_sum", "summed", "stored",
]


def trunk(nc, inp, const_d, bucket_d, out):
    ctx = ExitStack()
    with ctx:
        def sb(name, shape, dt=F32, stack=ctx):
            return stack.enter_context(nc.sbuf_tensor(name, shape, dt))

        s = {n: ctx.enter_context(nc.semaphore(n)) for n in SEMS}
        slot_in = [ctx.enter_context(nc.semaphore(f"slot_in{i}")) for i in range(RING)]
        rows_back = [ctx.enter_context(nc.semaphore(f"rows_back{i}")) for i in range(4)]
        bank = [ctx.enter_context(nc.psum_tensor(f"bank{i}", [P, 512], F32)) for i in range(8)]

        dist_d = nc.dram_tensor("dist_scratch", [SWA_H, BIAS_W], F32).ap()
        x2_d = nc.dram_tensor("x2_scratch", [T, D], F32).ap()
        rows_d = nc.dram_tensor("rows_scratch", [ROWS, D], F32).ap()

        K = sb("consts", [P, N_CONST])

        def const(name):
            a, b = CONST[name]
            return K[:, a:b]

        ident = const("ident")
        X = sb("x_tok", [P, TT, D])
        ring = sb("ring", [P, RING * PIECE])
        blk_e = sb("blk_expert", [1, TABLE], I32)
        n_blk = sb("n_blocks", [1, 2], I32)
        off = sb("blk_offset", [P, TABLE])
        posm = sb("pos_masked", [P, TT, N_EXP])
        dv = sb("dest_weight", [P, TT, N_EXP, 2])
        dvs = sb("dest_weight_block", [P, TT, 2])
        dw = sb("slot_row_weight", [P, 2])
        dw_next = sb("next_row_weight", [P, 2])
        slot_row = sb("slot_row", [P, 1], U32)
        tick = sb("tick", [P, 1])
        PR = sb("param_cols", [P, TAPS + NROW])
        SM = sb("small", [P, 320])
        GK = sb("gain_cols", [P, 6])
        BC = sb("row_bcast", [P, 172])

        front = ExitStack()
        HT = sb("hT", [P, KD, T], stack=front)
        OT = sb("oT", [P, KD, T], stack=front)
        XN = sb("xn_tok", [P, D], stack=front)
        GB = sb("gain_rows", [P, D], stack=front)
        UT = sb("uT", [P, GC, T], stack=front)
        ZP = sb("z_padded", [P, GC, T + CONV_W - 1], stack=front)
        CKV = sb("ckv", [P, TT, 320], stack=front)
        KNT = sb("knT", [P, MLA_H, T], stack=front)
        KRT = sb("krT", [P, T], stack=front)
        SQ = sb("sq_tok", [P, TT, GW], stack=front)
        SKV = sb("skv_tok", [P, TT, 256], stack=front)
        SQT = sb("sqT", [P, GC, T], stack=front)
        SKT = sb("skT", [P, SWA_KV, T], stack=front)
        PW = sb("lam_powers", [P, 2, SSM_TILES, SCAN_L], stack=front)
        BL = sb("ssm_b_lhs", [P, 2, 4, P], stack=front)
        CL = sb("ssm_c_lhs", [P, 2, 4, P], stack=front)
        front.close()

        def flat(ap):
            return ap.rearrange("p a b -> p (a b)")

        scr = ring[:, FRONT_RING * PIECE:RING * PIECE]
        XS = scr[:, 0:4096].rearrange("p (c j k l) -> p c j k l", c=2, j=HALF, k=SCAN_L)
        XSt = scr[:, 0:4096].rearrange("p (c j t) -> p c j t", c=2, j=HALF)
        APT = scr[:, 4096:6144]
        L0, L1 = scr[:, 0:2048], scr[:, 7168:9216]
        PT = scr[:, 2048:4096]
        BT = scr[:, 4096:6144].rearrange("p (h j) -> p h j", h=SWA_H)
        CQ = scr[:, 6144:7168].rearrange("p (t n) -> p t n", t=TT)
        QRT = scr[:, 6144:7168].rearrange("p (h t) -> p h t", h=MLA_H)
        CQT = scr[:, 7168:8192].rearrange("p (k t) -> p k t", k=4)
        QNT = CQT
        MQ = scr[:, 8192:9728].rearrange("p (t n) -> p t n", t=TT)
        MKV = scr[:, 9728:11776].rearrange("p (t n) -> p t n", t=TT)
        T1 = scr[:, 11776:12032].rearrange("p (c j k) -> p c j k", c=2, j=HALF)
        T2 = scr[:, 12032:12288].rearrange("p (c j k) -> p c j k", c=2, j=HALF)
        XNO = flat(OT[:, 0:8, :])
        xn_of = [XN[:, :], XNO]
        CKVT = OT[:, 0:2, :]
        KD2 = flat(OT[:, 2:4, :]).rearrange("p (t v n) -> p t v n", t=TT, v=SWA_KV)
        ZG = OT[:, 8:12, :]
        BDm = flat(OT[:, 0:4, :]).rearrange("p (c n) -> p c n", c=2)
        CMm = flat(OT[:, 4:8, :]).rearrange("p (c n) -> p c n", c=2)
        b_raw = flat(OT[:, 12:14, :]).rearrange("p (c n) -> p c n", c=2)
        c_raw = flat(OT[:, 14:16, :]).rearrange("p (c n) -> p c n", c=2)
        SR = flat(SQT[:, :, :]).rearrange("p (r n) -> p r n", r=8)[0:SSM_TILES]
        VR = flat(SQ[:, :, :])
        DSB = flat(SKV[:, :, :])[0:SWA_H, 0:BIAS_W]
        SQG = CL[:, :, :, :].rearrange("p a b c -> p (a b c)").rearrange("p (k t) -> p k t", k=GC)
        RG = PW[:, :, :, :].rearrange("p a b c -> p (a b c)").rearrange("p (r t) -> p r t", r=2)
        SQ2 = KNT
        RG2 = BL[:, :, :, :].rearrange("p a b c -> p (a b c)").rearrange("p (r t) -> p r t", r=4)
        ZT = ZP[:, :, 0:T]
        VX = GB[:, 0:1024].rearrange("p (m n) -> p m n", m=2)
        KX = GB[:, 1024:2048].rearrange("p (m n) -> p m n", m=2)
        KXT = UT
        GB2 = scr[:, 2048:4096]
        QX = scr[:, 4096:5120].rearrange("p (t n) -> p t n", t=TT)
        QXT = scr[:, 5120:6144].rearrange("p (k t) -> p k t", k=4)
        XL = scr[:, 6144:8192].rearrange("p (n h w) -> p n h w", n=TT, h=XA_H)
        XPT = scr[:, 8192:10240].rearrange("p (n i q) -> p n i q", n=TT, i=8)
        XOT = scr[:, 10240:11264].rearrange("p (k t) -> p k t", k=4)
        WR = flat(OT[:, 12:16, :])[:, 0:KD * 36].rearrange("p (k n) -> p k n", k=KD)
        RT = flat(OT[:, 8:12, :])
        RB = XN

        WH = sb("w_hi", [P, HI_RING, PIECE], F32R)
        WL = sb("w_lo", [P, LO_RING, PIECE], F32R)
        XG = sb("x_gathered", [P, KD, S2], F32R)
        HH = sb("h_hi", [P, TT, D], F32R)
        HL = sb("h_lo", [P, TT, D], F32R)
        HID = sb("hidden", [P, 4, S2], F32R)
        SEL = sb("select", [P, TT, S2], F32R)
        GU = X[0:S2, 0, 0:1024]
        TH = X[:, 0, 1024:1024 + 4 * SLOTS]
        H2 = X[:, 0, 1280:1280 + 4 * SLOTS]
        YS = X[0:S2, 1, :]

        tb = bank[TASK_NO["tab"] % 8]
        others = [b for i, b in enumerate(bank) if i != TASK_NO["tab"] % 8]
        gu, rest, yb, db = others[0:2], others[2:4], others[4:6], others[6]

        def wait_task(eng, name):
            eng.wait_ge(s["psum_drained"], TASK_NO[name] + 1)

        def wait_filled(eng, name):
            eng.wait_ge(s["psum_filled"], TASK_NO[name] + 1)

        class Steps:

            def __init__(self, eng, order):
                self.eng, self.order, self.count = eng, order, {}

            def sent(self, ins, sem=None):
                sem = sem or self.order
                self.count[sem] = self.count.get(sem, 0) + 1
                ins.then_inc(s[sem], 1)
                return sem, self.count[sem]

            def link(self, ins, sem=None):
                sem, n = self.sent(ins, sem)
                self.eng.wait_ge(s[sem], n)

        def col(name, c=0):
            return PR[:, TAPS + ROW[name] + c:TAPS + ROW[name] + c + 1]

        in_w = inp["w_in"][0].rearrange("(p k) n -> p k n", k=KD)

        def piece_source(key):
            g, q = key
            if g in IN_COLS:
                a, n = IN_COLS[g]
                return in_w[:, 4 * q:4 * q + 4, a:a + n], 4, n
            if g in ("xv", "xk", "xq"):
                w = inp[{"xv": "xa_wv", "xk": "xa_wk", "xq": "xa_wq"}[g]][0]
                return w.rearrange("(p k) n -> p k n", k=KD)[:, 4 * q:4 * q + 4, :], 4, 512
            if g in ("glu", "pw"):
                w = inp[{"glu": "ssm_glu_w", "pw": "conv_pw_w"}[g]][0]
                return w.rearrange("(k p) n -> p k n", p=P), 4, 512
            if g == "wqb":
                w = inp["mla_wq_b"][0].rearrange("(p k) n -> p k n", k=4)
                return w[:, :, 384 * q:384 * q + 384], 4, 384
            if g == "wkvb":
                return inp["mla_wkv_b"][0].rearrange("(p k) n -> p k n", k=2), 2, 1024
            if g == "co":
                w = inp["xa_wo"][0].rearrange("(k p) n -> p k n", p=P)
                return w[:, :, 512 * q:512 * q + 512], 4, 512
            n = int(g[2:])
            w = inp["w_out"][0].rearrange("(k p) n -> p k n", p=P)
            return w[:, 4 * q:4 * q + 4, 512 * n:512 * n + 512], 4, 512

        def piece_view(key):
            _, k, n = piece_source(key)
            a = (PIECE_NO[key] % FRONT_RING) * PIECE
            return ring[:, a:a + k * n].rearrange("p (k n) -> p k n", k=k)

        def moe_source(e, q):
            if q < 8:
                w = inp["moe_w_gate" if q < 4 else "moe_w_up"][0].rearrange("e (p k) n -> p e k n", k=KD)
                return w[:, e, 4 * (q % 4):4 * (q % 4) + 4, :]
            w = inp["moe_w_down"][0].rearrange("e (p k) n -> p e k n", k=4)
            return w[:, e, :, 512 * (q - 8):512 * (q - 8) + 512]

        def moe_slot(q):
            a = MOE_SLOT[q] * PIECE
            return ring[:, a:a + PIECE]

        front_uses = [len([n for n in range(NP) if n % FRONT_RING == i]) if i < FRONT_RING else 0
                      for i in range(RING)]

        block = ctx.enter_context(nc.Block())

        @block.sync
        def _(sp):
            def sp_load(dst, src, sem):
                sp.dma_start(dst, src).then_inc(s[sem], 16)

            sp.dma_start(X[:, 0, :], inp["x"][0, 0:P, :]).then_inc(s["x_in0"], 16)
            sp.dma_start(GB[:, :], inp["ln_mix_g"].to_broadcast([P, D])).then_inc(s["gain_in"], 16)
            sp.dma_start(X[:, 1, :], inp["x"][0, P:T, :]).then_inc(s["x_in1"], 16)
            for i, key in enumerate(PIECES):
                if i >= FRONT_RING:
                    wait_filled(sp, LAST_USE[PIECES[i - FRONT_RING][0]])
                src, _, _ = piece_source(key)
                sp.dma_start(piece_view(key), src).then_inc(slot_in[i % FRONT_RING], 16)
                if key == ("u", 3):
                    for r, name in enumerate(("ssm_a_re", "ssm_a_im")):
                        sp_load(SR[:, r, :], inp[name][0].rearrange("(j g) n -> j (g n)", g=2), "ssm_in")
                    sp_load(SM[0:SSM_TILES, 0:2], inp["ssm_log_dt"][0].rearrange("(j g) -> j g", g=2), "ssm_in")
                    for c, name in enumerate(("ssm_b_re", "ssm_b_im")):
                        sp_load(b_raw[:, c, :].rearrange("p (j i) -> p j i", i=16),
                             inp[name][0].rearrange("(j g) n i -> (g n) j i", g=2), "ssm_in")
                    for c, name in enumerate(("ssm_c_re", "ssm_c_im")):
                        sp_load(c_raw[:, c, 0:256].rearrange("p (j n) -> p j n", j=4),
                             inp[name][0].rearrange("(j g) o n -> (g o) j n", g=8), "ssm_in")
                    sp.wait_ge(s["xn"], 2)
                    wait_filled(sp, "xT03")
                    sp.dma_start(XN[:, :], inp["mem"][0, 0:P, :]).then_inc(s["mem_in"], 16)
                    sp.dma_start(GB[:, :], inp["mem_ln_g"].to_broadcast([P, D])).then_inc(s["mem_gain_in"], 16)
                if key == ("xv", 0):
                    wait_filled(sp, "mT03")
                    sp.dma_start(XN[:, :], inp["mem"][0, P:T, :]).then_inc(s["mem1_in"], 16)
                    sp.wait_ge(s["dist_out"], 16)
                    sp.wait_ge(s["sq_n"], 2)
                    for b in range(2):
                        band = bass.AP(dist_d.tensor, BIAS_W * b, [[1, P], [2 * BIAS_W, 4], [1, 2 * P]])
                        sp.dma_start(BT[:, 4 * b:4 * b + 4, :], band).then_inc(s["band_in"], 16)
                if key == ("wo1", WO_ORDER[1]):
                    wait_filled(sp, "so1")
                    sp.dma_start(GB2, inp["ln_cross_g"].to_broadcast([P, D])).then_inc(s["cross_gain_in"], 16)
                if key == ("xq", 1):
                    wait_filled(sp, "wo31")
                    sp.dma_start(WR[:, :, 0:4], inp["moe_w_group"][0].rearrange("(p k) n -> p k n", k=KD)).then_inc(
                        s["router_in"], 16)
                    sp.dma_start(WR[:, :, 4:36], inp["moe_w_expert"][0].rearrange("(p k) n -> p k n", k=KD)).then_inc(
                        s["router_in"], 16)
            wait_filled(sp, "xo1")
            sp.dma_start(GB[:, :], inp["ln_moe_g"].to_broadcast([P, D])).then_inc(s["moe_gain_in"], 16)
            wait_filled(sp, "co31")
            for q in range(PPE):
                sp.dma_start(moe_slot(q).rearrange("p (k n) -> p k n", k=4), moe_source(0, q)).then_inc(
                    slot_in[MOE_SLOT[q]], 16)
                if q == 7:
                    wait_task(sp, "co31")
                    for tt in range(TT):
                        sp.dma_start(x2_d[P * tt:P * tt + P, :], X[:, tt, :]).then_inc(s["x2_out"], 16)
            sp.wait_ge(s["tables"], 1)
            n_reg = sp.value_load(n_blk[0:1, 0:1], min_val=2, max_val=MAX_BLOCKS)

            def load_pieces(block_no, j, qs):
                e = sp.value_load(blk_e[0:1, bass.ds(block_no, 1)], min_val=0, max_val=N_EXP - 1)
                for q in qs:
                    sp.wait_ge(s["lo_ready"], PPE * j + q + 1)
                    sp.dma_start(moe_slot(q).rearrange("p (e k n) -> p e k n", e=1, k=4),
                                 moe_source(bass.ds(e, 1), q)).then_inc(slot_in[MOE_SLOT[q]], 16)

            load_pieces(1, 1, range(8))
            with sp.Fori(2, n_reg) as j:
                load_pieces(j, j, range(8))
                load_pieces(j - 1, j, range(8, PPE))
            load_pieces(n_reg - 1, n_reg, range(8, PPE))
            sp.wait_ge(s["ring_free"], 1)
            sp.wait_ge(s["x2_out"], 32)
            for i in range(4):
                tt, half = i // 2, i % 2
                sp.dma_start(ring[:, 16384 + 1024 * i:16384 + 1024 * i + 1024],
                             x2_d[P * tt:P * tt + P, 1024 * half:1024 * half + 1024]).then_inc(rows_back[i], 16)
            sp.wait_ge(s["all_scattered"], 1)
            for i in range(4):
                tt, half = i // 2, i % 2
                src = rows_d.rearrange("(t p r) d -> t p r d", t=TT, r=4)[tt][:, :, 1024 * half:1024 * half + 1024]
                sp.dma_start(ring[:, 4096 * i:4096 * i + 4096].rearrange("p (r d) -> p r d", r=4), src).then_inc(
                    rows_back[i], 16)
            for i in range(4):
                tt, half = i // 2, i % 2
                sp.wait_ge(s["summed"], i + 1)
                sp.dma_start(out[0, P * tt:P * tt + P, 1024 * half:1024 * half + 1024],
                             ring[:, 16384 + 1024 * i:16384 + 1024 * i + 1024]).then_inc(s["stored"], 16)
            sp.wait_ge(s["stored"], 64)

        @block.gpsimd
        def _(pool):
            st = Steps(pool, "pool_order")

            def load(dst, src, sem):
                pool.dma_start(dst, src).then_inc(s[sem], 16)

            load(VR[0:TAPS, 0:P], inp["conv_dw_w"][0].rearrange("w (k p) -> (w k) p", p=P), "params_in")
            for name, n in ROW_SIZE[:11]:
                load(VR[ROW[name]:ROW[name] + n, P:2 * P], inp[name][0].rearrange("(k p) -> k p", p=P), "params_in")
            for name in ("swa_qn_g", "swa_kn_g"):
                for i in range(2):
                    load(VR[ROW[name]:ROW[name] + 1, P + 64 * i:P + 64 * i + 64], inp[name], "params_in")
            load(VR[0:N_BUCKET, 256:264], inp["rel_bias"], "bias_in")
            load(VR[0:N_BUCKET + 1, 264:264 + BIAS_W], bucket_d, "bias_in")
            o = 0
            for name, n in (("swa_sinks", 8), ("mla_qn_rope_g", 64), ("mla_kn_rope_g", 64), ("moe_b_group", 4),
                            ("moe_b_expert", 32)):
                load(BC[:, o:o + n], inp[name].to_broadcast([P, n]), "rows_in")
                o += n
            load(GK[:, 0:4], inp["mla_qa_g"][0].rearrange("(p k) -> p k", k=4), "rows_in")
            load(GK[:, 4:6], inp["mla_kva_g"][0].rearrange("(p k) -> p k", k=2), "rows_in")
            wait_task(pool, "zg1")
            pool.wait_ge(s["zeroed"], 2)
            za = ZP[:, :, CONV_W - 1:]
            st.link(nc.gpsimd.tensor_scalar(ZG, ZG, 0.5, 0.5, ALU.mult, ALU.add))
            st.link(nc.gpsimd.tensor_tensor(za, za, ZG, ALU.mult))
            acc, product = OT[:, 4:8, :], ZG
            for w in range(CONV_W):
                tap = PR[:, GC * w:GC * w + GC].unsqueeze(2).to_broadcast([P, GC, T])
                st.link(nc.gpsimd.tensor_tensor(product if w else acc, ZP[:, :, w:w + T], tap, ALU.mult))
                if w:
                    st.link(nc.gpsimd.tensor_tensor(acc, acc, product, ALU.add))
            bias = PR[:, TAPS + ROW["conv_dw_b"]:TAPS + ROW["conv_dw_b"] + GC].unsqueeze(2).to_broadcast([P, GC, T])
            st.link(nc.gpsimd.tensor_tensor(acc, acc, bias, ALU.add), "conv_done")
            pool.wait_ge(s["tables"], 1)
            n_reg = pool.value_load(n_blk[0:1, 0:1], min_val=2, max_val=MAX_BLOCKS)
            pool.sem_inc(s["y_free"], 1)
            with pool.Fori(0, n_reg) as j:
                pool.wait_ge(s["dest_idx"], j + 1)
                pool.wait_ge(s["y_sb"], 4 * j + 9)
                pool.sem_inc(s["scatter_begun"], 1)
                pool.indirect_dma_start(rows_d, bass.IndirectOffsetOnAxis(ap=slot_row[0:S2, :], axis=0), YS, None,
                                        bounds_check=ROWS - 1, oob_is_err=False).then_inc(s["scattered"], 16)
                pool.wait_ge(s["scattered"], 16 * j + 16)
                pool.sem_inc(s["y_free"], 1)
            pool.sem_inc(s["all_scattered"], 1)
            for i in range(4):
                pool.wait_ge(rows_back[i], 32)
                r = ring[:, 4096 * i:4096 * i + 4096].rearrange("p (r d) -> p r d", r=4)
                nc.gpsimd.tensor_tensor(r[:, 0, :], r[:, 0, :], r[:, 1, :], ALU.add).then_inc(s["pair_sum"], 1)

        @block.tensor
        def _(pe):
            task = [0]

            def fill(name, cols=512, parts=P):
                assert TASKS[task[0]] == name, (name, TASKS[task[0]])
                if task[0] >= 8:
                    pe.wait_ge(s["psum_drained"], task[0] - 7)
                task[0] += 1
                return bank[(task[0] - 1) % 8][0:parts, 0:cols]

            def filled(mm):
                mm.then_inc(s["psum_filled"], 1)

            def arrived(key):
                i = PIECE_NO[key]
                pe.wait_ge(slot_in[i % FRONT_RING], 16 * (i // FRONT_RING + 1))


            def transposes(name, ins, parts=P, cols=P):
                b = fill(name, cols=len(ins) * cols, parts=parts)
                for i, a in enumerate(ins):
                    mm = pe.transpose(b[:, cols * i:cols * i + cols], a, ident[0:a.shape[0], 0:a.shape[0]])
                filled(mm)

            def model_transposes(prefix, tt, src):
                v = src.rearrange("p (f k) -> p k f", k=KD)
                for q in range(4):
                    transposes(f"{prefix}{tt}{q}", [v[:, 4 * q + i, :] for i in range(4)])

            def token_major(name, pieces, lhs, tt, n, cols, at=0):
                b = fill(name, cols=cols)
                chunks = [(key, c) for key in pieces for c in range(piece_source(key)[1])]
                for i, (key, c) in enumerate(chunks):
                    if c == 0:
                        arrived(key)
                    mm = pe.matmul(b, lhs(i)[:, P * tt:P * tt + P], piece_view(key)[:, c, at:at + cols],
                                   start=i == 0, stop=i == n - 1)
                filled(mm)
                return mm

            def feature_major(name, pieces, rhs, first, n):
                b = fill(name)
                chunks = [(key, c) for key in pieces for c in range(4)]
                for f in range(2):
                    a = P * (first + f)
                    for i, (key, c) in enumerate(chunks):
                        if c == 0:
                            arrived(key)
                        mm = pe.matmul(b[:, T * f:T * f + T], piece_view(key)[:, c, a:a + P], rhs(i),
                                       start=i == 0, stop=i == n - 1)
                filled(mm)

            def hT(i):
                return HT[:, i, :]

            def b_products(js):
                for j in js:
                    q, jj = j % 4, j // 4
                    b = fill(f"bu{j}")
                    for c in range(2):
                        mm = pe.matmul(b[:, T * c:T * c + T], BL[32 * q:32 * q + 32, c, jj, :],
                                       UT[32 * q:32 * q + 32, jj, :], start=True, stop=True)
                    filled(mm)

            def c_products(half):
                b = fill(f"y{half}")
                for f in range(2):
                    for q in range(4):
                        for c in range(2):
                            mm = pe.matmul(b[32 * q:32 * q + 32, T * f:T * f + T],
                                           CL[:, c, 2 * half + f, 32 * q:32 * q + 32], XSt[:, c, 4 * f + q, :],
                                           start=c == 0, stop=c == 1)
                filled(mm)

            pe.wait_ge(s["const_in"], 16)
            for tt in range(TT):
                pe.wait_ge(s["xn"], tt + 1)
                model_transposes("xT", tt, xn_of[tt])
            wait_task(pe, "xT13")
            u = [("u", q) for q in range(4)]
            feature_major("u0", u, hT, 0, KD)
            feature_major("u1", u, hT, 2, KD)
            pe.wait_ge(s["ssm_lam"], 1)
            transposes("ssmP", [SR[:, r, :] for r in (5, 6, 2, 7)], cols=SSM_TILES)
            pe.wait_ge(s["params_in"], 16 * 16)
            b = fill("params", cols=TAPS + NROW)
            pe.transpose(b[:, 0:TAPS], VR[0:TAPS, 0:P], ident[0:TAPS, 0:TAPS])
            filled(pe.transpose(b[:, TAPS:TAPS + NROW], VR[0:NROW, P:2 * P], ident[0:NROW, 0:NROW]))
            pe.wait_ge(s["bias_in"], 32)
            pe.wait_ge(s["zeroed"], 1)
            filled(pe.matmul(fill("bias", cols=BIAS_W, parts=SWA_H), VR[0:N_BUCKET + 1, 256:264],
                             VR[0:N_BUCKET + 1, 264:264 + BIAS_W], start=True, stop=True))
            za, zg = [("za", q) for q in range(4)], [("zg", q) for q in range(4)]
            feature_major("za0", za, hT, 0, KD)
            for c in range(2):
                pe.wait_ge(s["ssm_b"], 1)
                transposes(f"ssmB{c}", [BDm[:, c, P * i:P * i + P] for i in range(4)])
            for c in range(2):
                pe.wait_ge(s["ssm_c"], 1)
                transposes(f"ssmC{c}", [CMm[:, c, P * i:P * i + P] for i in range(4)])
            wait_task(pe, "ssmC1")
            b_products(range(HALF))
            feature_major("za1", za, hT, 2, KD)
            feature_major("zg0", zg, hT, 0, KD)
            feature_major("zg1", zg, hT, 2, KD)

            def projection(g, cols, tts=range(TT)):
                for tt in tts:
                    token_major(f"{g}{tt}", [(g, q) for q in range(4)], hT, tt, KD, cols)

            projection("cq", 512, (0,))
            pe.wait_ge(s["scan_done"], 1)
            c_products(0)
            b_products(range(HALF, SSM_TILES))
            projection("cq", 512, (1,))
            projection("ckv", 320)
            projection("sq", 512)
            projection("skv", 256)
            pe.wait_ge(s["scan_done"], 2)
            c_products(1)
            pe.wait_ge(s["mem_n"], 1)
            model_transposes("mT", 0, XN)
            pe.wait_ge(s["cq_n"], 1)
            for tt in range(TT):
                v = CQ[:, tt, :].rearrange("p (f k) -> p k f", k=4)
                transposes(f"cqT{tt}", [v[:, k, :] for k in range(4)])
            pe.wait_ge(s["ckv_n"], 1)
            transposes("ckvT", [CKV[:, tt, 0:256].rearrange("p (f k) -> p k f", k=2)[:, k, :]
                                for k in range(2) for tt in range(TT)])
            wait_task(pe, "cqT1")
            for tt in range(TT):
                for g in range(2):
                    b = fill(f"mq{tt}{g}", cols=384)
                    arrived(("wqb", g))
                    for k in range(4):
                        mm = pe.matmul(b, CQT[:, k, P * tt:P * tt + P], piece_view(("wqb", g))[:, k, :],
                                       start=k == 0, stop=k == 3)
                    filled(mm)
            wait_task(pe, "ckvT")
            for tt in range(TT):
                for g in range(2):
                    b = fill(f"mkv{tt}{g}")
                    arrived(("wkvb", 0))
                    for k in range(2):
                        mm = pe.matmul(b, CKVT[:, k, P * tt:P * tt + P],
                                       piece_view(("wkvb", 0))[:, k, 512 * g:512 * g + 512],
                                       start=k == 0, stop=k == 1)
                    filled(mm)
            pe.wait_ge(s["sq_n"], 2)
            for tt in range(TT):
                transposes(f"sqT{tt}", [SQ[:, tt, P * k:P * k + P] for k in range(GC)])
            transposes("skT", [KD2[:, tt, v, :] for tt in range(TT) for v in range(SWA_KV)])
            pe.wait_ge(s["mem_n"], 2)
            model_transposes("mT", 1, XN)
            wait_task(pe, "mT13")

            def memory(g, tt):
                token_major(f"{g}{tt}", [(g, q) for q in range(4)], hT, tt, KD, 512)

            memory("xv", 0)
            pe.wait_ge(s["mq_n"], 1)
            for tt in range(TT):
                transposes(f"qnT{tt}", [MQ[:, tt, QK_D * h:QK_D * h + NOPE] for h in range(MLA_H)])
            for tt in range(TT):
                transposes(f"qrT{tt}", [MQ[:, tt, QK_D * h + NOPE:QK_D * h + QK_D] for h in range(MLA_H)], parts=64)
            pe.wait_ge(s["mkv_n"], 1)
            for tt in range(TT):
                transposes(f"knT{tt}", [MKV[:, tt, 256 * h:256 * h + NOPE] for h in range(MLA_H)])
            transposes("krT", [CKV[:, tt, 256:320] for tt in range(TT)], parts=64)
            wait_task(pe, "krT")

            def latent_scores(name, n, heads):
                w = P * (n + 1)
                b = fill(name, cols=len(heads) * w)
                for i, h in enumerate(heads):
                    q = slice(P * n, P * n + P)
                    o = b[:, w * i:w * i + w]
                    pe.matmul(o, QNT[:, h, q], KNT[:, h, 0:w], start=True, stop=False)
                    mm = pe.matmul(o, QRT[0:64, h, q], KRT[0:64, 0:w], start=False, stop=True)
                filled(mm)

            latent_scores("ml0", 0, range(4))
            latent_scores("ml10", 1, (0, 1))
            latent_scores("ml11", 1, (2, 3))

            def latent_output(n):
                b = fill(f"mo{n}")
                for h in range(MLA_H):
                    for kb in range(n + 1):
                        mm = pe.matmul(b[:, P * h:P * h + P], MKV[:, kb, 256 * h + NOPE:256 * h + 256],
                                       PT[:, 512 * n + P * (h * (n + 1) + kb):512 * n + P * (h * (n + 1) + kb) + P],
                                       start=kb == 0, stop=kb == n)
                filled(mm)

            def window_scores(name, n, places):
                w = P * (n + 1)
                b = fill(name, cols=len(places) * w)
                pe.matmul(b.rearrange("p (h w) -> p h w", w=w), const("flip"),
                          BT[:, places[0]:places[0] + len(places), P * (1 - n):], start=True, stop=False)
                for i, at in enumerate(places):
                    h = HEAD_AT[at]
                    r = slice(64 * (h % 2), 64 * (h % 2) + 64)
                    mm = pe.matmul(b[:, w * i:w * i + w], SQT[r, h // 2, P * n:P * n + P], SKT[r, h // 4, 0:w],
                                   start=False, stop=i == len(places) - 1)
                filled(mm)

            def window_output(n):
                b = fill(f"so{n}")
                for at in range(SWA_H):
                    h = HEAD_AT[at]
                    o = b[64 * (h % 2):64 * (h % 2) + 64, P * (h // 2):P * (h // 2) + P]
                    for kb in range(n + 1):
                        a = P * (at * (n + 1) + kb)
                        mm = pe.matmul(o, SKV[:, kb, P + 64 * (h // 4):P + 64 * (h // 4) + 64], PT[:, a:a + P],
                                       start=kb == 0, stop=kb == n)
                filled(mm)

            def column_sums(name, src):
                b = fill(name, cols=T)
                for k in range(GC):
                    mm = pe.matmul(b, const("ones"), src[:, k, :], start=k == 0, stop=k == GC - 1)
                filled(mm)

            wait_task(pe, "skT")
            pe.wait_ge(s["band_in"], 32)
            window_scores("sl00", 0, range(4))
            window_scores("sl01", 0, range(4, 8))
            memory("xv", 1)
            pe.wait_ge(s["ml_p"], 1)
            transposes("mp0", [L0[:, P * h:P * h + P] for h in range(4)])
            wait_task(pe, "mp0")
            latent_output(0)
            pe.wait_ge(s["ml_p"], 2)
            for i in range(2):
                transposes(f"mp1{i}", [L0[:, 512 * (i + 1) + P * k:512 * (i + 1) + P * k + P] for k in range(4)])
            wait_task(pe, "mp11")
            latent_output(1)
            pe.wait_ge(s["gelu"], 1)
            for i in range(2):
                feature_major(f"glu{i}", [("glu", 0)], lambda k: OT[:, 12 + k, :], 2 * i, GC)
            pe.wait_ge(s["conv_done"], 1)
            column_sums("cm", OT[:, 4:8, :])
            for i in range(4):
                window_scores(f"sl1{i}", 1, (2 * i, 2 * i + 1))
            memory("xk", 0)
            pe.wait_ge(s["conv_sq"], 1)
            column_sums("cv", SQG)
            pe.wait_ge(s["og_sq"], 1)
            column_sums("gs2", SQ2)
            pe.wait_ge(s["sl_p"], 1)
            for i in range(2):
                transposes(f"sp0{i}", [L1[:, 512 * i + P * k:512 * i + P * k + P] for k in range(4)])
            wait_task(pe, "sp01")
            window_output(0)
            memory("xk", 1)
            pe.wait_ge(s["og_sq"], 2)
            column_sums("gs3", SQ2)
            pe.wait_ge(s["conv_z"], 1)
            for i in range(2):
                feature_major(f"pw{i}", [("pw", 0)], lambda k: ZT[:, k, :], 2 * i, GC)
            pe.wait_ge(s["sl_p"], 2)
            for i in range(4):
                transposes(f"sp1{i}", [L0[:, 512 * i + P * k:512 * i + P * k + P] for k in range(4)])
            wait_task(pe, "sp13")
            window_output(1)
            pe.wait_ge(s["kx_n"], 1)
            for tt in range(TT):
                transposes(f"kxT{tt}", [KX[:, tt, P * h:P * h + P] for h in range(XA_H)])
            pe.wait_ge(s["og_sq"], 3)
            column_sums("gs1", SQG)
            pe.wait_ge(s["og_sq"], 4)
            column_sums("gs0", SQ2)
            for n in range(4):
                for tt in range(TT):
                    b = fill(f"wo{n}{tt}")
                    for q in WO_ORDER:
                        arrived((f"wo{n}", q))
                        if n == 0 and tt == 0:
                            pe.wait_ge(s["og_n"], WO_ORDER.index(q) + 1)
                        for c in range(4):
                            pe.matmul(b, OT[:, 4 * q + c, P * tt:P * tt + P], piece_view((f"wo{n}", q))[:, c, :],
                                      start=q == WO_ORDER[0] and c == 0, stop=False)
                    filled(pe.matmul(b, ident, X[:, tt, 512 * n:512 * n + 512], start=False, stop=True))
            for tt in range(TT):
                pe.wait_ge(s["c_n"], tt + 1)
                model_transposes("cT", tt, xn_of[tt])
                wait_task(pe, f"cT{tt}3")
                token_major(f"xq{tt}", [("xq", q) for q in range(4)], hT, tt, KD, 512)
            for n in range(TT):
                pe.wait_ge(s["qx_n"], n + 1)
                transposes(f"qxT{n}", [QX[:, n, P * h:P * h + P] for h in range(XA_H)])
                wait_task(pe, f"qxT{n}")
                for i in range(2):
                    b = fill(f"xl{n}{i}")
                    for h in (2 * i, 2 * i + 1):
                        mm = pe.matmul(b[:, T * (h % 2):T * (h % 2) + T], QXT[:, h, P * n:P * n + P], KXT[:, h, :],
                                       start=True, stop=True)
                    filled(mm)
            for n in range(TT):
                pe.wait_ge(s["xl_p"], n + 1)
                for i in range(2):
                    transposes(f"xp{n}{i}", [XL[:, n, 2 * i + h, P * kb:P * kb + P] for h in range(2) for kb in range(2)])
                wait_task(pe, f"xp{n}1")
                b = fill(f"xo{n}")
                for h in range(XA_H):
                    for kb in range(2):
                        mm = pe.matmul(b[:, P * h:P * h + P], VX[:, kb, P * h:P * h + P], XPT[:, n, 2 * h + kb, :],
                                       start=kb == 0, stop=kb == 1)
                filled(mm)
                wait_task(pe, f"xo{n}")
                for c in range(4):
                    arrived(("co", c))
                    b = fill(f"co{c}{n}")
                    for k in range(XA_H):
                        pe.matmul(b, XOT[:, k, P * n:P * n + P], piece_view(("co", c))[:, k, :],
                                  start=k == 0, stop=False)
                    filled(pe.matmul(b, ident, X[:, n, 512 * c:512 * c + 512], start=False, stop=True))
            for tt in range(TT):
                pe.wait_ge(s["m_n"], tt + 1)
                model_transposes("hT", tt, xn_of[tt])
                wait_task(pe, f"hT{tt}3")
                pe.wait_ge(s["router_in"], 32)
                b = fill(f"rl{tt}", cols=36)
                for k in range(KD):
                    mm = pe.matmul(b, HT[:, k, P * tt:P * tt + P], WR[:, k, :], start=k == 0, stop=k == KD - 1)
                filled(mm)
            pe.wait_ge(s["choice"], 1)
            b = fill("pos", cols=96)
            chosen = RT[:, 0:64].rearrange("p (t e) -> p t e", t=TT)
            pe.matmul(b[:, 0:32], const("ltri"), chosen[:, 0, :], start=True, stop=True)
            pe.matmul(b[:, 32:64], const("ones"), chosen[:, 0, :], start=True, stop=False)
            pe.matmul(b[:, 32:64], const("ltri"), chosen[:, 1, :], start=False, stop=True)
            pe.matmul(b[:, 64:96], const("ones"), chosen[:, 0, :], start=True, stop=False)
            filled(pe.matmul(b[:, 64:96], const("ones"), chosen[:, 1, :], start=False, stop=True))
            wait_task(pe, "pos")
            pe.sem_inc(s["split_free"], HI_RING)


            def gather(b, k0):
                for k in range(k0, k0 + 8):
                    for part, h in ((0, HH), (1, HL)):
                        a = S2 * (k - k0) + SLOTS * part
                        v = h[:, :, :].rearrange("p t (f k) -> p t k f", k=KD)
                        for tt in range(TT):
                            mm = pe.matmul(b[:, a:a + SLOTS], v[:, tt, k, :], SEL[:, tt, 0:SLOTS],
                                           start=tt == 0, stop=tt == TT - 1)
                mm.then_inc(s["gathered"], 1)

            def gate_up(j):
                pe.wait_ge(s["xg_ready"], 2 * j + 2)
                for q in range(8):
                    pe.wait_ge(s["lo_ready"], PPE * j + PPE + q + 1)
                    for c in range(4):
                        for part, w in ((0, WH[:, q % HI_RING, :]), (1, WL[:, q % LO_RING, :])):
                            mm = pe.matmul(gu[q // 4][0:S2, :], XG[:, 4 * (q % 4) + c, :], w[:, FF * c:FF * c + FF],
                                           start=q % 4 == 0 and c == 0 and part == 0,
                                           stop=q % 4 == 3 and c == 3 and part == 1)
                    if q < 7:
                        mm.then_inc(s["split_free"], 1)
                return mm

            def down(j, first, at, parts):
                pe.wait_ge(s["hid"], j)
                for n in parts:
                    pe.wait_ge(s["lo_ready"], PPE * j + PPE + first + n + 1)
                    pe.wait_ge(s["y_sb"], 4 * j + n)
                    for c in range(4):
                        for part, w in ((0, WH[:, (at + n) % HI_RING, :]), (1, WL[:, (at + n) % LO_RING, :])):
                            mm = pe.matmul(yb[n % 2][0:S2, :], HID[:, c, :], w[:, 512 * c:512 * c + 512],
                                           start=c == 0 and part == 0, stop=c == 3 and part == 1)
                    mm.then_inc(s["split_free"], 1)

            def transpose_hidden(j):
                pe.wait_ge(s["gu_sb"], 2 * j + 2)
                for g in range(2):
                    v = GU[:, FF * g:FF * g + FF].rearrange("p (f k) -> p k f", k=4)
                    for k in range(4):
                        mm = pe.matmul(tb[:, 256 * g + SLOTS * k:256 * g + SLOTS * k + SLOTS], v[:, k, :],
                                       const("stack")[0:S2], start=True, stop=True)
                mm.then_inc(s["t_done"], 1)

            def destinations():
                for tt in range(TT):
                    mm = pe.matmul(db[0:S2, 0:2], SEL[:, tt, :].bitcast(F32), dvs[:, tt, :], start=tt == 0, stop=tt == 1)
                mm.then_inc(s["dest_done"], 1)

            pe.wait_ge(s["split_h"], 4)
            pe.wait_ge(s["sel"], 1)
            for i in range(2):
                gather(rest[i], 8 * i)
                if i == 0:
                    pe.wait_ge(s["columns"], 1)
                    filled(pe.matmul(fill("tab", cols=2 * TABLE), const("ones"), RT[:, 360:360 + 2 * TABLE],
                                     start=True, stop=True))
            destinations()
            gate_up(0).then_inc(s["split_free"], 5)
            pe.wait_ge(s["sel"], 2)
            gather(rest[0], 0)
            transpose_hidden(0)
            gather(rest[1], 8)
            pe.wait_ge(s["d_bank"], 1)
            destinations()
            n_reg = pe.value_load(n_blk[0:1, 0:1], min_val=2, max_val=MAX_BLOCKS)
            with pe.Fori(1, n_reg) as j:
                gate_up(j).then_inc(s["split_free"], 1)
                down(j, 8, 8, (0, 1))
                pe.wait_ge(s["sel"], j + 2)
                gather(rest[0], 0)
                down(j, 8, 8, (2, 3))
                transpose_hidden(j)
                gather(rest[1], 8)
                pe.wait_ge(s["d_bank"], j + 1)
                destinations()
            down(n_reg, 0, 0, range(4))


        @block.scalar
        def _(act):
            st = Steps(act, "act_order")
            task = [0]

            act.dma_start(K[:, :], const_d).then_inc(s["const_in"], 16)

            def drain(name, dst, view=None, cols=512, parts=P, func=ACT.Copy, scale=1.0, bias=None):
                assert TASKS[task[0]] == name, (name, TASKS[task[0]])
                act.wait_ge(s["psum_filled"], task[0] + 1)
                src = bank[task[0] % 8][0:parts, 0:cols]
                src = src if view is None else view(src)
                task[0] += 1
                if bias is None:
                    ins = nc.scalar.activation(dst, src, func, scale=scale)
                else:
                    ins = nc.scalar.activation(dst, src, func, bias=bias, scale=scale)
                ins.then_inc(s["psum_drained"], 1)

            def drain_parts(name, parts):
                assert TASKS[task[0]] == name, (name, TASKS[task[0]])
                act.wait_ge(s["psum_filled"], task[0] + 1)
                b = bank[task[0] % 8]
                task[0] += 1
                for i, (dst, src, kw) in enumerate(parts):
                    ins = nc.scalar.activation(dst, src(b), **kw)
                    if i < len(parts) - 1:
                        st.link(ins)
                    else:
                        ins.then_inc(s["psum_drained"], 1)

            def four(n):
                return lambda b: b.rearrange("p (k t) -> p k t", k=n)

            def mean_square(src, junk, at, sem):
                st.link(nc.scalar.activation(junk, src, ACT.Square, scale=float(D) ** -0.5,
                                             accum_out=SM[:, at:at + 1]), sem)

            def memory_square(i):
                for h in range(2):
                    st.link(nc.scalar.activation(flat(KNT[:, :, :]), XN[:, 1024 * h:1024 * h + 1024], ACT.Square,
                                                 scale=float(D) ** -0.5,
                                                 accum_out=SM[:, 272 + 2 * i + h:273 + 2 * i + h]),
                            "mem_sq" if h else None)

            def drain_model(prefix, tt):
                for q in range(4):
                    drain(f"{prefix}{tt}{q}", HT[:, 4 * q:4 * q + 4, P * tt:P * tt + P], four(4))

            def exps(scores, n, w, base, sem):
                for i in range(n):
                    ins = nc.scalar.activation(scores[:, w * i:w * i + w], scores[:, w * i:w * i + w], ACT.Exp,
                                               bias=SM[:, 224 + base + i:225 + base + i],
                                               accum_out=SM[:, 240 + base + i:241 + base + i])
                    st.link(ins, sem if i == n - 1 else None)

            act.wait_ge(s["x_in0"], 16)
            mean_square(X[:, 0, :], xn_of[0], 144, "mean_sq")
            act.wait_ge(s["x_in1"], 16)
            mean_square(X[:, 1, :], xn_of[1], 145, "mean_sq")
            drain_model("xT", 0)
            drain_model("xT", 1)
            act.wait_ge(s["ssm_in"], 16 * 7)
            st.link(nc.scalar.activation(SM[0:SSM_TILES, 2:4], SM[0:SSM_TILES, 0:2], ACT.Exp), "step_size")
            act.wait_ge(s["lam_in"], 1)
            st.link(nc.scalar.activation(SR[:, 4, :], SR[:, 2, :], ACT.Exp))
            st.link(nc.scalar.activation(SR[:, 6, :], SR[:, 3, :], ACT.Sin))
            st.link(nc.scalar.activation(SR[:, 7, :], SR[:, 3, :], ACT.Sin, scale=0.5), "lam_out")
            drain("u0", UT[:, 0:2, :], four(2))
            drain("u1", UT[:, 2:4, :], four(2))
            drain("ssmP", SM[:, 16:80], cols=64)
            drain("params", PR[:, :], cols=TAPS + NROW)
            drain("bias", DSB, cols=BIAS_W, parts=SWA_H)
            act.wait_ge(s["psum_drained"], TASK_NO["bias"] + 1)
            act.dma_start(dist_d, DSB).then_inc(s["dist_out"], 16)
            act.wait_ge(s["zeroed"], 1)
            drain("za0", ZP[:, 0:2, CONV_W - 1:CONV_W - 1 + T], four(2))
            for c in range(2):
                drain(f"ssmB{c}", BL[:, c, :, :], four(4))
            for c in range(2):
                drain(f"ssmC{c}", CL[:, c, :, :], four(4), scale=1.0 if c == 0 else -1.0)

            def drain_states(js):
                for j in js:
                    drain(f"bu{j}", XSt[:, :, j % HALF, :], four(2))

            drain_states(range(HALF))
            act.wait_ge(s["mem_in"], 16)
            memory_square(0)
            drain("za1", ZP[:, 2:4, CONV_W - 1:CONV_W - 1 + T], four(2))
            for i in range(2):
                drain(f"zg{i}", ZG[:, 2 * i:2 * i + 2, :], four(2), func=ACT.Tanh, scale=0.5)
            drain("cq0", CQ[:, 0, :])
            drain("y0", OT[:, 12:14, :], four(2))
            drain_states(range(HALF, SSM_TILES))
            drain("cq1", CQ[:, 1, :])
            for tt in range(TT):
                drain(f"ckv{tt}", CKV[:, tt, :], cols=320)
            act.wait_ge(s["psum_drained"], TASK_NO["bias"] + 1)
            for tt in range(TT):
                drain(f"sq{tt}", SQ[:, tt, :])
            act.wait_ge(s["dist_out"], 16)
            for tt in range(TT):
                drain(f"skv{tt}", SKV[:, tt, :], cols=256)
            drain("y1", OT[:, 14:16, :], four(2))
            drain_model("mT", 0)
            act.wait_ge(s["rows_in"], 16 * 7)
            for tt in range(TT):
                drain_parts(f"cqT{tt}", [(CQT[:, k, P * tt:P * tt + P], lambda b, k=k: b[:, P * k:P * k + P],
                                          dict(func=ACT.Copy, scale=GK[:, k:k + 1])) for k in range(4)])
            drain_parts("ckvT", [(CKVT[:, k, :], lambda b, k=k: b[:, T * k:T * k + T],
                                  dict(func=ACT.Copy, scale=GK[:, 4 + k:5 + k])) for k in range(2)])
            act.wait_ge(s["mem1_in"], 16)
            memory_square(1)
            for tt in range(TT):
                for g in range(2):
                    drain(f"mq{tt}{g}", MQ[:, tt, 384 * g:384 * g + 384], cols=384)
            act.wait_ge(s["gelu_in"], 1)
            st.link(nc.scalar.activation(L0[:, 0:1024], L0[:, 0:1024], ACT.Tanh, scale=0.7978845608028654), "gelu_th")
            for tt in range(TT):
                for g in range(2):
                    drain(f"mkv{tt}{g}", MKV[:, tt, 512 * g:512 * g + 512])
            for tt in range(TT):
                drain(f"sqT{tt}", SQT[:, :, P * tt:P * tt + P], four(4), scale=SM[:, 152:153])
            drain("skT", SKT[:, :, :].rearrange("p v (t q) -> p t v q", t=TT),
                  lambda b: b.rearrange("p (t v q) -> p t v q", t=TT, v=SWA_KV), scale=col("swa_kn_g"))
            drain_model("mT", 1)
            drain("xv0", VX[:, 0, :])
            for tt in range(TT):
                drain(f"qnT{tt}", QNT[:, :, P * tt:P * tt + P], four(4), scale=col("mla_qn_nope_g"))
            for tt in range(TT):
                drain(f"qrT{tt}", QRT[0:64, :, P * tt:P * tt + P], four(4), parts=64)
            for tt in range(TT):
                drain(f"knT{tt}", KNT[:, :, P * tt:P * tt + P], four(4), scale=col("mla_kn_nope_g"))
            drain("krT", KRT[0:64, :], cols=T, parts=64)
            mla_scale = float(QK_D) ** -0.5
            drain("ml0", L0[:, 0:512], scale=mla_scale)
            drain("ml10", L0[:, 512:1024], scale=mla_scale)
            drain("ml11", L0[:, 1024:1536], scale=mla_scale)
            drain("sl00", L1[:, 0:512])
            drain("sl01", L1[:, 512:1024])
            act.wait_ge(s["ml_max"], 1)
            exps(L0[:, 0:512], 4, P, 0, "ml_exp")
            act.wait_ge(s["ml_max"], 2)
            exps(L0[:, 512:1536], 4, T, 4, "ml_exp")
            act.wait_ge(s["sink_in"], 1)
            st.link(nc.scalar.activation(SM[:, 256:264], SM[:, 256:264], ACT.Exp))
            exps(L1[:, 0:1024], 8, P, 0, "sl_exp")
            drain("xv1", VX[:, 1, :])
            drain("mp0", PT[:, 0:512])
            act.wait_ge(s["conv_done"], 1)
            drain("mo0", OT[:, 8:12, 0:P], four(4))
            drain("mp10", PT[:, 512:1024])
            drain("mp11", PT[:, 1024:1536])
            drain("mo1", OT[:, 8:12, P:T], four(4))
            for i in range(2):
                drain_parts(f"glu{i}", [(UT[:, 2 * i + f, :], lambda b, f=f: b[:, T * f:T * f + T],
                                         dict(func=ACT.Tanh, scale=0.5, bias=SM[:, 153 + 2 * i + f:154 + 2 * i + f]))
                                        for f in range(2)])
            drain("cm", RG[:, 0, :], cols=T, scale=1.0 / GW)
            for i in range(4):
                drain(f"sl1{i}", L0[:, 512 * i:512 * i + 512])
            act.wait_ge(s["sink_in"], 2)
            st.link(nc.scalar.activation(SM[:, 264:272], SM[:, 264:272], ACT.Exp))
            exps(L0[:, 0:2048], 8, T, 8, "sl_exp")
            drain("xk0", KX[:, 0, :])

            def root_mean_square(name, dst):
                drain(name, dst, cols=T, func=ACT.Sqrt, scale=1.0 / GW, bias=const("eps"))

            root_mean_square("cv", RG[:, 1, :])
            root_mean_square("gs2", RG2[:, 2, :])
            drain("sp00", PT[:, 0:512])
            drain("sp01", PT[:, 512:1024])
            drain("so0", OT[:, 0:4, 0:P], four(4))
            act.wait_ge(s["conv_y"], 1)
            st.link(nc.scalar.activation(SQG, ZT, ACT.Tanh, scale=0.5), "conv_th")
            drain("xk1", KX[:, 1, :])
            root_mean_square("gs3", RG2[:, 3, :])
            for i in range(2):
                drain_parts(f"pw{i}", [(OT[:, 4 + 2 * i + f, :], lambda b, f=f: b[:, T * f:T * f + T],
                                        dict(func=ACT.Identity, scale=1.0, bias=col("conv_pw_b", 2 * i + f)))
                                       for f in range(2)])
            for i in range(4):
                drain(f"sp1{i}", PT[:, 512 * i:512 * i + 512])
            drain("so1", OT[:, 0:4, P:T], four(4))
            for m in range(2):
                drain(f"kxT{m}", KXT[:, :, P * m:P * m + P], four(4), scale=col("xa_kn_g"))
            root_mean_square("gs1", RG2[:, 1, :])
            root_mean_square("gs0", RG2[:, 0, :])
            for n in range(4):
                for tt in range(TT):
                    drain(f"wo{n}{tt}", X[:, tt, 512 * n:512 * n + 512])
                    if n == 3 and tt == 0:
                        wait_task(act, "wo30")
                        mean_square(X[:, 0, :], xn_of[0], 148, "c_sq")
            for tt in range(TT):
                drain_model("cT", tt)
                if tt == 0:
                    wait_task(act, "wo31")
                    mean_square(X[:, 1, :], xn_of[1], 149, "c_sq")
                drain(f"xq{tt}", QX[:, tt, :])
            for n in range(TT):
                drain(f"qxT{n}", QXT[:, :, P * n:P * n + P], four(4), scale=col("xa_qn_g"))
                for i in range(2):
                    drain(f"xl{n}{i}", XL[:, n, 2 * i:2 * i + 2, :], four(2), scale=float(P) ** -0.5)
            for n in range(TT):
                act.wait_ge(s["xl_max"], n + 1)
                exps(XL[:, n, :, :].rearrange("p h w -> p (h w)"), 4, T, 4 * n, "xl_exp")
            for n in range(TT):
                for i in range(2):
                    drain(f"xp{n}{i}", XPT[:, n, 4 * i:4 * i + 4, :], four(4))
                drain(f"xo{n}", XOT[:, :, P * n:P * n + P], four(4))
                if n:
                    wait_task(act, "co30")
                    mean_square(X[:, 0, :], xn_of[0], 150, "m_sq")
                for c in range(4):
                    drain(f"co{c}{n}", X[:, n, 512 * c:512 * c + 512])
            wait_task(act, "co31")
            mean_square(X[:, 1, :], xn_of[1], 151, "m_sq")
            for tt in range(TT):
                drain_model("hT", tt)
                drain(f"rl{tt}", RT[:, 128 + 36 * tt:164 + 36 * tt], cols=36)
            act.wait_ge(s["g_max"], 2)
            st.link(nc.scalar.activation(RB[:, 0:8], RB[:, 0:8], ACT.Exp))
            st.link(nc.scalar.activation(RB[:, 8:10], RB[:, 8:10], ACT.Exp), "g_exp")
            drain("pos", RT[:, 256:352], cols=96)
            drain("tab", RT[:, 480:480 + 2 * TABLE], cols=2 * TABLE)
            assert task[0] == len(TASKS)

            wait_task(act, "pos")
            act.wait_ge(s["split_h"], 4)
            act.wait_ge(s["x2_out"], 32)
            act.sem_inc(s["y_sb"], 5)

            def drain_rows(b, k0, n):
                act.wait_ge(s["gathered"], n)
                nc.scalar.activation(XG[:, k0:k0 + 8, :], b[:, :].rearrange("p (k m) -> p k m", k=8),
                                     ACT.Copy).then_inc(s["xg_ready"], 1)

            def high_part(j, at, q):
                seen = 16 * (front_uses[MOE_SLOT[q]] + (1 if q < 8 else 0))
                act.wait_ge(slot_in[MOE_SLOT[q]], 16 * j + seen)
                act.wait_ge(s["split_free"], PPE * j + at + 1)
                return nc.scalar.activation(WH[:, at % HI_RING, :], moe_slot(q), ACT.Copy)

            def drain_gate_up(j):
                act.wait_ge(s["split_free"], PPE * j + HI_RING + 8)
                for g in range(2):
                    nc.scalar.activation(GU[:, FF * g:FF * g + FF], gu[g][0:S2, :], ACT.Copy).then_inc(s["gu_sb"], 1)

            def tanh_gate(j):
                act.wait_ge(s["t_done"], j)
                nc.scalar.activation(TH, tb[:, 0:4 * SLOTS], ACT.Tanh, scale=0.5).then_inc(s["th_done"], 1)

            def drain_results(j, first, parts):
                act.wait_ge(s["dest_idx"], j)
                for n in parts:
                    act.wait_ge(s["split_free"], PPE * j + HI_RING + first + n + 1)
                    nc.scalar.activation(YS[:, 512 * n:512 * n + 512], yb[n % 2][0:S2, :], ACT.Copy,
                                         scale=dw[0:S2, 1:2]).then_inc(s["y_sb"], 1)

            for q in range(HI_RING):
                high_part(0, q, q).then_inc(s["hi_ready"], 1)
            for i in range(2):
                drain_rows(rest[i], 8 * i, i + 1)
            for q in range(HI_RING, 8):
                high_part(0, q, q).then_inc(s["hi_ready"], 1 if q < 7 else 5)
            drain_gate_up(0)
            drain_rows(rest[0], 0, 3)
            act.wait_ge(s["tables"], 1)
            n_reg = act.value_load(n_blk[0:1, 0:1], min_val=2, max_val=MAX_BLOCKS)

            def turn(j, last):
                drain_rows(rest[1], 8, 2 * j + 2)
                tanh_gate(j)
                for q in range(3, 11):
                    high_part(j, q, q).then_inc(s["hi_ready"], 1)
                drain_gate_up(j)
                high_part(j, 11, 11).then_inc(s["hi_ready"], 1)
                drain_results(j, 8, (0, 1))
                drain_rows(rest[0], 0, 2 * j + 3)
                if not last:
                    high_part(j + 1, 0, 0).then_inc(s["hi_ready"], 1)
                    high_part(j + 1, 1, 1).then_inc(s["hi_ready"], 1)
                drain_results(j, 8, (2, 3))
                if not last:
                    high_part(j + 1, 2, 2).then_inc(s["hi_ready"], 1)

            for q in range(3):
                high_part(1, q, q).then_inc(s["hi_ready"], 1)
            last_block = act.value_load(n_blk[0:1, 1:2], min_val=1, max_val=MAX_BLOCKS - 1)
            with act.Fori(1, last_block) as j:
                turn(j, last=False)
            turn(last_block, last=True)
            tanh_gate(n_reg)
            for n in range(4):
                high_part(n_reg, n, 8 + n).then_inc(s["hi_ready"], 1)
            drain_results(n_reg, 0, range(4))


        @block.vector
        def _(dve):
            st = Steps(dve, "dve_order")
            link = st.link
            v = nc.vector

            def bc(ap, shape):
                return ap.to_broadcast(shape)

            def rsqrt(r):
                a, y, w = (SM[:, o:o + r] for o in (160, 176, 192))
                link(v.tensor_scalar(w.bitcast(I32), a.bitcast(I32), 1, None, ALU.arith_shift_right))
                link(v.tensor_scalar(y.bitcast(I32), w.bitcast(I32), -1.0, float(0x5F3759DF), ALU.mult, ALU.add))
                for _ in range(3):
                    link(v.tensor_tensor(w, y, y, ALU.mult))
                    link(v.tensor_tensor(w, w, a, ALU.mult))
                    link(v.tensor_scalar(w, w, -0.5, 1.5, ALU.mult, ALU.add))
                    link(v.tensor_tensor(y, y, w, ALU.mult))

            def model_norm(dst, src, gain, at, sem):
                link(v.tensor_scalar(SM[:, 160:161], SM[:, at:at + 1], EPS, None, ALU.add))
                rsqrt(1)
                link(v.scalar_tensor_tensor(dst, src, SM[:, 176:177], gain, ALU.mult, ALU.mult), sem)

            def head_norm(src, tmp, r, d, sem=None):
                t = tmp[:, 0:r * d].rearrange("p (r d) -> p r d", r=r)
                link(v.tensor_tensor(t, src, src, ALU.mult))
                link(v.tensor_reduce(SM[:, 160:160 + r], t, AX.X, ALU.add))
                link(v.tensor_scalar(SM[:, 160:160 + r], SM[:, 160:160 + r], 1.0 / d, EPS, ALU.mult, ALU.add))
                rsqrt(r)
                link(v.tensor_tensor(src, src, bc(SM[:, 176:176 + r].unsqueeze(2), [P, r, d]), ALU.mult), sem)

            def complex_product(dst, a, b, tmp, shape):
                link(v.tensor_tensor(tmp, a[1], b[1], ALU.mult))
                link(v.tensor_tensor(dst[0], a[0], b[0], ALU.mult))
                link(v.tensor_tensor(dst[0], dst[0], tmp, ALU.subtract))
                link(v.tensor_tensor(tmp, a[1], b[0], ALU.mult))
                link(v.tensor_tensor(dst[1], a[0], b[1], ALU.mult))
                link(v.tensor_tensor(dst[1], dst[1], tmp, ALU.add))

            dve.wait_ge(s["gain_in"], 16)
            for tt in range(TT):
                dve.wait_ge(s["mean_sq"], tt + 1)
                model_norm(xn_of[tt], X[:, tt, :], GB[:, :], 144 + tt, "xn")

            dve.wait_ge(s["ssm_in"], 16 * 7)
            dve.wait_ge(s["step_size"], 1)
            dt = bc(SM[0:SSM_TILES, 2:4].unsqueeze(2), [SSM_TILES, 2, 64])

            def row(r):
                return SR[:, r, :]

            def grouped(r):
                return SR[:, r, :].rearrange("p (g n) -> p g n", g=2)

            link(v.tensor_tensor(grouped(2), grouped(0), dt, ALU.mult))
            link(v.tensor_tensor(grouped(3), grouped(1), dt, ALU.mult))
            magic = 12582912.0
            link(v.tensor_scalar(row(5), row(3), 1.0 / (2.0 * np.pi), magic, ALU.mult, ALU.add))
            link(v.tensor_scalar(row(5), row(5), magic, None, ALU.subtract))
            link(v.scalar_tensor_tensor(row(3), row(5), -6.28125, row(3), ALU.mult, ALU.add))
            link(v.scalar_tensor_tensor(row(3), row(5), -(2.0 * np.pi - 6.28125), row(3), ALU.mult, ALU.add))
            link(v.tensor_scalar(row(3), row(3), 3.1415925, -3.1415925, ALU.min, ALU.max), "lam_in")
            link(v.memset(VR[N_BUCKET:N_BUCKET + 1, 256:264], 1.0), "zeroed")
            link(v.memset(ZP[:, :, 0:CONV_W - 1], 0.0), "zeroed")
            dve.wait_ge(s["lam_out"], 1)
            link(v.tensor_tensor(row(7), row(7), row(7), ALU.mult))
            link(v.tensor_scalar(row(7), row(7), -2.0, 1.0, ALU.mult, ALU.add))
            link(v.tensor_tensor(row(5), row(4), row(7), ALU.mult))
            link(v.tensor_tensor(row(6), row(4), row(6), ALU.mult))
            link(v.tensor_tensor(row(4), row(0), row(0), ALU.mult))
            link(v.tensor_tensor(row(7), row(1), row(1), ALU.mult))
            link(v.tensor_tensor(row(4), row(4), row(7), ALU.add))
            link(v.reciprocal(row(4), row(4)))
            link(v.tensor_scalar(row(3), row(5), 1.0, None, ALU.subtract))
            link(v.tensor_tensor(row(2), row(3), row(0), ALU.mult))
            link(v.tensor_tensor(row(7), row(6), row(1), ALU.mult))
            link(v.tensor_tensor(row(2), row(2), row(7), ALU.add))
            link(v.tensor_tensor(row(2), row(2), row(4), ALU.mult))
            link(v.tensor_tensor(row(7), row(6), row(0), ALU.mult))
            link(v.tensor_tensor(row(3), row(3), row(1), ALU.mult))
            link(v.tensor_tensor(row(7), row(7), row(3), ALU.subtract))
            link(v.tensor_tensor(row(7), row(7), row(4), ALU.mult), "ssm_lam")
            wait_filled(dve, "xT13")
            dve.wait_ge(s["const_in"], 16)
            for c in range(2):
                shape = [P, 4, 2, 64]
                out4 = CMm[:, c, :].rearrange("p (j g n) -> p j g n", j=4, g=2)
                link(v.tensor_tensor(out4, bc(c_raw[:, c, 0:256].rearrange("p (j n) -> p j n", j=4).unsqueeze(2), shape),
                                     bc(const("cmask").rearrange("p (g n) -> p g n", g=2).unsqueeze(1), shape),
                                     ALU.mult), "ssm_c" if c else None)
            link(v.memset(BDm, 0.0))
            wait_task(dve, "ssmP")
            lam_r, lam_i, fac_r, fac_i = (SM[:, 16 + 16 * i:32 + 16 * i] for i in range(4))
            bs = [P, SSM_TILES, 16]
            bt = [APT[:, 256 * i:256 * i + 256].rearrange("p (j i) -> p j i", i=16) for i in range(3)]
            complex_product((bt[0], bt[1]), (b_raw[:, 0, 0:256].rearrange("p (j i) -> p j i", i=16),
                                             b_raw[:, 1, 0:256].rearrange("p (j i) -> p j i", i=16)),
                            (bc(fac_r.unsqueeze(2), bs), bc(fac_i.unsqueeze(2), bs)), bt[2], bs)
            for c in range(2):
                for g in range(2):
                    o = BDm[64 * g:64 * g + 64, c, :].rearrange("p (j i) -> p j i", i=32)
                    link(v.tensor_copy(o[:, :, 16 * g:16 * g + 16], bt[c][64 * g:64 * g + 64]),
                         "ssm_b" if c and g else None)
            for c, lam in enumerate((lam_r, lam_i)):
                link(v.tensor_copy(PW[:, c, :, 0:1], lam.unsqueeze(2)))
            for n in (1, 2, 4, 8):
                sh = [P, SSM_TILES, n]
                t = APT[:, 0:SSM_TILES * n].rearrange("p (j n) -> p j n", n=n)
                complex_product((PW[:, 0, :, n:2 * n], PW[:, 1, :, n:2 * n]), (PW[:, 0, :, 0:n], PW[:, 1, :, 0:n]),
                                (bc(PW[:, 0, :, n - 1:n], sh), bc(PW[:, 1, :, n - 1:n], sh)), t, sh)
            signed = []
            for at, power in ((80, 0), (112, SCAN_L - 1)):
                a = SM[:, at:at + 32].rearrange("p (c j) -> p c j", c=2)
                link(v.tensor_copy(a[:, 0, :].unsqueeze(2), PW[:, 1, :, power:power + 1]))
                link(v.tensor_scalar(a[:, 1, :], a[:, 0, :], -1.0, None, ALU.mult))
                signed.append(a)

            def scan_half(half):
                tiles = slice(HALF * half, HALF * half + HALF)

                def step(dst, src, power, sign, t1, t2, shape):
                    re = bc(PW[:, 0, tiles, power].unsqueeze(1).unsqueeze(3), shape)
                    im = bc(sign[:, :, tiles].unsqueeze(3), shape)
                    link(v.tensor_tensor(t1, src, re, ALU.mult))
                    link(v.tensor_tensor(t2, src, im, ALU.mult))
                    link(v.tensor_tensor(dst, dst, t1, ALU.add))
                    link(v.tensor_tensor(dst, dst, t2[:, ::-1], ALU.add))

                for i in range(1, SCAN_L):
                    step(XS[:, :, :, :, i], XS[:, :, :, :, i - 1], 0, signed[0], T1, T2, [P, 2, HALF, SCAN_L])
                for k in range(1, SCAN_L):
                    step(XS[:, :, :, k, SCAN_L - 1:], XS[:, :, :, k - 1, SCAN_L - 1:], SCAN_L - 1, signed[1],
                         T1[:, :, :, 0:1], T2[:, :, :, 0:1], [P, 2, HALF, 1])
                n = SCAN_L - 1
                sh = [P, HALF, n, n]
                t = APT[:, 0:HALF * n * n].rearrange("p (j k l) -> p j k l", j=HALF, k=n)
                for dst, src, power, op in ((0, 0, 0, ALU.add), (0, 1, 1, ALU.subtract), (1, 1, 0, ALU.add),
                                            (1, 0, 1, ALU.add)):
                    link(v.tensor_tensor(t, bc(PW[:, power, tiles, 0:n].unsqueeze(2), sh),
                                         bc(XS[:, src, :, 0:n, n:], sh), ALU.mult))
                    o = XS[:, dst, :, 1:, 0:n]
                    link(v.tensor_tensor(o, o, t, op), "scan_done" if (dst, src) == (1, 0) else None)

            wait_task(dve, f"bu{HALF - 1}")
            scan_half(0)

            def memory_norm(i):
                dve.wait_ge(s["mem_sq"], i + 1)
                link(v.tensor_tensor(SM[:, 146 + i:147 + i], SM[:, 272 + 2 * i:273 + 2 * i],
                                     SM[:, 273 + 2 * i:274 + 2 * i], ALU.add))
                model_norm(XN[:, :], XN[:, :], GB[:, :], 146 + i, "mem_n")

            dve.wait_ge(s["mem_gain_in"], 16)
            memory_norm(0)
            wait_task(dve, f"bu{SSM_TILES - 1}")
            scan_half(1)

            wait_task(dve, "cq1")
            head_norm(CQ, APT, TT, 512, "cq_n")

            wait_task(dve, "ckv1")
            head_norm(CKV[:, :, 0:256], APT, TT, 256, "ckv_n")

            def rope(x, heads, TMP):
                sh = [P, TT, heads, 32]
                cos, sin = (bc(const(n).rearrange("p (t f) -> p t f", t=TT).unsqueeze(2), sh) for n in ("cos", "sin"))
                a, b, c, d = (TMP[:, 256 * i:256 * i + 64 * heads].rearrange("p (t h f) -> p t h f", t=TT, h=heads)
                              for i in range(4))
                x1, x2 = x[:, :, :, 0:32], x[:, :, :, 32:64]
                link(v.tensor_tensor(a, x1, cos, ALU.mult))
                link(v.tensor_tensor(b, x2, sin, ALU.mult))
                link(v.tensor_tensor(c, x1, sin, ALU.mult))
                link(v.tensor_tensor(d, x2, cos, ALU.mult))
                link(v.tensor_tensor(x1, a, b, ALU.subtract))
                return v.tensor_tensor(x2, c, d, ALU.add)

            dve.wait_ge(s["rows_in"], 16 * 7)
            kr = CKV[:, :, 256:320]
            head_norm(kr, APT, TT, 64)
            link(v.tensor_tensor(kr, kr, bc(BC[:, 72:136].unsqueeze(1), [P, TT, 64]), ALU.mult))
            link(rope(kr.unsqueeze(2), 1, APT))
            wait_task(dve, "sq1")
            link(v.tensor_scalar(SM[:, 152:153], col("swa_qn_g"), float(SWA_D) ** -0.5, None, ALU.mult))
            link(v.tensor_scalar(SM[:, 153:157], PR[:, TAPS + ROW["ssm_glu_b"]:TAPS + ROW["ssm_glu_b"] + 4], 0.5, None,
                                 ALU.mult))
            head_norm(flat(SQ[:, :, :]).rearrange("p (r n) -> p r n", n=SWA_D), APT, TT * SWA_H, SWA_D, "sq_n")
            wait_task(dve, "skv1")
            keys = SKV[:, :, 0:128].rearrange("p t (v n) -> p t v n", v=SWA_KV)
            ks = [P, TT, SWA_KV, SWA_D]
            kt = APT[:, 0:256].rearrange("p (t v n) -> p t v n", t=TT, v=SWA_KV)
            link(v.tensor_tensor(kt, keys, keys, ALU.mult))
            link(v.tensor_reduce(SM[:, 160:164].rearrange("p (t v) -> p t v", t=TT), kt, AX.X, ALU.add))
            link(v.tensor_scalar(SM[:, 160:164], SM[:, 160:164], 1.0 / SWA_D, EPS, ALU.mult, ALU.add))
            rsqrt(4)
            link(v.tensor_tensor(kt, keys, bc(SM[:, 176:180].rearrange("p (t v) -> p t v", t=TT).unsqueeze(3), ks),
                                 ALU.mult))
            link(v.tensor_copy(flat(OT[:, 2:4, :]).rearrange("p (r d n) -> p r d n", d=2, n=SWA_D),
                               bc(APT[:, 0:256].rearrange("p (r n) -> p r n", n=SWA_D).unsqueeze(2),
                                  [P, TT * SWA_KV, 2, SWA_D])), "sq_n")

            wait_task(dve, "y1")
            yo = OT[:, 12:16, :]
            for k in range(GC):
                link(v.scalar_tensor_tensor(yo[:, k, :], UT[:, k, :], col("ssm_d", k), yo[:, k, :], ALU.mult, ALU.add))
            g1 = L0[:, 0:1024].rearrange("p (k t) -> p k t", k=GC)
            link(v.tensor_tensor(g1, yo, yo, ALU.mult))
            link(v.tensor_scalar(g1, g1, 0.044715, 1.0, ALU.mult, ALU.add))
            link(v.tensor_tensor(g1, g1, yo, ALU.mult), "gelu_in")
            memory_norm(1)
            dve.wait_ge(s["gelu_th"], 1)
            link(v.tensor_scalar(g1, g1, 0.5, 0.5, ALU.mult, ALU.add))
            link(v.tensor_tensor(yo, yo, g1, ALU.mult), "gelu")
            wait_task(dve, "mq11")
            q8 = flat(MQ).rearrange("p (r n) -> p r n", n=QK_D)
            head_norm(q8[:, :, 0:NOPE], L0, TT * MLA_H, NOPE)
            qr = q8[:, :, NOPE:QK_D]
            head_norm(qr, L0, TT * MLA_H, ROPE)
            link(v.tensor_tensor(qr, qr, bc(BC[:, 8:72].unsqueeze(1), [P, TT * MLA_H, ROPE]), ALU.mult))
            link(rope(MQ.rearrange("p t (h n) -> p t h n", n=QK_D)[:, :, :, NOPE:QK_D], MLA_H, L0), "mq_n")
            wait_task(dve, "mkv11")
            head_norm(flat(MKV).rearrange("p (r n) -> p r n", n=256)[:, :, 0:NOPE], L0, TT * MLA_H, NOPE, "mkv_n")

            def row_maximum(scores, n, w, base, sem, sink=None):
                m, neg = SM[:, 208:208 + n], SM[:, 224 + base:224 + base + n]
                link(v.tensor_reduce(m, scores.rearrange("p (h w) -> p h w", w=w), AX.X, ALU.max))
                if sink is not None:
                    link(v.tensor_tensor(m.rearrange("p (b i) -> p b i", b=2), m.rearrange("p (b i) -> p b i", b=2),
                                         sink, ALU.max))
                link(v.tensor_scalar(neg, m, -1.0, None, ALU.mult), sem)

            def normalise(scores, n, w, base, sem):
                sums = SM[:, 240 + base:240 + base + n]
                link(v.reciprocal(sums, sums))
                p3 = scores.rearrange("p (h w) -> p h w", w=w)
                link(v.tensor_tensor(p3, p3, bc(sums.unsqueeze(2), [P, n, w]), ALU.mult), sem)

            wait_task(dve, "ml11")
            for n, scores in ((0, L0[:, 0:512]), (1, L0[:, 512:1536])):
                w = P * (n + 1)
                p3 = scores.rearrange("p (h w) -> p h w", w=w)
                mask = const("causal")[:, P * (1 - n):]
                link(v.tensor_tensor(p3, p3, bc(mask.unsqueeze(1), [P, MLA_H, w]), ALU.add))
                row_maximum(scores, MLA_H, w, 4 * n, "ml_max")
            sink = BC[:, 0:8].rearrange("p (i b) -> p b i", b=2)

            def window_maximum(n, scores):
                row_maximum(scores, SWA_H, P * (n + 1), 8 * n, "sl_max", sink=sink)
                link(v.tensor_tensor(SM[:, 256 + 8 * n:264 + 8 * n].rearrange("p (b i) -> p b i", b=2), sink,
                                     SM[:, 224 + 8 * n:232 + 8 * n].rearrange("p (b i) -> p b i", b=2), ALU.add),
                     "sink_in")

            def window_normalise(n, scores):
                dve.wait_ge(s["sl_exp"], n + 1)
                sums = SM[:, 240 + 8 * n:248 + 8 * n]
                link(v.tensor_tensor(sums, sums, SM[:, 256 + 8 * n:264 + 8 * n], ALU.add))
                normalise(scores, SWA_H, P * (n + 1), 8 * n, "sl_p")

            for n, scores in ((0, L0[:, 0:512]), (1, L0[:, 512:1536])):
                dve.wait_ge(s["ml_exp"], n + 1)
                normalise(scores, MLA_H, P * (n + 1), 4 * n, "ml_p")
            wait_task(dve, "sl01")
            window_maximum(0, L1[:, 0:1024])
            window_normalise(0, L1[:, 0:1024])

            wait_task(dve, "glu1")
            link(v.tensor_scalar(UT[:, :, :], UT[:, :, :], 0.5, 0.5, ALU.mult, ALU.add))
            link(v.tensor_tensor(yo, yo, UT[:, :, :], ALU.mult), "glu_o")

            def group_square(g, squares):
                o = OT[:, 4 * g:4 * g + 4, :]
                link(v.tensor_tensor(squares, o, o, ALU.mult), "og_sq")

            def group_scale(g):
                o = OT[:, 4 * g:4 * g + 4, :]
                wait_task(dve, f"gs{g}")
                link(v.reciprocal(RG2[:, g, :], RG2[:, g, :]))
                for k in range(GC):
                    link(v.scalar_tensor_tensor(o[:, k, :], o[:, k, :], col("mix_out_g", 4 * g + k), RG2[:, g, :],
                                                ALU.mult, ALU.mult), "og_n" if k == GC - 1 else None)

            oc = OT[:, 4:8, :]
            wait_task(dve, "cm")
            link(v.tensor_tensor(oc, oc, bc(RG[:, 0, :].unsqueeze(1), [P, GC, T]), ALU.subtract))
            link(v.tensor_tensor(SQG, oc, oc, ALU.mult), "conv_sq")
            group_square(2, SQ2[:, :, :])
            wait_task(dve, "sl13")
            window_maximum(1, L0[:, 0:2048])
            wait_task(dve, "cv")
            link(v.reciprocal(RG[:, 1, :], RG[:, 1, :]))
            link(v.tensor_tensor(oc, oc, bc(RG[:, 1, :].unsqueeze(1), [P, GC, T]), ALU.mult))
            for k in range(GC):
                link(v.tensor_scalar(ZT[:, k, :], oc[:, k, :], col("conv_ln_g", k), col("conv_ln_b", k), ALU.mult,
                                     ALU.add), "conv_y" if k == GC - 1 else None)
            group_scale(2)
            group_square(3, SQ2[:, :, :])
            dve.wait_ge(s["conv_th"], 1)
            link(v.tensor_scalar(SQG, SQG, 0.5, 0.5, ALU.mult, ALU.add))
            link(v.tensor_tensor(ZT, ZT, SQG, ALU.mult), "conv_z")
            window_normalise(1, L0[:, 0:2048])
            group_scale(3)
            wait_task(dve, "xk1")
            head_norm(flat(KX).rearrange("p (r n) -> p r n", n=P), XN, TT * XA_H, P, "kx_n")
            wait_task(dve, "pw1")
            group_square(1, SQG)
            wait_task(dve, "so1")
            group_square(0, SQ2[:, :, :])
            group_scale(1)
            group_scale(0)

            dve.wait_ge(s["cross_gain_in"], 16)
            for tt in range(TT):
                dve.wait_ge(s["c_sq"], tt + 1)
                model_norm(xn_of[tt], X[:, tt, :], GB2, 148 + tt, "c_n")
            wait_filled(dve, "cT03")
            for tt in range(TT):
                wait_task(dve, f"xq{tt}")
                head_norm(QX[:, tt, :].rearrange("p (r n) -> p r n", n=P), XN, XA_H, P, "qx_n")
            for n in range(TT):
                wait_task(dve, f"xl{n}1")
                row_maximum(XL[:, n].rearrange("p h w -> p (h w)"), XA_H, T, 4 * n, "xl_max")
            for n in range(TT):
                dve.wait_ge(s["xl_exp"], n + 1)
                normalise(XL[:, n].rearrange("p h w -> p (h w)"), XA_H, T, 4 * n, "xl_p")

            dve.wait_ge(s["moe_gain_in"], 16)
            for tt in range(TT):
                dve.wait_ge(s["m_sq"], tt + 1)
                model_norm(xn_of[tt], X[:, tt, :], GB[:, :], 150 + tt, "m_n")
                link(v.tensor_copy(HH[:, tt, :], xn_of[tt]), "split_h")
                link(v.tensor_tensor(HL[:, tt, :], xn_of[tt], HH[:, tt, :].bitcast(F32), ALU.subtract), "split_h")

            wait_task(dve, "rl1")
            wait_filled(dve, "hT03")
            RL = RT[:, 128:200].rearrange("p (t n) -> p t n", t=TT)
            link(v.tensor_tensor(RL, RL, bc(BC[:, 136:172].unsqueeze(1), [P, TT, 36]), ALU.add))
            place = [16]

            def take(*shape):
                n = int(np.prod(shape))
                a = RB[:, place[0]:place[0] + n]
                place[0] += n
                if len(shape) == 1:
                    return a
                if len(shape) == 2:
                    return a.rearrange("p (a b) -> p a b", a=shape[0])
                return a.rearrange("p (a b c) -> p a b c", a=shape[0], b=shape[1])

            far = 64.0
            numbers = const("i32")

            def first_max(x, n, top, which, one_hot):
                t = take(TT, n)
                link(v.tensor_reduce(top, x, AX.X, ALU.max))
                link(v.tensor_tensor(t, x, bc(top.unsqueeze(2), [P, TT, n]), ALU.is_equal))
                link(v.tensor_scalar(t, t, -far, far, ALU.mult, ALU.add))
                link(v.tensor_tensor(t, t, bc(numbers[:, 0:n].unsqueeze(1), [P, TT, n]), ALU.add))
                link(v.tensor_reduce(which, t, AX.X, ALU.min))
                link(v.tensor_tensor(one_hot, bc(numbers[:, 0:n].unsqueeze(1), [P, TT, n]),
                                     bc(which.unsqueeze(2), [P, TT, n]), ALU.is_equal))

            g_top, g_at, g_hot = take(TT), take(TT), take(TT, N_GROUPS)
            first_max(RL[:, :, 0:4], N_GROUPS, g_top, g_at, g_hot)
            link(v.tensor_tensor(RB[:, 0:8].rearrange("p (t n) -> p t n", t=TT), RL[:, :, 0:4],
                                 bc(g_top.unsqueeze(2), [P, TT, N_GROUPS]), ALU.subtract), "g_max")
            in_g = take(TT, N_GROUPS, PER_GROUP)
            shape = [P, TT, N_GROUPS, PER_GROUP]
            link(v.tensor_tensor(in_g, RL[:, :, 4:36].rearrange("p t (g e) -> p t g e", g=N_GROUPS),
                                 bc(g_hot.unsqueeze(3), shape), ALU.mult))
            el = take(TT, PER_GROUP)
            link(v.tensor_reduce(el, in_g.rearrange("p t g e -> p t e g"), AX.X, ALU.add))
            tops, ats, hots = [], [], []
            for k in range(2):
                tops.append(take(TT))
                ats.append(take(TT))
                hots.append(take(TT, PER_GROUP))
                first_max(el, PER_GROUP, tops[k], ats[k], hots[k])
                if k == 0:
                    link(v.scalar_tensor_tensor(el, hots[0], NEG, el, ALU.mult, ALU.add))
            link(v.tensor_tensor(RB[:, 8:10], tops[1], tops[0], ALU.subtract), "g_max")
            marks = [take(TT, N_EXP) for _ in range(2)]
            for k in range(2):
                e_at = take(TT)
                link(v.scalar_tensor_tensor(e_at, g_at, float(PER_GROUP), ats[k], ALU.mult, ALU.add))
                link(v.tensor_tensor(marks[k], bc(numbers.unsqueeze(1), [P, TT, N_EXP]),
                                     bc(e_at.unsqueeze(2), [P, TT, N_EXP]), ALU.is_equal))
            chosen = RT[:, 0:64].rearrange("p (t e) -> p t e", t=TT)
            link(v.tensor_tensor(chosen, marks[0], marks[1], ALU.add), "choice")
            dve.wait_ge(s["g_exp"], 1)
            gs, p1, w1, w2 = take(TT), take(TT), take(TT), take(TT)
            link(v.tensor_reduce(gs, RB[:, 0:8].rearrange("p (t n) -> p t n", t=TT), AX.X, ALU.add))
            link(v.tensor_scalar(p1, RB[:, 8:10], 1.0, None, ALU.add))
            link(v.tensor_tensor(p1, p1, gs, ALU.mult))
            link(v.reciprocal(p1, p1))
            link(v.tensor_scalar(w1, p1, 0.5, None, ALU.mult))
            link(v.tensor_tensor(w2, w1, RB[:, 8:10], ALU.mult))
            row2 = take(TT)
            link(v.tensor_scalar(row2, const("row0"), 2.0, None, ALU.add))
            t = take(TT, N_EXP)
            for part, (a, b) in enumerate(((const("row0"), row2), (w1, w2))):
                o = dv[:, :, :, part]
                link(v.tensor_tensor(t, marks[1], bc(b.unsqueeze(2), [P, TT, N_EXP]), ALU.mult))
                link(v.tensor_tensor(o, marks[0], bc(a.unsqueeze(2), [P, TT, N_EXP]), ALU.mult))
                link(v.tensor_tensor(o, o, t, ALU.add))
            wait_task(dve, "pos")
            link(v.tensor_scalar(posm[:, :, :], RT[:, 256:320].rearrange("p (t e) -> p t e", t=TT), 1.0, None, ALU.add))
            link(v.tensor_tensor(posm[:, :, :], posm[:, :, :], chosen, ALU.mult))
            link(v.tensor_scalar(posm[:, :, :], posm[:, :, :], 1.0, None, ALU.subtract))
            for tt in range(TT):
                link(v.tensor_scalar(SEL[:, tt, :], const("slot"), posm[:, tt, 0:1], None, ALU.is_equal), "sel_part")
            link(v.tensor_copy(dvs[:, :, :].unsqueeze(2), dv[:, :, 0:1, :]), "sel")
            cnt = RT[:, 320:352]
            nb, cum, start = take(N_EXP), take(N_EXP), take(N_EXP)
            link(v.tensor_scalar(nb, cnt, 0.0, None, ALU.is_gt))
            for m in range(1, T // SLOTS):
                link(v.scalar_tensor_tensor(nb, cnt, float(m * SLOTS), nb, ALU.is_gt, ALU.add))
            link(v.tensor_scalar(nb[:, 0:1], nb[:, 0:1], 1.0, None, ALU.max))
            link(v.tensor_tensor_scan(cum, const("ones")[:, 0:N_EXP], nb, 0.0, ALU.mult, ALU.add))
            link(v.tensor_tensor(start, cum, nb, ALU.subtract))
            link(v.tensor_copy(n_blk[:, 0:1], cum[0:1, N_EXP - 1:N_EXP]))
            link(v.tensor_scalar(n_blk[:, 1:2], cum[0:1, N_EXP - 1:N_EXP], 1.0, None, ALU.subtract))
            be, first, started = take(1), take(1), take(N_EXP)
            link(v.tensor_scalar(started, cum, const("part"), None, ALU.is_le))
            link(v.tensor_reduce(be, started, AX.X, ALU.add))
            link(v.scalar_tensor_tensor(started, start, const("part"), start, ALU.is_le, ALU.mult))
            link(v.tensor_reduce(first, started, AX.X, ALU.max))
            link(v.tensor_tensor(first, const("part"), first, ALU.subtract))
            assert place[0] <= D
            link(v.tensor_scalar(RT[:, 360:360 + TABLE], ident[:, 0:TABLE], be, None, ALU.mult))
            link(v.tensor_scalar(RT[:, 360 + TABLE:360 + 2 * TABLE], ident[:, 0:TABLE], first, None, ALU.mult),
                 "columns")
            wait_task(dve, "tab")
            link(v.tensor_scalar(blk_e[:, :], RT[0:1, 480:480 + TABLE], float(N_EXP - 1), None, ALU.min))
            link(v.tensor_scalar(off[:, :], RT[:, 480 + TABLE:480 + 2 * TABLE], float(SLOTS), None, ALU.mult), "tables")

            def select(b, e):
                for tt in range(TT):
                    nc.vector.tensor_scalar(SEL[:, tt, :], const("slot"), off[:, bass.ds(b, 1)],
                                            posm[:, tt, bass.ds(e, 1)], ALU.add, ALU.is_equal).then_inc(
                        s["sel_part"], 1)
                return nc.vector.tensor_copy(dvs[:, :, :].unsqueeze(2), dv[:, :, bass.ds(e, 1), :])


            dve.sem_inc(s["lo_ready"], PPE)
            dve.sem_inc(s["hid_steps"], 3)

            def low_part(j, at, q):
                dve.wait_ge(s["hi_ready"], PPE * j + at + 1)
                dve.wait_ge(s["split_free"], PPE * j + at + 1 + HI_RING - LO_RING)
                return nc.vector.tensor_tensor(WL[:, at % LO_RING, :], moe_slot(q),
                                               WH[:, at % HI_RING, :].bitcast(F32), ALU.subtract)

            def use_destinations(j):
                dve.wait_ge(s["y_free"], j)
                nc.vector.tensor_copy(dw[0:S2, :], dw_next[0:S2, :]).then_inc(s["dw_set"], 1)
                dve.wait_ge(s["dw_set"], j)
                nc.vector.tensor_scalar(slot_row[0:S2, :], dw[0:S2, 0:1], const("half")[0:S2], None, ALU.add).then_inc(
                    s["dest_idx"], 1)

            def take_destinations(j):
                dve.wait_ge(s["dest_done"], j + 1)
                nc.vector.tensor_copy(dw_next[0:S2, :], db[0:S2, 0:2]).then_inc(s["d_bank"], 1)

            def hidden(j):
                dve.wait_ge(s["th_done"], j)
                nc.vector.scalar_tensor_tensor(H2, TH, 1.0, tb[:, 0:4 * SLOTS], ALU.add, ALU.mult).then_inc(
                    s["hid_steps"], 1)
                dve.wait_ge(s["hid_steps"], 3 * j + 1)
                nc.vector.tensor_tensor(H2, H2, tb[:, 256:256 + 4 * SLOTS], ALU.mult).then_inc(s["hid_steps"], 1)
                dve.wait_ge(s["hid_steps"], 3 * j + 2)
                h4 = H2.rearrange("p (k m) -> p k m", k=4)
                nc.vector.tensor_copy(HID[:, :, 0:SLOTS], h4).then_inc(s["hid_steps"], 1)
                dve.wait_ge(s["hid_steps"], 3 * j + 3)
                nc.vector.tensor_tensor(HID[:, :, SLOTS:S2], h4, HID[:, :, 0:SLOTS].bitcast(F32),
                                        ALU.subtract).then_inc(s["hid"], 1)

            for q in range(2):
                low_part(0, q, q).then_inc(s["lo_ready"], 1)
            take_destinations(0)
            e1 = dve.value_load(blk_e[0:1, 1:2], min_val=0, max_val=N_EXP - 1)
            select(1, e1).then_inc(s["sel"], 1)
            for q in range(2, 8):
                low_part(0, q, q).then_inc(s["lo_ready"], 1 if q < 7 else 5)
            n_reg = dve.value_load(n_blk[0:1, 0:1], min_val=2, max_val=MAX_BLOCKS)
            with dve.Fori(1, n_reg) as j:
                for q in range(3):
                    low_part(j, q, q).then_inc(s["lo_ready"], 1)
                e = dve.value_load(blk_e[0:1, bass.ds(j + 1, 1)], min_val=0, max_val=N_EXP - 1)
                dve.wait_ge(s["dest_done"], j + 1)
                select(j + 1, e).then_inc(s["sel"], 1)
                hidden(j)
                for q in range(3, 6):
                    low_part(j, q, q).then_inc(s["lo_ready"], 1)
                use_destinations(j)
                take_destinations(j)
                for q in range(6, PPE):
                    low_part(j, q, q).then_inc(s["lo_ready"], 1)
            use_destinations(n_reg)
            hidden(n_reg)
            for n in range(4):
                low_part(n_reg, n, 8 + n).then_inc(s["lo_ready"], 1)
            link(v.memset(tick[:, :], 0.0), "ring_free")
            for i in range(4):
                dve.wait_ge(rows_back[i], 32)
                r = ring[:, 4096 * i:4096 * i + 4096].rearrange("p (r d) -> p r d", r=4)
                xo = ring[:, 16384 + 1024 * i:16384 + 1024 * i + 1024]
                link(v.tensor_tensor(xo, xo, r[:, 2, :], ALU.add))
                link(v.tensor_tensor(xo, xo, r[:, 3, :], ALU.add))
                dve.wait_ge(s["pair_sum"], i + 1)
                link(v.tensor_tensor(xo, xo, r[:, 0, :], ALU.add), "summed")


_INS = ['x', 'mem', 'rel_bias', 'ln_mix_g', 'w_in', 'swa_qn_g', 'swa_kn_g', 'swa_sinks', 'conv_dw_w', 'conv_dw_b',
        'conv_ln_g', 'conv_ln_b', 'conv_pw_w', 'conv_pw_b', 'mla_qa_g', 'mla_kva_g', 'mla_wq_b', 'mla_wkv_b',
        'mla_qn_nope_g', 'mla_qn_rope_g', 'mla_kn_nope_g', 'mla_kn_rope_g', 'ssm_a_re', 'ssm_a_im', 'ssm_log_dt',
        'ssm_b_re', 'ssm_b_im', 'ssm_c_re', 'ssm_c_im', 'ssm_d', 'ssm_glu_w', 'ssm_glu_b', 'mix_out_g', 'w_out',
        'ln_cross_g', 'mem_ln_g', 'xa_wq', 'xa_wk', 'xa_wv', 'xa_qn_g', 'xa_kn_g', 'xa_wo', 'ln_moe_g',
        'moe_w_group', 'moe_b_group', 'moe_w_expert', 'moe_b_expert', 'moe_w_gate', 'moe_w_up', 'moe_w_down']


def kernel(**inputs):
    import concourse.bacc as _bacc
    from concourse.bass_utils import run_bass_kernel_spmd as _run

    nc = _bacc.Bacc("TRN2", target_bir_lowering=False, num_devices=1)
    arrays, args = {}, {}
    for name in _INS:
        a = np.ascontiguousarray(inputs[name])
        arrays[f"in_{name}_dram"] = a
        args[name] = nc.dram_tensor(f"in_{name}_dram", a.shape, mybir.dt.from_np(a.dtype), kind="ExternalInput").ap()
    fixed = []
    for name, a in zip(("const", "bucket"), constants()):
        arrays[f"in_{name}_dram"] = a
        fixed.append(nc.dram_tensor(f"in_{name}_dram", a.shape, F32, kind="ExternalInput").ap())
    out = nc.dram_tensor("out_0_dram", (1, T, D), F32, kind="ExternalOutput").ap()
    trunk(nc, args, *fixed, out)
    r = _run(nc, [arrays], core_ids=[0])
    return r.results[0]["out_0_dram"]
```
